# Optimizing a Trainium2 kernel written in Bass

```python
import jax, jax.numpy as jnp
from jax import lax
import numpy as np

D_MODEL = 1024
BATCH = 1
SEQ = 512
DEPTH = 1

GRID_W = 64
CTX_LEN = 256
N_HEADS = 4
D_KEY = D_MODEL // 2
D_VAL = D_MODEL
HEAD_K = D_KEY // N_HEADS
HEAD_V = D_VAL // N_HEADS
DECAY_RANK = 16
DECAY_TAU = 16.0
CHUNK = 64
D_CONV = D_MODEL
CONV_W = 3
D_FF = ((-(-8 * D_MODEL // 3)) + 255) // 256 * 256
EPS = 1e-6
IN_SPLITS = (D_KEY, D_KEY, D_VAL, D_VAL, 2 * DECAY_RANK, D_CONV, D_CONV, D_CONV, D_MODEL, D_MODEL)
N_IN = sum(IN_SPLITS)


def rmsnorm(x, g):
    xf = x.astype(jnp.float32)
    y = xf * lax.rsqrt(jnp.mean(xf * xf, axis=-1, keepdims=True) + EPS)
    return (y * g.astype(jnp.float32)).astype(x.dtype)

def modulate(h, shift, scale):
    return h * (1.0 + scale[:, None, :]) + shift[:, None, :]

def gla_chunked(q, k, v, log_a, s0):
    Bn, H, T, K = q.shape
    V = v.shape[-1]
    N = T // CHUNK
    f = lambda t: t.astype(jnp.float32).reshape(Bn, H, N, CHUNK, t.shape[-1])
    q, k, v, log_a = f(q), f(k), f(v), f(log_a)
    q = q * (K ** -0.5)
    b = jnp.cumsum(log_a, axis=3)
    b_mid = b[:, :, :, CHUNK // 2 - 1:CHUNK // 2, :]
    b_last = b[:, :, :, CHUNK - 1:, :]
    causal = jnp.tril(jnp.ones((CHUNK, CHUNK), dtype=bool))
    scores = jnp.einsum('bhnik,bhnjk->bhnij', q * jnp.exp(b - b_mid), k * jnp.exp(b_mid - b))
    scores = jnp.where(causal, scores, 0.0)
    o_intra = jnp.einsum('bhnij,bhnjv->bhniv', scores, v)
    kv = jnp.einsum('bhnjk,bhnjv->nbhkv', k * jnp.exp(b_last - b), v)
    decay = jnp.moveaxis(jnp.exp(b_last[:, :, :, 0, :]), 2, 0)

    def step(s, inp):
        d, kv_n = inp
        return d[..., None] * s + kv_n, s

    s_final, s_before = lax.scan(step, s0.astype(jnp.float32), (decay, kv))
    o_inter = jnp.einsum('bhnik,nbhkv->bhniv', q * jnp.exp(b), s_before)
    return (o_intra + o_inter).reshape(Bn, H, T, V), s_final

def gla_bidir(q, k, v, la_f, la_b, s0_f, s0_b):
    o_f, s_f = gla_chunked(q, k, v, la_f, s0_f)
    flip = lambda t: jnp.flip(t, axis=2)
    o_b, s_b = gla_chunked(flip(q), flip(k), flip(v), flip(la_b), s0_b)
    return o_f + flip(o_b), s_f, s_b

def project(h, w_in, w_dec_up, b_dec):
    Bn, T, _ = h.shape
    z = h @ w_in
    q, k, v, g, dd, cb, cc, ch, ga, gb = jnp.split(z, np.cumsum(IN_SPLITS)[:-1].tolist(), axis=-1)
    dd = dd.reshape(Bn, T, 2, DECAY_RANK)
    zd = jnp.einsum('btdr,drk->dbtk', dd, w_dec_up) + b_dec[:, None, None, :]
    log_a = jax.nn.log_sigmoid(zd.astype(jnp.float32)) / DECAY_TAU
    heads = lambda t, hd: t.reshape(Bn, T, N_HEADS, hd).transpose(0, 2, 1, 3)
    return (heads(q, HEAD_K), heads(k, HEAD_K), heads(v, HEAD_V), g,
            heads(log_a[0], HEAD_K), heads(log_a[1], HEAD_K), cb, cc, ch, ga, gb)

def seq_conv(u, w):
    pad = CONV_W // 2
    T = u.shape[1]
    up = jnp.pad(u, ((0, 0), (pad, pad), (0, 0)))
    y = up[:, 0:T] * w[0]
    for j in range(1, CONV_W):
        y = y + up[:, j:j + T] * w[j]
    return y

def merge_branches(o, g, cb, cc, ch, ga, gb, rows, g_head, w_gla_out, w_conv, w_conv_out, w_mix_out):
    Bn, H, T, V = o.shape
    o = rmsnorm(o, g_head).transpose(0, 2, 1, 3).reshape(Bn, T, H * V).astype(g.dtype)
    y_gla = (o * jax.nn.silu(g)) @ w_gla_out
    u = cc * ch
    if rows is None:
        uc = seq_conv(u, w_conv)
    else:
        uc = seq_conv(u.reshape(Bn * rows, T // rows, -1), w_conv).reshape(Bn, T, -1)
    y_conv = (cb * uc) @ w_conv_out
    merged = jax.nn.sigmoid(ga) * y_gla + jax.nn.sigmoid(gb) * y_conv
    return merged @ w_mix_out

def swiglu(h, w_in, w_out):
    a, b = jnp.split(h @ w_in, 2, axis=-1)
    return (jax.nn.silu(a) * b) @ w_out

def first_inputs(seed: int = 0) -> dict:
    key = jax.random.key(seed)
    ks = jax.random.split(key, 20)
    nrm = lambda k, shape, s: jax.random.normal(k, shape, jnp.float32) * s
    return {
        "x": nrm(ks[0], (BATCH, SEQ, D_MODEL), 1.0),
        "c": nrm(ks[1], (BATCH, D_MODEL), 1.0),
        "ctx": nrm(ks[2], (BATCH, CTX_LEN, D_MODEL), 1.0),
        "c_ctx": nrm(ks[3], (D_MODEL,), 1.0),
        "w_ada": nrm(ks[4], (DEPTH, D_MODEL, 6 * D_MODEL), 0.5 * D_MODEL ** -0.5),
        "b_ada": nrm(ks[5], (DEPTH, 6 * D_MODEL), 0.01),
        "g_mix": 1.0 + nrm(ks[6], (DEPTH, D_MODEL), 0.02),
        "w_in": nrm(ks[7], (DEPTH, D_MODEL, N_IN), D_MODEL ** -0.5),
        "w_dec_up": nrm(ks[8], (DEPTH, 2, DECAY_RANK, D_KEY), DECAY_RANK ** -0.5),
        "b_dec": nrm(ks[9], (DEPTH, 2, D_KEY), 0.1),
        "g_head": 1.0 + nrm(ks[10], (DEPTH, HEAD_V), 0.02),
        "w_gla_out": nrm(ks[11], (DEPTH, D_VAL, D_MODEL), D_VAL ** -0.5),
        "w_conv": nrm(ks[12], (DEPTH, CONV_W, D_CONV), CONV_W ** -0.5),
        "w_conv_out": nrm(ks[13], (DEPTH, D_CONV, D_MODEL), D_CONV ** -0.5),
        "w_mix_out": nrm(ks[14], (DEPTH, D_MODEL, D_MODEL), D_MODEL ** -0.5),
        "g_ffn": 1.0 + nrm(ks[15], (DEPTH, D_MODEL), 0.02),
        "w_ffn_in": nrm(ks[16], (DEPTH, D_MODEL, 2 * D_FF), D_MODEL ** -0.5),
        "w_ffn_out": nrm(ks[17], (DEPTH, D_FF, D_MODEL), D_FF ** -0.5),
        "g_final": 1.0 + nrm(ks[18], (D_MODEL,), 0.02),
    }

def first_block(x, c, ctx, c_ctx, w_ada, b_ada, g_mix, w_in, w_dec_up, b_dec, g_head, w_gla_out,
              w_conv, w_conv_out, w_mix_out, g_ffn, w_ffn_in, w_ffn_out, g_final):
    rows = x.shape[1] // GRID_W
    bc = ctx.shape[0]
    zeros_state = jnp.zeros((bc, N_HEADS, HEAD_K, HEAD_V), jnp.float32)
    for l in range(DEPTH):
        last = l == DEPTH - 1
        mod_lat = jnp.split(jax.nn.silu(c) @ w_ada[l] + b_ada[l], 6, axis=-1)
        mod_ctx = jnp.split(jax.nn.silu(c_ctx)[None, :] @ w_ada[l] + b_ada[l], 6, axis=-1)
        sh1, sc1, gt1, sh2, sc2, gt2 = mod_lat
        sh1c, sc1c, gt1c, sh2c, sc2c, gt2c = mod_ctx

        pl = project(modulate(rmsnorm(x, g_mix[l]), sh1, sc1), w_in[l], w_dec_up[l], b_dec[l])
        pc = project(modulate(rmsnorm(ctx, g_mix[l]), sh1c, sc1c), w_in[l], w_dec_up[l], b_dec[l])
        o_c, s_cf, s_cb = gla_bidir(pc[0], pc[1], pc[2], pc[4], pc[5], zeros_state, zeros_state)
        o_l, _, _ = gla_bidir(pl[0], pl[1], pl[2], pl[4], pl[5], s_cf, s_cb)
        mix_l = merge_branches(o_l, pl[3], pl[6], pl[7], pl[8], pl[9], pl[10], rows, g_head[l],
                               w_gla_out[l], w_conv[l], w_conv_out[l], w_mix_out[l])
        x = x + gt1[:, None, :] * mix_l
        if not last:
            mix_c = merge_branches(o_c, pc[3], pc[6], pc[7], pc[8], pc[9], pc[10], None, g_head[l],
                                   w_gla_out[l], w_conv[l], w_conv_out[l], w_mix_out[l])
            ctx = ctx + gt1c[:, None, :] * mix_c

        x = x + gt2[:, None, :] * swiglu(modulate(rmsnorm(x, g_ffn[l]), sh2, sc2), w_ffn_in[l], w_ffn_out[l])
        if not last:
            ctx = ctx + gt2c[:, None, :] * swiglu(modulate(rmsnorm(ctx, g_ffn[l]), sh2c, sc2c),
                                                  w_ffn_in[l], w_ffn_out[l])
    return rmsnorm(x, g_final)


DEPTH_2 = 2

D_CONV_2 = D_MODEL // 2
N_CONV_GROUPS = 4
CONV_WIDTH = 31
D_POOL = D_MODEL // 2
POOL_WINDOWS = (2, 4, 8, 16)
N_POOL_GROUPS = len(POOL_WINDOWS)
POOL_GROUP = D_POOL // N_POOL_GROUPS
HG_HEADS = 8
HG_DK = D_MODEL // HG_HEADS
HG_DV = HG_DK
D_HG = HG_HEADS * HG_DK
D_FF_2 = -(-8 * D_MODEL // (3 * 256)) * 256
N_EVEN = (DEPTH_2 + 1) // 2
N_ODD = DEPTH_2 // 2


def rmsnorm_2(x, g):
    xf = x.astype(jnp.float32)
    y = xf * lax.rsqrt(jnp.mean(xf * xf, axis=-1, keepdims=True) + EPS)
    return (y * g.astype(jnp.float32)).astype(x.dtype)

def layernorm(x, g, b):
    xf = x.astype(jnp.float32)
    mu = jnp.mean(xf, axis=-1, keepdims=True)
    var = jnp.mean(jnp.square(xf - mu), axis=-1, keepdims=True)
    y = (xf - mu) * lax.rsqrt(var + EPS)
    return (y * g.astype(jnp.float32) + b.astype(jnp.float32)).astype(x.dtype)

def swiglu_ffn(h, w1, w3, w2):
    return (jax.nn.silu(h @ w1) * (h @ w3)) @ w2

def conv_pool_mixer(h, w_in, dw_w, dw_b, ln_g, ln_b, pool_w, pool_scale, w_out):
    B, T, _ = h.shape
    z = h @ w_in
    a_val = z[..., :D_CONV_2]
    a_gate = z[..., D_CONV_2:2 * D_CONV_2]
    u = z[..., 2 * D_CONV_2:]

    a = a_val * jax.nn.sigmoid(a_gate)
    a = lax.conv_general_dilated(
        a, dw_w[:, None, :].astype(a.dtype), window_strides=(1,),
        padding=[(CONV_WIDTH - 1, 0)],
        dimension_numbers=('NWC', 'WIO', 'NWC'),
        feature_group_count=D_CONV_2) + dw_b
    a = jax.nn.silu(layernorm(a, ln_g, ln_b))

    ug = u.reshape(B, T, N_POOL_GROUPS, POOL_GROUP)
    cs = jnp.cumsum(ug.astype(jnp.float32), axis=1)
    cs = jnp.pad(cs, ((0, 0), (1, 0), (0, 0), (0, 0)))
    t = jnp.arange(T)
    means = []
    for g, w in enumerate(POOL_WINDOWS):
        lo = jnp.maximum(t + 1 - w, 0)
        s = cs[:, 1:, g] - cs[:, lo, g]
        cnt = jnp.minimum(t + 1, w).astype(jnp.float32)[:, None]
        means.append(s / cnt)
    pooled = jnp.stack(means, axis=2)
    d = (pooled - ug.astype(jnp.float32)).astype(u.dtype)
    p = jnp.einsum('btgc,gcd->btgd', d, pool_w).reshape(B, T, D_POOL) * pool_scale

    return jnp.concatenate([a, p], axis=-1) @ w_out

def hgrn2_mixer(h, w_in, lb, gn_g, w_out):
    B, T, _ = h.shape
    NC = T // CHUNK
    z = h @ w_in
    q, f_raw, i, g = jnp.split(z, 4, axis=-1)
    f = lb + (1.0 - lb) * jax.nn.sigmoid(f_raw.astype(jnp.float32))
    log_f = jnp.log(f)
    k = 1.0 - f

    def to_chunks(a, dh):
        a = a.astype(jnp.float32).reshape(B, NC, CHUNK, HG_HEADS, dh)
        return a.transpose(1, 0, 3, 2, 4)

    qc = to_chunks(q, HG_DK)
    kc = to_chunks(k, HG_DK)
    vc = to_chunks(i, HG_DV)
    bc = jnp.cumsum(to_chunks(log_f, HG_DK), axis=3)
    tril = jnp.tril(jnp.ones((CHUNK, CHUNK), dtype=bool))

    def step(S, inp):
        qt, kt, vt, bt = inp
        diff = bt[:, :, :, None, :] - bt[:, :, None, :, :]
        decay = jnp.exp(jnp.where(tril[:, :, None], diff, -jnp.inf))
        scores = jnp.einsum('bhtk,bhsk,bhtsk->bhts', qt, kt, decay)
        o = (jnp.einsum('bhts,bhsv->bhtv', scores, vt)
             + jnp.einsum('bhtk,bhkv->bhtv', qt * jnp.exp(bt), S))
        b_last = bt[:, :, -1:, :]
        S = (jnp.exp(b_last[:, :, 0, :])[..., None] * S
             + jnp.einsum('bhsk,bhsv->bhkv', kt * jnp.exp(b_last - bt), vt))
        return S, o

    S0 = jnp.zeros((B, HG_HEADS, HG_DK, HG_DV), jnp.float32)
    _, o = lax.scan(step, S0, (qc, kc, vc, bc))
    o = o.transpose(1, 0, 3, 2, 4).reshape(B, T, HG_HEADS, HG_DV)
    o = o * lax.rsqrt(jnp.mean(o * o, axis=-1, keepdims=True) + EPS)
    o = o * gn_g.astype(jnp.float32).reshape(HG_HEADS, HG_DV)
    o = o.reshape(B, T, D_HG).astype(h.dtype) * jax.nn.silu(g)
    return o @ w_out

def second_inputs(seed: int = 0) -> dict:
    key = jax.random.key(seed)
    ks = jax.random.split(key, 20)
    nrm = lambda k, shape, s: jax.random.normal(k, shape, jnp.float32) * s
    gain = lambda k, shape: 1.0 + 0.05 * jax.random.normal(k, shape, jnp.float32)
    d_in0 = 2 * D_CONV_2 + D_POOL
    return {
        "x": jax.random.normal(ks[0], (BATCH, SEQ, D_MODEL), jnp.float32),
        "norm_mix_g": gain(ks[1], (DEPTH_2, D_MODEL)),
        "norm_ffn_g": gain(ks[2], (DEPTH_2, D_MODEL)),
        "final_g": gain(ks[3], (D_MODEL,)),
        "cp_w_in": nrm(ks[4], (N_EVEN, D_MODEL, d_in0), D_MODEL ** -0.5),
        "cp_dw_w": nrm(ks[5], (N_EVEN, CONV_WIDTH, D_CONV_2), CONV_WIDTH ** -0.5),
        "cp_dw_b": nrm(ks[6], (N_EVEN, D_CONV_2), 0.01),
        "cp_ln_g": gain(ks[7], (N_EVEN, D_CONV_2)),
        "cp_ln_b": nrm(ks[8], (N_EVEN, D_CONV_2), 0.01),
        "cp_pool_w": nrm(ks[9], (N_EVEN, N_POOL_GROUPS, POOL_GROUP, POOL_GROUP), POOL_GROUP ** -0.5),
        "cp_pool_scale": gain(ks[10], (N_EVEN, D_POOL)),
        "cp_w_out": nrm(ks[11], (N_EVEN, D_CONV_2 + D_POOL, D_MODEL), (D_CONV_2 + D_POOL) ** -0.5),
        "hg_w_in": nrm(ks[12], (N_ODD, D_MODEL, 4 * D_HG), D_MODEL ** -0.5),
        "hg_lb_logits": nrm(ks[13], (DEPTH_2, D_HG), 0.1),
        "hg_gn_g": gain(ks[14], (N_ODD, D_HG)),
        "hg_w_out": nrm(ks[15], (N_ODD, D_HG, D_MODEL), D_HG ** -0.5),
        "ffn_w1": nrm(ks[16], (DEPTH_2, D_MODEL, D_FF_2), D_MODEL ** -0.5),
        "ffn_w3": nrm(ks[17], (DEPTH_2, D_MODEL, D_FF_2), D_MODEL ** -0.5),
        "ffn_w2": nrm(ks[18], (DEPTH_2, D_FF_2, D_MODEL), D_FF_2 ** -0.5),
    }

def second_block(x, norm_mix_g, norm_ffn_g, final_g, cp_w_in, cp_dw_w, cp_dw_b,
              cp_ln_g, cp_ln_b, cp_pool_w, cp_pool_scale, cp_w_out, hg_w_in,
              hg_lb_logits, hg_gn_g, hg_w_out, ffn_w1, ffn_w3, ffn_w2):
    p = jax.nn.softmax(hg_lb_logits.astype(jnp.float32), axis=0)
    lower_bounds = jnp.cumsum(p, axis=0) - p[0:1]
    h = x
    for layer in range(DEPTH_2):
        hn = rmsnorm_2(h, norm_mix_g[layer])
        j = layer // 2
        if layer % 2 == 0:
            mix = conv_pool_mixer(hn, cp_w_in[j], cp_dw_w[j], cp_dw_b[j], cp_ln_g[j],
                                  cp_ln_b[j], cp_pool_w[j], cp_pool_scale[j], cp_w_out[j])
        else:
            mix = hgrn2_mixer(hn, hg_w_in[j], lower_bounds[layer], hg_gn_g[j], hg_w_out[j])
        h = h + mix
        h = h + swiglu_ffn(rmsnorm_2(h, norm_ffn_g[layer]), ffn_w1[layer], ffn_w3[layer], ffn_w2[layer])
    return rmsnorm_2(h, final_g)


def setup_inputs(seed=0):
    out = dict(first_inputs(seed))
    for name, value in second_inputs(seed + 1).items():
        if name != "x":
            out[name + "_2"] = value
    return out


def reference(
    x, c, ctx, c_ctx, w_ada, b_ada, g_mix, w_in, w_dec_up, b_dec, g_head, w_gla_out, w_conv,
    w_conv_out, w_mix_out, g_ffn, w_ffn_in, w_ffn_out, g_final, norm_mix_g_2, norm_ffn_g_2,
    final_g_2, cp_w_in_2, cp_dw_w_2, cp_dw_b_2, cp_ln_g_2, cp_ln_b_2, cp_pool_w_2,
    cp_pool_scale_2, cp_w_out_2, hg_w_in_2, hg_lb_logits_2, hg_gn_g_2, hg_w_out_2, ffn_w1_2,
    ffn_w3_2, ffn_w2_2,
):
    x = first_block(
        x, c, ctx, c_ctx, w_ada, b_ada, g_mix, w_in, w_dec_up, b_dec, g_head, w_gla_out, w_conv,
        w_conv_out, w_mix_out, g_ffn, w_ffn_in, w_ffn_out, g_final,
    )
    return second_block(
        x, norm_mix_g_2, norm_ffn_g_2, final_g_2, cp_w_in_2, cp_dw_w_2, cp_dw_b_2, cp_ln_g_2,
        cp_ln_b_2, cp_pool_w_2, cp_pool_scale_2, cp_w_out_2, hg_w_in_2, hg_lb_logits_2,
        hg_gn_g_2, hg_w_out_2, ffn_w1_2, ffn_w3_2, ffn_w2_2,
    )


_drawn_inputs = setup_inputs


def setup_inputs(seed=0):
    import zlib

    import numpy as np

    out = dict(_drawn_inputs(seed))
    spreads = {}
    factors = {'ctx': 2.906,
     'c_ctx': 4.319,
     'b_ada': 3.015,
     'g_mix': 4.414,
     'b_dec': 7.336,
     'g_head': 36.529,
     'g_ffn': 20.154,
     'cp_dw_b_2': 5.142,
     'cp_ln_b_2': 8.0,
     'hg_gn_g_2': 2.696}
    for name, (base, spread) in spreads.items():
        noise = np.random.default_rng([zlib.crc32(name.encode()), seed]).standard_normal(out[name].shape)
        drawn = base * np.exp(spread * noise) if base else spread * noise
        out[name] = __import__('jax').numpy.asarray(drawn.astype(out[name].dtype))
    for name, factor in factors.items():
        out[name] = (out[name] * factor).astype(out[name].dtype)
    return out
```

```python
from contextlib import ExitStack

import numpy as np

import concourse.bass as bass
import concourse.mybir as mybir
from concourse.alu_op_type import AluOpType as ALU

ACT = mybir.ActivationFunctionType
F32 = mybir.dt.float32
F32R = mybir.dt.float32r
BF16 = mybir.dt.bfloat16
U32 = mybir.dt.uint32
I32 = mybir.dt.int32

P = 128
D = 1024
KC = D // P
T = 512
CTX = 256
TC = T + CTX
TT, TTC = T // P, TC // P
CH = 64
NCH, NCHC = T // CH, TC // CH
HEADS, HEAD_V = 4, 256
DFF = 2816
FC = DFF // P
HG = 8
CONVW = 31
CPC = 4
EPS = 1e-6
DECAY_TAU = 16.0
W_MID = {0: CH // 2 - 1, 1: CH // 2}
W_LAST = {0: CH - 1, 1: 0}
LEVELS = [32, 16, 8, 4, 2, 1]
FFO = [6, 6, 5, 5]
FFO_AT = [0, 6, 12, 17]

VEC_SIZES = [("b_ada", 48), ("g_mix", 8), ("b_dec", 8), ("g_head", 2),
             ("w_conv", 24), ("g_ffn", 8), ("g_final", 8), ("norm_mix", 16), ("norm_ffn", 16),
             ("final_g", 8), ("dw_w", 4 * CONVW), ("dw_b", 4), ("ln_g", 4), ("ln_b", 4),
             ("pool_scale", 4), ("lb_logits", 16), ("gn_g", 8)]
VEC = {}
NVEC = 0
for _name, _n in VEC_SIZES:
    VEC[_name] = NVEC
    NVEC += _n

Q_QK, Q_V, Q_GLA, Q_MERGE, Q_MIX = 0, 2, 4, 12, 20
Q_FFI = [22, 46, 75]
Q_FFO = [33, 57, 86]
Q_CPI, Q_CPO, Q_HG, Q_HGO = 41, 44, 65, 73
Q_END = 94

KB = 1024
SBUF_AT = 16512


def at_index(t, i):
    if isinstance(i, int):
        return t[:, i]
    return t[:, bass.ds(i, 1)].squeeze(1)


def span(i, n):
    return slice(i, i + n) if isinstance(i, int) else bass.ds(i, n)


def wide(ap, n):
    u = ap.unsqueeze(len(ap.shape))
    return u.broadcast_to(list(ap.shape) + [n])


def build(nc, dram):
    ctx = ExitStack()
    with ctx:
        def at(name, shape, dt, kb):
            return nc.alloc_sbuf_tensor_at(name, shape, dt, offset=SBUF_AT + int(kb * KB))

        raw = [at(f"w_raw{s}", [P, D], F32, 4 * s) for s in range(4)]
        w_hi = [at(f"w_hi{s}", [P, D], F32R, 16 + 4 * s) for s in range(4)]
        w_lo = [at(f"w_lo{s}", [P, D], F32R, 32 + 4 * s) for s in range(4)]

        vec = at("vec", [P, NVEC], F32, 48)
        ident = at("ident", [P, P], F32, 49.5)
        ones = at("ones", [P, P], F32, 50)
        causal = [at("causal_f", [P, P], F32, 50.5), at("causal_b", [P, P], F32, 51)]
        keep = at("keep", [P, TC + 1], F32, 51.5)
        w_up = at("w_up", [32, 2, HEADS, P], F32, 55872 / KB)
        level_mask = at("level_mask", [P, len(LEVELS), P], F32, 55872 / KB)
        mod1 = at("mod1", [P, 16, 2], F32, 59968 / KB)
        mod2 = at("mod2", [P, 32], F32, 60096 / KB)
        mod_sum = at("mod_sum", [P, 4], F32, 60224 / KB)
        amp1 = at("amp1", [P, KC, 2], F32, 60288 / KB)
        amp2 = at("amp2", [P, KC], F32, 60352 / KB)
        eps = at("eps", [P, 1], F32, 60384 / KB)
        gain_xg = at("gain_xg", [P, KC], F32, 60416 / KB)
        b_dec_h = at("b_dec_h", [P, 1], F32, 60480 / KB)
        dec = at("dec", [P, NCHC], F32, 60512 / KB)
        lb = at("lb", [P, HG], F32, 60576 / KB)
        om_lb = at("om_lb", [P, HG], F32, 60608 / KB)
        lb_t = at("lb_t", [P, 16], F32, 60640 / KB)
        inv_cnt = at("inv_cnt", [P, CPC, 16], F32, 60704 / KB)
        cnt_i = at("cnt_i", [P, 16], I32, 60960 / KB)
        o_ss = at("o_ss", [P, TT], F32, 61024 / KB)
        o_rs = at("o_rs", [P, TT], F32, 61056 / KB)
        o_rstd = at("o_rstd", [P, TT], F32, 61088 / KB)
        cnt_f = at("cnt_f", [P, 16], F32, 61120 / KB)
        spare = at("spare", [P, 16], F32, 61184 / KB)

        h1_hi, h1_lo = at("h1_hi", [P, KC, T], F32R, 60), at("h1_lo", [P, KC, T], F32R, 92)
        x_all = at("x_all", [P, KC, TC], F32, 128)
        hc_hi, hc_lo = at("hc_hi", [P, KC, CTX], F32R, 152), at("hc_lo", [P, KC, CTX], F32R, 160)
        sq0 = [at(f"sq0_{i}", [P, TC], F32, 168 + 3 * i) for i in range(2)]
        rstd0 = at("rstd0", [P, TC], F32, 174)
        cond = at("cond", [P, 2, D], F32, 196)
        ada1_w = [at(f"ada1_w{i}", [P, D], F32, 108 + 4 * i) for i in range(4)]
        ada1_out = [at("ada1_out0", [P, D], F32, 124), at("ada1_out1", [P, D], F32, 80)]
        dd_raw, dd_hi, dd_lo = at("dd_raw", [P, D], F32, 184), at("dd_hi", [P, D], F32R, 188), at("dd_lo", [P, D], F32R, 192)
        q_sb = at("q_sb", [P, HEADS, T], F32, 108)
        k_sb = at("k_sb", [P, HEADS, TC], F32, 116)
        v_sb = at("v_sb", [P, HEADS, TTC * HEAD_V], F32, 128)
        y_sb = at("y_sb", [P, KC, T], F32, 152)
        g_sb = at("g_sb", [P, KC, T], F32, 168)
        vT = [at(f"vT{i}", [P, TC], F32, 82 + 3 * i) for i in range(2)]
        dd_sb = at("dd_sb", [32, TC], F32, 76)
        state = [at(f"state{i}", [P, HEAD_V], F32, 79 + i) for i in range(3)]
        v_h = at("v_h", [P, TTC, HEAD_V], F32, 82)
        s_dir = [at("s_f", [P, TT, P], F32, 205), at("s_b", [P, TT, P], F32, 88)]
        cc_sb = at("cc_sb", [P, T], F32, 90)
        t0, t1, t2 = (at(f"t{i}", [P, TC], F32, 184 + 3 * i) for i in range(3))
        o_tok = at("o_tok", [P, TT, HEAD_V], F32, 184)
        q_mid, k_mid, q_dec = (at(n, [P, T], F32, 193 + 2 * i) for i, n in enumerate(("q_mid", "k_mid", "q_dec")))
        k_dec = at("k_dec", [P, TC], F32, 199)
        kd_tok = at("kd_tok", [P, TTC, P], F32, 202)
        w_up_h = at("w_up_h", [32, P], F32, 207)

        og_hi, og_lo = at("og_hi", [P, KC, T], F32R, 108), at("og_lo", [P, KC, T], F32R, 184)
        og_sg = [at(f"og_sg{i}", [P, T], F32, 124 + 2 * i) for i in range(2)]
        og_val = [at(f"og_val{i}", [P, T], F32, 200 + 2 * i) for i in range(2)]
        y_hi, y_lo = at("y_hi", [P, KC, T], F32R, 128), at("y_lo", [P, KC, T], F32R, 168)
        mg_hi, mg_lo = at("mg_hi", [P, KC, T], F32R, 152), at("mg_lo", [P, KC, T], F32R, 76)
        ada_w = [at(f"ada_w{i}", [P, D], F32, 144 + 4 * i) for i in range(2)]
        sig_a, mrg_a = at("sig_a", [P, T], F32, 124), at("mrg_a", [P, T], F32, 126)
        sig_b, mrg_b = at("sig_b", [P, T], F32, 200), at("mrg_b", [P, T], F32, 202)
        mrg_v = at("mrg_v", [P, T], F32, 204)
        x_res = at("x_res", [P, KC, T], F32, 108)

        x = at("x", [P, KC, T], F32, 60)
        h_hi, h_lo = at("h_hi", [P, KC, T], F32R, 76), at("h_lo", [P, KC, T], F32R, 92)
        gu_hi, gu_lo = at("gu_hi", [P, FC, T], F32R, 108), at("gu_lo", [P, FC, T], F32R, 152)
        sa = [at(f"sa{i}", [P, T], F32, 196 + 2 * i) for i in range(2)]
        fval = [at(f"fval{i}", [P, T], F32, 200 + 2 * i) for i in range(2)]
        sq = [at(f"sq{i}", [P, T], F32, 196 + 2 * i) for i in range(2)]
        acc = at("acc", [P, T], F32, 200)
        nv = [at("nv0", [P, T], F32, 202), at("nv1", [P, T], F32, 196)]
        acc2 = at("acc2", [P, T], F32, 202)
        rstd_xg = at("rstd_xg", [P, T], F32, 198)
        rstd = at("rstd", [P, T], F32, 204)

        APAD, UPAD = CONVW - 1, 16
        a_sb = at("a_sb", [P, CPC, APAD + T], F32, 108)
        u_sb = at("u_sb", [P, CPC, UPAD + T], F32, 117)
        cv = at("cv", [P, CPC, T], F32, 126)
        cat_hi, cat_lo = at("cat_hi", [P, KC, T], F32R, 134), at("cat_lo", [P, KC, T], F32R, 150)
        win = [at(f"win{i}", [P, UPAD + T], F32, 166 + 2.25 * i) for i in range(2)]
        pd = at("pd", [P, CPC, T], F32, 171)
        tap = [at(f"tap{i}", [P, P], F32, 179 + 0.5 * i) for i in range(4)]
        pool_w = at("pool_w", [P, CPC, P], F32, 181)
        csg = [at(f"csg{i}", [P, T], F32, 183 + 2 * i) for i in range(2)]
        csq = at("csq", [P, CPC, T], F32, 187)
        lnv = [at(f"lnv{i}", [P, T], F32, 183 + 2 * i) for i in range(2)]
        lns = [at(f"lns{i}", [P, T], F32, 166 + 2 * i) for i in range(2)]

        r_hi, r_lo = at("r_hi", [P, KC, T], F32R, 108), at("r_lo", [P, KC, T], F32R, 124)
        hq, hk, hb, hg, hv = ([at(f"{n}{i}", [P, T], F32, 140 + 10 * i + 2 * m) for i in range(2)]
                              for m, n in enumerate(("hq", "hk", "hb", "hg", "hv")))
        hv_tok, hkd_tok = at("hv_tok", [P, TT, P], F32, 160), at("hkd_tok", [P, TT, P], F32, 162)
        hx = [at(f"hx{i}", [P, T], F32, 164 + 2 * i) for i in range(6)]
        hqb, hkd = at("hqb", [P, T], F32, 176), at("hkd", [P, T], F32, 178)
        hd = [at(f"hd{i}", [P, T], F32, 180 + 2 * i) for i in range(2)]
        he = [at(f"he{i}", [P, T], F32, 184 + 2 * i) for i in range(2)]
        hs = at("hs", [P, TT, P], F32, 188)
        hst = at("hst", [P, NCH, P], F32, 190)
        ho_tok = at("ho_tok", [P, TT, P], F32, 194)
        hsf = at("hsf", [P, T], F32, 196)
        hval = at("hval", [P, T], F32, 198)
        hlf = at("hlf", [P, T], F32, 200)
        hdec = at("hdec", [P, NCH], F32, 202)
        hsquares = at("hsquares", [P, T], BF16, 202.5)

        ps = ctx.enter_context(nc.psum_tensor("ps", [P, 8, 512], F32))
        z_ps = ps[:, 6:8, :].rearrange("p a n -> p (a n)")

        cond2 = ps[:, 4:6, :].rearrange("p a n -> p (a n)")

        block = ctx.enter_context(nc.Block())

        class Semaphores(dict):
            def __missing__(self, name):
                self[name] = ctx.enter_context(nc.semaphore(name))
                return self[name]

        S = Semaphores()
        raw_full, hi_done, lo_done, unit_done = ([S[f"{n}{s}"] for s in range(4)]
                                                 for n in ("raw_full", "hi_done", "lo_done", "unit_done"))

        def v_at(name, i=0, n=1):
            return vec[:, VEC[name] + i:VEC[name] + i + n]

        def v_dyn(name, i, n=1):
            if isinstance(i, int):
                return v_at(name, i, n)
            return vec[:, bass.ds(VEC[name] + i, n)]

        def wait_former(eng, sem, count):
            if not (isinstance(count, int) and count == 0):
                eng.wait_ge(sem, count)

        def wait_apart(eng, sem, count):
            if isinstance(count, int):
                wait_former(eng, sem, count)
                return
            need = eng.snap(count)
            eng.wait_ge(S["const_ready"], 1)
            eng.wait_ge(sem, need)

        def sp_unit(sp, s, q, src, n=D):
            wait_former(sp, lo_done[s], q)
            sp.dma_start(raw[s][:, 0:n], src).then_inc(raw_full[s], 16)

        def sp_rounds(sp, q0, n, units):
            with sp.Fori(0, n) as r:
                for s in range(4):
                    sp_unit(sp, s, r + q0, units[bass.ds(r, 1), s].squeeze(0))

        def sp_start(sp):
            sp.dma_start(vec[:, :], dram["vectors"]).then_inc(S["vec_in"], 16)
            sp.dma_start(cond[:, :, :], dram["conditions"].unsqueeze(0).broadcast_to([P, 2, D])).then_inc(S["small_in"], 16)

            def ada(a):
                if a >= 4:
                    sp.wait_ge(S["ada1_used"], a - 3)
                sp.dma_start(ada1_w[a % 4][:, :], dram["w_ada"][a // 2 + KC * (a % 2)]).then_inc(S[f"ada_full{a % 4}"], 16)

            for a in range(4):
                ada(a)
            sp.dma_start(x_all[:, :, 0:T], dram["x"]).then_inc(S["x_in"], 16)
            sp.dma_start(x_all[:, :, T:TC], dram["ctx"]).then_inc(S["x_in"], 16)
            for a in range(4, 8):
                ada(a)
            sp.dma_start(dd_raw[:, :], dram["w_decay"]).then_inc(S["dd_in"], 16)
            sp.wait_ge(S["const_step"], 1)
            for d in range(2):
                sp.dma_start(w_up[16 * d:16 * d + 16, d, :, :], dram["w_dec_up"][d]).then_inc(S["dd_in"], 16)
            for s in range(4):
                sp_unit(sp, s, 0, dram["w_qkv"][0, s])
            for a in range(8, 16):
                ada(a)
            for q in range(1, 4):
                for s in range(4):
                    sp_unit(sp, s, q, dram["w_qkv"][q, s])
            sp_rounds(sp, Q_GLA, 8, dram["w_conv_gate"])

        def sp_ada(sp, a, i):
            sp.wait_ge(S["ada2_used"], a - 1)
            sp.dma_start(ada_w[i][:, :], dram["w_ada"][bass.ds(a + 16, 1)].squeeze(0)).then_inc(S[f"ada_full{i}"], 16)

        def sp_merge(sp):
            for q in range(Q_MERGE, Q_MERGE + 2):
                for s in range(4):
                    sp_unit(sp, s, q, dram["w_merge"][q - Q_MERGE, s])
            sp.wait_ge(S["og_val"], KC)
            sp.dma_start(ada_w[1][:, :], dram["conditions"][0:1].broadcast_to([P, D])).then_inc(S["small_in"], 16)
            sp.dma_start(ada_w[0][:, :], dram["w_ada"][16]).then_inc(S["ada_full0"], 16)
            sp.wait_ge(S["cond_ready"], 3)
            sp.dma_start(ada_w[1][:, :], dram["w_ada"][17]).then_inc(S["ada_full1"], 16)
            with sp.Fori(0, 6) as r:
                for half in range(2):
                    for s in (2 * half, 2 * half + 1):
                        sp_unit(sp, s, r + (Q_MERGE + 2), dram["w_merge"][bass.ds(r + 2, 1), s].squeeze(0))
                    for i in range(2):
                        sp_ada(sp, 4 * r + (2 * half + 2 + i), i)
            for r in (6, 7):
                for half in range(2):
                    for s in (2 * half, 2 * half + 1):
                        sp_unit(sp, s, Q_MIX + r - 6, dram["w_mix"][r - 6, s])
                    for i in range(2):
                        a = 4 * r + 2 * half + 2 + i
                        if a < 32:
                            sp.wait_ge(S["ada2_used"], a - 1)
                            sp.dma_start(ada_w[i][:, :], dram["w_ada"][a + 16]).then_inc(S[f"ada_full{i}"], 16)
            sp.wait_ge(unit_done[0], Q_MERGE + 8)
            sp.dma_start(x_res[:, :, :], dram["x"]).then_inc(S["small_in"], 16)

        def sp_ffn(sp, e):
            sp_rounds(sp, Q_FFI[e], FC // 2, dram["w_ffn_in"][e])
            with sp.Fori(0, KC) as n:
                for s in range(4):
                    sp_unit(sp, s, n + Q_FFO[e],
                            dram["w_ffn_out"][e][bass.ds(n, 1), :, FFO_AT[s] * P:(FFO_AT[s] + FFO[s]) * P].squeeze(0),
                            FFO[s] * P)

        def sp_mixers(sp):
            sp_rounds(sp, Q_CPI, 5, dram["w_cp"])

        @block.sync
        def _(sp):
            sp_start(sp)
            sp_merge(sp)
            sp_ffn(sp, 0)
            sp.wait_ge(S["resid_x"], 16)
            sp.dma_start(pool_w[:, :, :], dram["pool_w"]).then_inc(S["small_in"], 16)
            sp_mixers(sp)
            sp_ffn(sp, 1)
            sp_rounds(sp, Q_HG, 10, dram["w_hg"])
            sp_ffn(sp, 2)
            sp.wait_ge(S["out_ready"], KC)
            sp.dma_start(dram["out"], x[:, :, :]).then_inc(S["out_stored"], 16)
            sp.wait_ge(S["out_stored"], 16)

        def pool_lo(pool, s, q, n=D):
            pool.wait_ge(hi_done[s], q + 1)
            wait_former(pool, unit_done[s], q)
            pool.tensor_tensor(w_lo[s][:, 0:n], raw[s][:, 0:n], w_hi[s][:, 0:n].bitcast(F32),
                               ALU.subtract).then_inc(lo_done[s], 1)

        def pool_rounds(pool, q0, q1, sizes=(D, D, D, D)):
            with pool.Fori(q0, q1) as q:
                for s in range(4):
                    pool_lo(pool, s, q, sizes[s])

        def pool_constants(pool):
            done = 0

            def step(ins):
                nonlocal done
                ins.then_inc(S["const_step"], 1)
                done += 1
                pool.wait_ge(S["const_step"], done)

            step(pool.memset(w_up[:, :, :, :], 0.0))
            step(pool.memset(ones[:, :], 1.0))
            step(pool.memset(ident[:, :], 0.0))
            step(pool.affine_select(out=ident[:, :], in_=ident[:, :], compare_op=ALU.not_equal, fill=1.0,
                                    base=0, pattern=[[-1, P]], channel_multiplier=1))
            for d in range(2):
                step(pool.memset(causal[d][:, :], 1.0))
                sign = 1 - 2 * d
                step(pool.affine_select(out=causal[d][:, :], in_=causal[d][:, :], compare_op=ALU.is_ge, fill=0.0,
                                        base=0, pattern=[[sign, P]], channel_multiplier=-sign))
                step(pool.memset(causal[d][CH * d:CH * d + CH, CH - CH * d:P - CH * d], 0.0))
            step(pool.memset(keep[:, :], 1.0))
            step(pool.memset(keep[:, 0:TC + 1:CH], 0.0))
            step(pool.iota(cnt_i[:, :], pattern=[[1, 16]], base=1, channel_multiplier=0))
            pool.memset(eps[:, :], EPS).then_inc(S["const_ready"], 1)

        def pool_normalise(pool):
            pool.wait_ge(S["norm_recip"], 1)
            for k in range(KC):
                pool.tensor_tensor(x_all[:, k, :], x_all[:, k, :], rstd0[:, :], ALU.mult).then_inc(S["x_normed"], 1)
                if k % 2:
                    pool_lo(pool, k // 2, 0)

        def pool_levels(pool):
            done = 0

            def step(ins):
                nonlocal done
                done += 1
                ins.then_inc(S["level_step"], 1)
                pool.wait_ge(S["level_step"], done)

            pool.wait_ge(S["w_up_copied"], 2 * HEADS)
            step(pool.memset(level_mask[:, :, :], 0.0))
            for i, m in enumerate(LEVELS):
                second = level_mask[:, i, :].rearrange("p (b a m) -> p b a m", a=2, m=m)[:, :, 1, :]
                step(pool.memset(second, 1.0))
                step(pool.affine_select(out=second, in_=second, compare_op=ALU.is_ge, fill=0.0, base=0,
                                        pattern=[[-2 * m, P // (2 * m)], [0, m]], channel_multiplier=1))
                step(pool.affine_select(out=second, in_=second, compare_op=ALU.is_ge, fill=0.0, base=m - 1,
                                        pattern=[[2 * m, P // (2 * m)], [0, m]], channel_multiplier=-1))

        def pool_pooling(pool):
            steps = 0

            def step(ins):
                nonlocal steps
                ins.then_inc(S["window"], 1)
                steps += 1
                pool.wait_ge(S["window"], steps)

            pool.wait_ge(S["zeros"], 6)
            pool.wait_ge(S["dve_step"], 12 + 2 * CPC)
            for g in range(CPC):
                pool.wait_ge(S["cp_u"], g + 1)
                step(pool.tensor_tensor(u_sb[:, g, UPAD:], u_sb[:, g, UPAD:], rstd_xg[:, :], ALU.mult))
                src = u_sb[:, g, :]
                for e in range(g + 1):
                    dst = win[e % 2]
                    step(pool.tensor_tensor(dst[:, UPAD:], src[:, UPAD:], src[:, UPAD - (1 << e):UPAD + T - (1 << e)],
                                            ALU.add))
                    src = dst[:, :]
                step(pool.tensor_scalar(pd[:, g, 16:T], src[:, UPAD + 16:], 1.0 / (2 << g), None, ALU.mult))
                step(pool.tensor_tensor(pd[:, g, 0:16], src[:, UPAD:UPAD + 16], inv_cnt[:, g, :], ALU.mult))
                pool.tensor_tensor(pd[:, g, :], pd[:, g, :], u_sb[:, g, UPAD:], ALU.subtract).then_inc(S["pd_ready"], 1)

        @block.gpsimd
        def _(pool):
            pool_constants(pool)
            pool_normalise(pool)
            pool_rounds(pool, 1, Q_FFI[0])
            pool_levels(pool)
            ffo = [n * P for n in FFO]
            pool_rounds(pool, Q_FFI[0], Q_FFO[0])
            pool_rounds(pool, Q_FFO[0], Q_CPI, ffo)
            pool_rounds(pool, Q_CPI, Q_CPO + 1)
            pool_pooling(pool)
            pool_rounds(pool, Q_CPO + 1, Q_FFO[1])
            pool_rounds(pool, Q_FFO[1], Q_HG, ffo)
            pool_rounds(pool, Q_HG, Q_FFO[2])
            pool_rounds(pool, Q_FFO[2], Q_END, ffo)

        def products(pe, out, s, k, hi, lo, first, last):
            wl, wh = w_lo[s][:, k * P:(k + 1) * P], w_hi[s][:, k * P:(k + 1) * P]
            pe.matmul(out, wl, hi, start=first, stop=False)
            pe.matmul(out, wh, lo, start=False, stop=False)
            return pe.matmul(out, wh, hi, start=False, stop=last)

        def pe_unit(pe, bank, s, q, hi, lo, ready=None):
            pe.wait_ge(lo_done[s], q + 1)
            for k in range(KC):
                if ready:
                    ready(k)
                mm = products(pe, ps[:, bank, :], s, k, hi[:, k, :], lo[:, k, :], k == 0, k == KC - 1)
            mm.then_inc(unit_done[s], 1)

        def pe_start(pe):
            pe.wait_ge(S["const_ready"], 1)
            for k in range(KC):
                pe.wait_ge(S["norm_sq"], k + 1)
                pe.matmul(ps[:, 4, :], ones[:, :], sq0[k % 2][:, 0:T], start=(k == 0), stop=(k == KC - 1))
                pe.matmul(ps[:, 5, 0:CTX], ones[:, :], sq0[k % 2][:, T:TC], start=(k == 0), stop=(k == KC - 1))\
                  .then_inc(S["sq0_mm"], 1)
            pe.wait_ge(S["dd_split"], 1)
            for k in range(KC):
                pe.wait_ge(S["h_lo"], k + 1)
                wl, wh = dd_lo[:, k * P:(k + 1) * P], dd_hi[:, k * P:(k + 1) * P]
                for out, hi, lo in ((ps[:, 6, :], h1_hi, h1_lo), (ps[:, 7, 0:CTX], hc_hi, hc_lo)):
                    pe.matmul(out, wl, hi[:, k, :], start=(k == 0), stop=False)
                    pe.matmul(out, wh, lo[:, k, :], start=False, stop=False)
                    mm = pe.matmul(out, wh, hi[:, k, :], start=False, stop=(k == KC - 1))
                if k == KC - 1:
                    mm.then_inc(S["dd_mm"], 1)
                for s in range(4):
                    pe.wait_ge(lo_done[s], 1)
                    mm = products(pe, ps[:, s, :], s, k, h1_hi[:, k, :], h1_lo[:, k, :], k == 0, k == KC - 1)
                    if k == KC - 1:
                        mm.then_inc(unit_done[s], 1)

        def pe_qkv(pe):
            def unit(u):
                s, q, bank = u % 4, u // 4, u % 2
                pe.wait_ge(lo_done[s], q + 1)
                pe.wait_ge(S["qkv_lat_read"], u if u >= 6 else u - 2)
                for k in range(KC):
                    mm = products(pe, ps[:, bank, :], s, k, h1_hi[:, k, :], h1_lo[:, k, :], k == 0, k == KC - 1)
                pe.wait_ge(*((S["qkv_ctx_read"], u - 4) if u >= 6 else (S["qkv_lat_read"], u)))
                for k in range(KC):
                    mm = products(pe, ps[:, 2 + bank, 0:CTX], s, k, hc_hi[:, k, :], hc_lo[:, k, :],
                                  k == 0, k == KC - 1)
                mm.then_inc(unit_done[s], 1)

            def v_turn(m):
                pe.wait_ge(S["qkv_lat_read"], m + 10)
                pe.wait_ge(S["qkv_ctx_read"], m + 6)
                if m >= 2:
                    pe.wait_ge(S["v_read"], m - 1)
                for c in range(TTC):
                    mm = pe.transpose(ps[:, (4 if c < TT else 6) + m % 2, (c % TT) * P:(c % TT + 1) * P],
                                      vT[m % 2][:, c * P:(c + 1) * P], ident[:, :])
                mm.then_inc(S["v_turned"], 1)

            for u in range(4, 16):
                unit(u)
                if u > 8:
                    v_turn(u - 9)
            v_turn(7)

        def pe_gla(pe):
            pe.wait_ge(S["v_read"], 8)
            def head(h):
                for d in range(2):
                    w = 2 * h + d
                    pe.wait_ge(S["w_up_copied"], w + 1)
                    wait_former(pe, S["kd_read"], 2 * w)
                    wait_former(pe, S["state_step"], 11 * w)
                    if d == 0:
                        wait_former(pe, S["oT_read_a"], h)
                        wait_former(pe, S["oT_read_d"], h)
                    pe.matmul(ps[:, 6, :], w_up_h[:, :], dd_sb[:, 0:T], start=True, stop=True)
                    pe.matmul(ps[:, 7, 0:CTX], w_up_h[:, :], dd_sb[:, T:TC], start=True, stop=True)\
                      .then_inc(S["z_mm"], 1)
                    for s, (name, n) in enumerate((("kd_read", 2 * w), ("scores_read", w), ("state_step", 11 * w),
                                                   ("state_step", 11 * w))):
                        wait_former(pe, S[name], n)
                        pe_unit(pe, s, s, w + Q_GLA, h1_hi, h1_lo)
                    pe.wait_ge(S["decayed"], 4 * w + 1)
                    pe.wait_ge(S["decay_sum"], 5 * w + 1)
                    pe.wait_ge(S["z_log"], 3 * w + 1)
                    for c in range(TT, TTC):
                        mm = pe.transpose(ps[:, 6, (c - TT) * P:(c - TT + 1) * P], k_dec[:, c * P:(c + 1) * P], ident[:, :])
                    mm.then_inc(S["kd_scores_mm"], 1)
                    pe.wait_ge(S["cc_read"], w + 1)
                    for c in range(TT):
                        mm = pe.transpose(ps[:, 0, c * P:(c + 1) * P], k_dec[:, c * P:(c + 1) * P], ident[:, :])
                    mm.then_inc(S["kd_scores_mm"], 1)
                    pe.wait_ge(S["decayed"], 4 * w + 2)
                    pe.wait_ge(S["decayed"], 4 * w + 3)
                    pe.wait_ge(S["conv3"], 5 * w + 1)
                    for c in range(TT):
                        mm = pe.matmul(ps[:, 1, c * P:(c + 1) * P], k_mid[:, c * P:(c + 1) * P],
                                       q_mid[:, c * P:(c + 1) * P], start=True, stop=True)
                    mm.then_inc(S["kd_scores_mm"], 1)
                    order = [8, 9, 10, 11, *range(8)] if d == 0 else [11, 10, 9, 8, *range(7, -1, -1)]

                    def k_v(p):
                        if p == 0:
                            pe.wait_ge(S["conv3"], 5 * w + 5)
                            pe.wait_ge(S["v_h_ready"], h + 1)
                            pe.wait_ge(S["kd_read"], 2 * w + 1)
                            pe.wait_ge(S["g_read"], w + 1)
                        else:
                            pe.wait_ge(S["kd_read"], 2 * w + 2)
                            if p >= 2:
                                pe.wait_ge(S["state_step"], 11 * w + 2 * (p - 1))
                        for n in (2 * p, 2 * p + 1):
                            if n < 11:
                                c, rows = order[n] // 2, slice(order[n] % 2 * CH, order[n] % 2 * CH + CH)
                                pe.matmul(ps[:, (2, 3, 6, 7)[n % 4], 0:HEAD_V],
                                          kd_tok[rows, c, :], v_h[rows, c, :], start=True, stop=True)\
                                  .then_inc(S["kv_mm"], 1)

                    def o_at(c, rows=slice(0, P)):
                        return ps[rows, 4 + c // 2, (c % 2) * HEAD_V:(c % 2 + 1) * HEAD_V]

                    def inter(i):
                        pe.wait_ge(S["state_step"], 11 * w + 4 + i)
                        g = order[4 + i]
                        rows = slice(g % 2 * CH, g % 2 * CH + CH)
                        pe.matmul(o_at(g // 2, rows), q_dec[:, g * CH:(g + 1) * CH], state[(4 + i) % 3][:, :],
                                  start=False, stop=(i == 7 and d == 1), skip_group_check=True)\
                          .then_inc(S["inter_mm"], 1)

                    k_v(0)
                    k_v(1)
                    pe.wait_ge(S["scores_read"], w + 1)
                    if d == 0:
                        wait_former(pe, S["o_tok_ready"], 2 * h)
                    for c in range(TT):
                        pe.matmul(o_at(c), s_dir[d][:, c, :], v_h[:, c, :], start=(d == 0 and c % 2 == 0), stop=False,
                                  skip_group_check=True)
                    k_v(2)
                    pe.wait_ge(S["decayed"], 4 * w + 4)
                    for p in range(3, 6):
                        k_v(p)
                        inter(2 * p - 6)
                        inter(2 * p - 5)
                    inter(6)
                    inter(7)
                pe.wait_ge(S["o_tok_ready"], 2 * h + 2)
                for c in range(TT):
                    for half in range(2):
                        mm = pe.transpose(ps[:, 6 + half, c * P:(c + 1) * P],
                                          o_tok[:, c, half * P:(half + 1) * P], ident[:, :])
                mm.then_inc(S["oT_mm"], 1)

            head(0)
            with pe.Fori(1, HEADS) as h:
                head(h)

        def pe_merge(pe):
            def merge(r):
                q = r + Q_MERGE
                for s, (hi, lo, done) in enumerate(((og_hi, og_lo, "og_lo"), (h1_hi, h1_lo, None),
                                                    (y_hi, y_lo, "y_lo"), (h1_hi, h1_lo, None))):
                    wait_former(pe, S["merge_a" if s < 2 else "merge_b"], r)
                    if done:
                        pe.wait_ge(S[done], KC)
                    pe_unit(pe, s, s, q, hi, lo)

            merge(0)
            with pe.Fori(1, KC) as r:
                merge(r)

        def pe_columns(pe, q0, n, hi, lo, free, ready=None):
            for r in range(n):
                for s in range(4):
                    free(s, r)
                    pe_unit(pe, s, s, q0 + r, hi, lo, ready if r == 0 and s == 0 else None)

        def pe_mix(pe):
            pe.wait_ge(S["mg_lo"], KC)

            def free(s, r):
                pe.wait_ge(*((S["merge_b"], KC) if r == 0 else (S["resid_x"], s + 1)))

            pe_columns(pe, Q_MIX, 2, mg_hi, mg_lo, free)

        def pe_norm(pe, n_acc):
            pe.wait_ge(S["norm_acc"], n_acc)
            pe.matmul(ps[:, 6, :], ones[:, :], acc[:, :], start=True, stop=True).then_inc(S["norm_stat"], 1)

        def h_ready(pe, base):
            return lambda k: pe.wait_ge(S["h_lo"], base + k + 1)

        def pe_ffn(pe, e, h_base, resid_base, n_acc=None):
            def hidden(r):
                q = r + Q_FFI[e]
                for s in range(4):
                    if s % 2 == 0:
                        wait_former(pe, S[f"ffn_val{s // 2}"], r + 11 * e)
                    if isinstance(r, int):
                        pe.wait_ge(S["resid_x"], resid_base - 3 + s)
                    pe_unit(pe, s, s, q, h_hi, h_lo, h_ready(pe, h_base) if s == 0 else None)
                    if isinstance(r, int) and s == 0 and n_acc:
                        pe_norm(pe, n_acc)

            hidden(0)
            with pe.Fori(1, FC // 2) as r:
                hidden(r)
            with pe.Fori(0, KC // 2) as m:
                for p in range(2):
                    q = 2 * m + (p + Q_FFO[e])
                    for i in range(2):
                        pe.wait_ge(S[f"ffn_lo{i}"], 11 * (e + 1))
                    pe.wait_ge(S["resid_x"], 2 * m + (p + resid_base - 1))
                    for s in range(4):
                        pe.wait_ge(lo_done[s], q + 1)
                        for k in range(FFO[s]):
                            g = FFO_AT[s] + k
                            mm = products(pe, ps[:, 4 + p, :], s, k, gu_hi[:, g, :], gu_lo[:, g, :], g == 0, g == FC - 1)
                        mm.then_inc(unit_done[s], 1)

        def pe_cp(pe):
            for r in range(2):
                for s in range(4):
                    wait_former(pe, S[f"conv_in{s // 2}"], r)
                    pe_unit(pe, s, s, r + Q_CPI, h_hi, h_lo, h_ready(pe, 16) if s == 0 else None)
                    if r == 0 and s == 0:
                        pe_norm(pe, 7 + 2 * 7)
                        pe.matmul(ps[:, 7, :], ones[:, :], acc2[:, :], start=True, stop=True).then_inc(S["norm_stat"], 1)
            for s in range(4):
                pe.wait_ge(S[f"conv_in{s // 2}"], 2)
                pe_unit(pe, s, s, Q_CPI + 2, h_hi, h_lo)
            pe.wait_ge(S["conv_in1"], 2)
            for i in range(CONVW):
                pe.wait_ge(S["tap_ready"], i + 1)
                pe.matmul(ps[:, 4, :], tap[i % 4][:, :], a_sb[:, 3, i:i + T], start=(i == 0), stop=(i == CONVW - 1))\
                  .then_inc(S["tap_mm"], 1)
            pe.wait_ge(S["small_in"], 64)
            for g in range(CPC):
                pe.wait_ge(S["pd_ready"], g + 1)
                pe.wait_ge(S["cp_u"], g + 1)
                pe.matmul(ps[:, g, :], pool_w[:, g, :], pd[:, g, :], start=True, stop=True).then_inc(S["pool_mm"], 1)
            for name, n in (("conv_dve", 3 * CONVW), ("conv_pe", 1)):
                pe.wait_ge(S[name], n)
            for g in range(CPC):
                mm = pe.matmul(ps[:, 5, :], ones[:, :], cv[:, g, :], start=(g == 0), stop=(g == CPC - 1))
            mm.then_inc(S["ln_sum"], 1)

            pe.wait_ge(S["ln_sq"], CPC)
            for g in range(CPC):
                mm = pe.matmul(ps[:, 6, :], ones[:, :], csq[:, g, :], start=(g == 0), stop=(g == CPC - 1))
            mm.then_inc(S["norm_stat"], 1)

            def free(s, r):
                pe.wait_ge(*((S["cat_lo_p"], s + 1) if r == 0 else (S["resid_x"], 16 + s + 1)))

            def ready(k):
                pe.wait_ge(*((S["cat_lo_a"], k + 1) if k < CPC else (S["cat_lo_p"], k - CPC + 1)))

            pe_columns(pe, Q_CPO, 2, cat_hi, cat_lo, free, ready)

        def pe_hg(pe):
            taken = ("hg_f_read", "hg_q_read", "hg_i_read", "hg_g_read")

            def units(w, free, ready=None, between=None):
                for s in range(4):
                    free(s)
                    pe_unit(pe, s, s, w + Q_HG, h_hi, h_lo, ready if s == 0 else None)
                    if s == 1 and between:
                        between()

            def turn_back(g):
                pe.wait_ge(S["ho_tok_ready"], g + 1)
                pe.wait_ge(S["hkd_tok_ready"], g + 1)
                for c in range(TT):
                    mm = pe.transpose(ps[:, 4, c * P:(c + 1) * P], ho_tok[:, c, :], ident[:, :])
                mm.then_inc(S["hoT_mm"], 1)

            def mix(g, par, heads_taken):
                pe.wait_ge(S["hkd_ready"], g + 1)
                wait_former(pe, S["hval_ready"], g)
                for c in range(TT):
                    mm = pe.transpose(ps[:, 4, c * P:(c + 1) * P], hkd[:, c * P:(c + 1) * P], ident[:, :])
                mm.then_inc(S["hkd_mm"], 1)
                pe.wait_ge(S["hg_i_read"], g + 1)
                wait_former(pe, S["ho_tok_ready"], g)
                for c in range(TT):
                    mm = pe.transpose(ps[:, 5, c * P:(c + 1) * P], hv[par][:, c * P:(c + 1) * P], ident[:, :])
                mm.then_inc(S["hv_mm"], 1)
                for l in range(7):
                    if l < 4:
                        pe.wait_ge(S[taken[l]], heads_taken)
                    else:
                        pe.wait_ge(S["hg_scores_read"], 7 * g + l - 3)
                    if l:
                        pe.wait_ge(S["hx_ready"], 12 * g + 2 * l)
                    for c in range(TT):
                        cols = slice(c * P, (c + 1) * P)
                        a, b = (hk[par], hq[par]) if l == 0 else (hx[l - 1], hx[l - 1])
                        mm = pe.matmul(ps[:, l % 4, cols], a[:, cols], b[:, cols], start=True, stop=True)
                    mm.then_inc(S["hg_scores_mm"], 1)
                pe.wait_ge(S["hkd_tok_ready"], g + 1)
                pe.wait_ge(S["hv_tok_ready"], g + 1)
                wait_former(pe, S["hg_state"], 7 * g)
                for n in range(7):
                    rows = slice(n % 2 * CH, n % 2 * CH + CH)
                    pe.matmul(ps[:, 6 + n % 2, (n // 2) * P:(n // 2 + 1) * P], hkd_tok[rows, n // 2, :],
                              hv_tok[rows, n // 2, :], start=True, stop=True).then_inc(S["hkv_mm"], 1)
                pe.wait_ge(S["hg_scores_read"], 7 * g + 7)
                for c in range(TT):
                    pe.matmul(ps[:, 5, c * P:(c + 1) * P], hs[:, c, :], hv_tok[:, c, :], start=(c == 0), stop=False,
                              skip_group_check=True)
                pe.wait_ge(S["hqb_ready"], g + 1)
                for n in range(1, NCH):
                    pe.wait_ge(S["hg_state"], 7 * g + n)
                    rows = slice(n % 2 * CH, n % 2 * CH + CH)
                    mm = pe.matmul(ps[rows, 5, (n // 2) * P:(n // 2 + 1) * P], hqb[:, n * CH:(n + 1) * CH], hst[:, n, :],
                                   start=False, stop=(n == NCH - 1), skip_group_check=True)
                mm.then_inc(S["ho_mm"], 1)

            units(0, lambda s: pe.wait_ge(S["cat_lo_p"], 4), ready=h_ready(pe, 32))
            units(1, lambda s: pe.wait_ge(S[taken[s]], 1))
            mix(0, 0, 2)
            last_score = (5, 6, 7, 4)
            with pe.Fori(0, 3) as m:
                for p in range(2):
                    units(2 * m + (2 + p), lambda s: pe.wait_ge(S["hg_scores_read"], 14 * m + (7 * p + last_score[s])),
                          between=lambda: turn_back(2 * m + p))
                    mix(2 * m + (1 + p), 1 - p, 2 * m + (3 + p))
            turn_back(6)
            mix(7, 1, HG)
            turn_back(7)

            def free(s, r):
                pe.wait_ge(*((S["hg_scores_read"], 7 * HG) if r == 0 else (S["resid_x"], 32 + s + 1)))

            pe_columns(pe, Q_HGO, 2, r_hi, r_lo, free, lambda k: pe.wait_ge(S["r_lo"], k + 1))

        @block.tensor
        def _(pe):
            pe_start(pe)
            pe_qkv(pe)
            pe_gla(pe)
            pe_merge(pe)
            pe_mix(pe)
            pe_norm(pe, 7)
            pe_ffn(pe, 0, 8, 8)
            pe_cp(pe)
            pe_ffn(pe, 1, 24, 24, 7 * 4)
            pe_norm(pe, 7 * 5)
            pe_hg(pe)
            pe_ffn(pe, 2, 40, 40, 7 * 6)
            pe_norm(pe, 7 * 7)

        def act_hi(act, s, q, n=D):
            act.wait_ge(raw_full[s], 16 * (q + 1))
            wait_former(act, unit_done[s], q)
            act.activation(w_hi[s][:, 0:n], raw[s][:, 0:n], ACT.Copy).then_inc(hi_done[s], 1)

        def act_start(act):
            act.wait_ge(S["dve_step"], 3)
            act.activation(lb_t[:, :], lb_t[:, :], ACT.Exp).then_inc(S["cond_ready"], 1)
            act.wait_ge(S["small_in"], 16)
            act.activation(cond[:, :, :], cond[:, :, :], ACT.Silu).then_inc(S["cond_ready"], 1)
            act.wait_ge(S["x_in"], 32)
            for k in range(KC):
                if k >= 2:
                    act.wait_ge(S["sq0_mm"], k - 1)
                act.activation(sq0[k % 2][:, :], x_all[:, k, :], ACT.Square).then_inc(S["norm_sq"], 1)
            act.wait_ge(S["sq0_mm"], KC)
            act.wait_ge(S["const_ready"], 1)
            act.activation(rstd0[:, :], ps[:, 4:6, :].rearrange("p a n -> p (a n)")[:, 0:TC], ACT.Sqrt, bias=eps[:, :],
                           scale=1.0 / D).then_inc(S["norm_rms"], 1)
            act.wait_ge(S["dd_in"], 48)
            act.activation(dd_hi[:, :], dd_raw[:, :], ACT.Copy).then_inc(S["dd_hi"], 1)
            sides = ((slice(0, T), h1_hi), (slice(T, TC), hc_hi))
            for k in range(KC):
                if k < 4:
                    act_hi(act, k, 0)
                act.wait_ge(S["x_normed"], k + 1)
                act.wait_ge(S["mod1_ready"], 2 * k + 2)
                for v, (cols, _) in enumerate(sides):
                    ins = act.activation(x_all[:, k, cols], x_all[:, k, cols], ACT.Identity, bias=mod1[:, k, v:v + 1],
                                         scale=amp1[:, k, v:v + 1])
                ins.then_inc(S["h_val"], 1)
                act.wait_ge(S["h_val"], k + 1)
                for cols, hi in sides:
                    ins = act.activation(hi[:, k, :], x_all[:, k, cols], ACT.Copy)
                ins.then_inc(S["h_hi"], 1)

        def act_qkv(act):
            act.wait_ge(S["dd_mm"], 1)
            act.activation(dd_sb[:, 0:T], ps[0:32, 6, :], ACT.Copy).then_inc(S["qkv_lat_read"], 1)
            for u in range(16):
                s, q = u % 4, u // 4
                act.wait_ge(unit_done[s], q + 1)
                if u < 4:
                    act.activation(q_sb[:, s, :], ps[:, s, :], ACT.Copy, scale=float(P) ** -0.5)\
                       .then_inc(S["qkv_lat_read"], 1)
                elif u < 8:
                    act.activation(k_sb[:, s, 0:T], ps[:, u % 2, :], ACT.Copy).then_inc(S["qkv_lat_read"], 1)
                else:
                    if u >= 10:
                        act.wait_ge(S["v_turned"], u - 9)
                    act.activation(vT[u % 2][:, 0:T], ps[:, u % 2, :], ACT.Copy).then_inc(S["qkv_lat_read"], 1)
                act_hi(act, s, q + 1)

        def act_gla(act):
            act.wait_ge(S["v_read"], 8)
            def head(h):
                for d in range(2):
                    w = 2 * h + d
                    wait_former(act, S["z_mm"], w)
                    wait_apart(act, S["decay_sum"], 5 * w)
                    act.activation(b_dec_h[:, :], v_dyn("b_dec", h + 4 * d), ACT.Copy).then_inc(S["b_dec_copied"], 1)
                    act.activation(w_up_h[:, :], at_index(w_up[:, d, :, :], h), ACT.Copy).then_inc(S["w_up_copied"], 1)
                    if d == 0:
                        wait_apart(act, S["inter_mm"], 16 * h)
                        act.activation(v_h[:, :, :].rearrange("p c v -> p (c v)"), at_index(v_sb, h), ACT.Copy)\
                           .then_inc(S["v_h_ready"], 1)
                        wait_former(act, S["oT_mm"], h)
                    act.wait_ge(S["z_mm"], w + 1)
                    act.wait_ge(S["b_dec_copied"], w + 1)
                    act.activation(t0[:, :], z_ps[:, 0:TC], ACT.Abs, bias=b_dec_h[:, :]).then_inc(S["z_log"], 1)
                    act.wait_ge(S["z_log"], 3 * w + 1)
                    act.activation(t0[:, :], t0[:, :], ACT.Exp, scale=-1.0).then_inc(S["z_log"], 1)
                    act.wait_ge(S["z_log"], 3 * w + 2)
                    act.activation(t0[:, :], t0[:, :], ACT.Ln, bias=ones[:, 0:1]).then_inc(S["z_log"], 1)
                    inv = 1.0 / DECAY_TAU
                    act.wait_ge(S["decay_sum"], 5 * w + 4)
                    wait_former(act, S["kd_scores_mm"], 3 * w)
                    act.activation(k_dec[:, :], t1[:, :], ACT.Exp, scale=inv).then_inc(S["decay_exp"], 1)
                    act.wait_ge(S["decay_sum"], 5 * w + 5)
                    wait_former(act, S["kd_scores_mm"], 3 * w)
                    act.activation(q_mid[:, :], t0[:, 0:T], ACT.Exp, scale=inv).then_inc(S["decay_exp"], 1)
                    act.activation(k_mid[:, :], t0[:, 0:T], ACT.Exp, scale=-inv).then_inc(S["decay_exp"], 1)
                    wait_former(act, S["inter_mm"], 8 * w)
                    act.activation(q_dec[:, :], t2[:, 0:T], ACT.Exp, scale=inv).then_inc(S["decay_exp"], 1)
                    wait_former(act, S["state_step"], 11 * w)
                    act.activation(dec[:, :], t2[:, W_LAST[d]:TC:CH], ACT.Exp, scale=inv).then_inc(S["decay_exp"], 1)
                    q = w + Q_GLA
                    act.wait_ge(unit_done[0], q + 1)
                    wait_former(act, S["conv3"], 5 * w)
                    act.activation(cc_sb[:, :], ps[:, 0, :], ACT.Copy).then_inc(S["cc_read"], 1)
                    for s in range(3):
                        act_hi(act, s, q + 1)
                    wait_apart(act, unit_done[3], q + 1)
                    act.activation(at_index(g_sb, w), ps[:, 3, :], ACT.Copy).then_inc(S["g_read"], 1)
                    act_hi(act, 3, q + 1)
                    wait_former(act, S["kv_mm"], 11 * w)
                    act.wait_ge(S["kd_scores_mm"], 3 * w + 1)
                    act.activation(kd_tok[:, TT:TTC, :].rearrange("p c k -> p (c k)"), ps[:, 6, 0:CTX], ACT.Copy)\
                       .then_inc(S["kd_read"], 1)
                    act.wait_ge(S["kd_scores_mm"], 3 * w + 2)
                    act.activation(kd_tok[:, 0:TT, :].rearrange("p c k -> p (c k)"), ps[:, 0, :], ACT.Copy)\
                       .then_inc(S["kd_read"], 1)
                act.wait_ge(S["inter_mm"], 16 * h + 16)
                for c in range(TT):
                    squares = t1[:, T:TC] if c == 3 else t2[:, c * HEAD_V:(c + 1) * HEAD_V]
                    act.activation(squares, ps[:, 4 + c // 2, (c % 2) * HEAD_V:(c % 2 + 1) * HEAD_V], ACT.Square,
                                   accum_out=o_ss[:, c:c + 1]).then_inc(S["o_ss"], 1)
                act.wait_ge(S["o_ss"], 5 * h + 4)
                act.activation(o_rs[:, :], o_ss[:, :], ACT.Sqrt, bias=eps[:, :], scale=1.0 / HEAD_V).then_inc(S["o_ss"], 1)
                act.wait_ge(S["oT_mm"], h + 1)
                act.activation(spare[:, 8:9], eps[:, :], ACT.Copy)
                act.activation(at_index(v_sb, h)[:, 0:T], ps[:, 6, :], ACT.Copy).then_inc(S["oT_read_a"], 1)

            head(0)
            with act.Fori(1, HEADS) as h:
                head(h)

        def act_gated(act):
            for j in range(KC + 1):
                if j < KC:
                    if j >= 2:
                        act.wait_ge(S["og_val"], j - 1)
                    act.activation(og_sg[j % 2][:, :], g_sb[:, j, :], ACT.Silu).then_inc(S["og_sg"], 1)
                if j >= 1:
                    act.wait_ge(S["og_val"], j)
                    act.activation(og_hi[:, j - 1, :], og_val[(j - 1) % 2][:, :], ACT.Copy).then_inc(S["og_hi"], 1)
            for k in range(KC):
                act.activation(y_hi[:, k, :], y_sb[:, k, :], ACT.Copy).then_inc(S["y_hi"], 1)

        def act_merge(act):
            act.wait_ge(S["small_in"], 32)
            act.activation(cond2, ada_w[1][:, :], ACT.Silu).then_inc(S["cond_ready"], 1)
            act.wait_ge(S["y_lo"], KC)
            def merge(r):
                q = r + Q_MERGE
                wait_former(act, S["merge_a"], r)
                act.wait_ge(unit_done[1], q + 1)
                act.activation(sig_a[:, :], ps[:, 1, :], ACT.Sigmoid).then_inc(S["sig_a"], 1)
                act_hi(act, 0, q + 1)
                act_hi(act, 1, q + 1)
                wait_former(act, S["merge_b"], r)
                act.wait_ge(unit_done[3], q + 1)
                act.activation(sig_b[:, :], ps[:, 3, :], ACT.Sigmoid).then_inc(S["sig_b"], 1)
                act_hi(act, 2, q + 1)
                act_hi(act, 3, q + 1)
                wait_apart(act, S["merged"], r + 1)
                act.activation(at_index(mg_hi, r), mrg_v[:, :], ACT.Copy).then_inc(S["mg_hi"], 1)

            merge(0)
            with act.Fori(1, KC) as r:
                merge(r)

        def act_square(act, i, n):
            wait_former(act, S["norm_acc"], 7 * (i - 1) + (max(1, n - 2) if n >= 2 else 0))
            act.activation(sq[n % 2][:, :], x[:, n, :], ACT.Square).then_inc(S["norm_sq"], 1)

        def act_high(act, n, gain):
            act.activation(h_hi[:, n, :], x[:, n, :], ACT.Copy, scale=gain).then_inc(S["h_hi"], 1)

        def act_resid(act, i, q0, resid_base, per_round, sizes, last=False, gain=None, twice=False):
            for n in range(KC):
                r, s0 = (n, 0) if per_round == 1 else (n // 4, n % 4)
                for s in (range(4) if per_round == 1 else (s0,)):
                    if not (last and r == KC // per_round - 1):
                        act_hi(act, s, q0 + r + 1, sizes[s] if r < KC // per_round - 1 else D)
                act.wait_ge(S["resid_x"], resid_base + n + 1)
                if gain:
                    act_high(act, n, gain(n))
                if not twice:
                    act_square(act, i, n)
                    continue
                wait_former(act, S["norm_acc"], 7 * (i - 1) + 2 * max(0, n - 1))
                for j, (total, scale) in enumerate(((acc, 1.0), (acc2, v_at("g_final", n)))):
                    act.activation((total if n == 0 else sq[j])[:, :], x[:, n, :], ACT.Square, scale=scale)\
                       .then_inc(S["norm_sq"], 1)

        def act_rms(act, i, n=D):
            act.wait_ge(S["norm_stat"], i)
            act.activation(rstd[:, :], ps[:, 6, :], ACT.Sqrt, bias=eps[:, :], scale=1.0 / n).then_inc(S["norm_rms"], 1)

        def act_split(act, val_base, shift=None):
            for k in range(KC):
                act.wait_ge(S["h_val"], val_base + k + 1)
                if shift is None:
                    act.activation(h_hi[:, k, :], nv[k % 2][:, :], ACT.Copy).then_inc(S["h_hi"], 1)
                else:
                    act.activation(h_hi[:, k, :], nv[k % 2][:, :], ACT.Identity, bias=shift[:, k:k + 1])\
                       .then_inc(S["h_hi"], 1)

        FFO_N = [n * P for n in FFO]

        def act_ffn(act, e, i, resid_base, last=False, gain=None, twice=False):
            def hidden(r):
                q = r + Q_FFI[e]
                for p in range(2):
                    if e == 0:
                        act.wait_ge(unit_done[2 * p], q + 1)
                        wait_former(act, S[f"ffn_val{p}"], r)
                        act.activation(sa[p][:, :], ps[:, 2 * p, :], ACT.Silu).then_inc(S[f"ffn_sa{p}"], 1)
                    else:
                        act.wait_ge(S[f"ffn_scaled{p}"], 2 * r + (22 * (e - 1) + 1))
                        act.activation(sa[p][:, :], sa[p][:, :], ACT.Silu).then_inc(S[f"ffn_sa{p}"], 1)
                    for s in (2 * p, 2 * p + 1):
                        act_hi(act, s, q + 1)
                    wait_apart(act, S[f"ffn_val{p}"], r + (11 * e + 1))
                    act.activation(at_index(gu_hi, 2 * r + p), fval[p][:, :], ACT.Copy).then_inc(S[f"ffn_hi{p}"], 1)

            hidden(0)
            with act.Fori(1, FC // 2) as r:
                hidden(r)
            act_resid(act, i, Q_FFO[e], resid_base, 1, FFO_N, last, gain, twice)

        def act_cp(act):
            for r in range(2):
                q = r + Q_CPI
                for p in range(2):
                    act.wait_ge(S["cp_scaled"], 4 * r + 2 * p + 1)
                    act.activation(csg[p][:, :], csg[p][:, :], ACT.Sigmoid).then_inc(S[f"conv_sg{p}"], 1)
                    act_hi(act, 2 * p, q + 1)
                    act_hi(act, 2 * p + 1, q + 1)
            for s in range(4):
                act.wait_ge(unit_done[s], Q_CPI + 3)
                act.activation(u_sb[:, s, UPAD:], ps[:, s, :], ACT.Copy).then_inc(S["cp_u"], 1)
                act_hi(act, s, Q_CPO)
            for i in range(CONVW):
                if i >= 4:
                    act.wait_ge(S["tap_mm"], i - 3)
                act.activation(tap[i % 4][:, :], ident[:, :], ACT.Copy, scale=v_at("dw_w", 3 * CONVW + i))\
                   .then_inc(S["tap_ready"], 1)
            act.wait_ge(S["tap_mm"], CONVW)
            act.activation(cv[:, 3, :], ps[:, 4, :], ACT.Identity, bias=v_at("dw_b", 3)).then_inc(S["conv_pe"], 1)
            for g in range(CPC):
                act.wait_ge(S["pool_mm"], g + 1)
                act.activation(cat_hi[:, CPC + g, :], ps[:, g, :], ACT.Copy, scale=v_at("pool_scale", g))\
                   .then_inc(S["cat_hi_p"], 1)
            for g in range(CPC):
                act.wait_ge(S["ln_centred"], g + 1)
                act.activation(csq[:, g, :], cv[:, g, :], ACT.Square).then_inc(S["ln_sq"], 1)
            act_rms(act, 4, CPC * P)
            for g in range(CPC):
                act.wait_ge(S["ln_val"], g + 1)
                if g >= 2:
                    act.wait_ge(S["cat_lo_a"], g - 1)
                act.activation(lns[g % 2][:, :], lnv[g % 2][:, :], ACT.Silu, bias=v_at("ln_b", g)).then_inc(S["ln_silu"], 1)
                act.wait_ge(S["ln_silu"], g + 1)
                act.activation(cat_hi[:, g, :], lns[g % 2][:, :], ACT.Copy).then_inc(S["cat_hi_a"], 1)

        def act_hg(act):
            def decays(g, par):
                act.wait_ge(S["hf_ready"], g + 1)
                act.activation(hlf[:, :], hlf[:, :], ACT.Ln).then_inc(S["hlog_ready"], 1)
                act.wait_ge(S["hd_ready"], 7 * g + 1)
                wait_former(act, S["hkd_mm"], g)
                act.activation(hkd[:, :], hd[0][:, :], ACT.Exp).then_inc(S["hd_used"], 1)
                wait_former(act, S["ho_mm"], g)
                act.activation(hqb[:, :], hb[par][:, :], ACT.Exp).then_inc(S["hqb_exp"], 1)
                wait_former(act, S["hg_state"], 7 * g)
                act.activation(hdec[:, :], hb[par][:, CH - 1:T:CH], ACT.Exp).then_inc(S["hdec_ready"], 1)
                for i, m in enumerate(LEVELS):
                    act.wait_ge(S["hd_ready"], 7 * g + i + 2)
                    wait_former(act, S["hx_ready"], 12 * g + 2 * max(i - 1, 0))
                    for half, scale in ((0, -1.0), (1, 1.0)):
                        def part(t):
                            return t[:, :].rearrange("p (b a m) -> p b a m", a=2, m=m)[:, :, half, :]
                        act.activation(part(he[i % 2]), part(hd[(i + 1) % 2]), ACT.Exp, scale=scale)\
                           .then_inc(S["hd_used"], 1)

            def take(w, par, between=None):
                q = w + Q_HG
                act.wait_ge(unit_done[0], q + 1)
                wait_former(act, S["hf_ready"], w)
                act.activation(hsf[:, :], ps[:, 0, :], ACT.Sigmoid).then_inc(S["hg_f_read"], 1)
                act_hi(act, 0, q + 1)
                act.wait_ge(unit_done[1], q + 1)
                act.activation(hq[par][:, :], ps[:, 1, :], ACT.Copy).then_inc(S["hg_q_read"], 1)
                act_hi(act, 1, q + 1)
                if between:
                    between()
                act.wait_ge(unit_done[2], q + 1)
                act.activation(hv[par][:, :], ps[:, 2, :], ACT.Copy).then_inc(S["hg_i_read"], 1)
                act_hi(act, 2, q + 1)
                act.wait_ge(unit_done[3], q + 1)
                act.activation(hg[par][:, :], ps[:, 3, :], ACT.Sigmoid).then_inc(S["hg_sig"], 1)
                act_hi(act, 3, q + 1)

            def high(g):
                wait_apart(act, S["hval_ready"], g + 1)
                act.activation(at_index(r_hi, g), hval[:, :], ACT.Copy).then_inc(S["r_hi"], 1)

            def mix(g):
                act.wait_ge(S["hkd_mm"], g + 1)
                wait_former(act, S["hkv_mm"], 7 * g)
                act.activation(hkd_tok[:, :, :].rearrange("p c k -> p (c k)"), ps[:, 4, :], ACT.Copy)\
                   .then_inc(S["hkd_tok_ready"], 1)
                act.wait_ge(S["ho_mm"], g + 1)
                for c in range(TT):
                    act.activation(hsquares[:, c * P:(c + 1) * P], ps[:, 5, c * P:(c + 1) * P], ACT.Square, accum_out=o_ss[:, c:c + 1])\
                       .then_inc(S["ho_ss"], 1)
                act.wait_ge(S["ho_ss"], 5 * g + 4)
                act.activation(o_rs[:, :], o_ss[:, :], ACT.Sqrt, bias=eps[:, :], scale=1.0 / P).then_inc(S["ho_ss"], 1)

            take(0, 0)
            decays(0, 0)
            take(1, 1)
            mix(0)
            with act.Fori(0, 3) as m:
                for p in range(2):
                    decays(2 * m + (1 + p), 1 - p)
                    take(2 * m + (2 + p), p, between=lambda: high(2 * m + p))
                    mix(2 * m + (1 + p))
            decays(7, 1)
            high(6)
            mix(7)
            high(7)

        @block.scalar
        def _(act):
            full = [D] * 4
            act_start(act)
            act_qkv(act)
            act_gla(act)
            act_gated(act)
            act_merge(act)
            act_resid(act, 1, Q_MIX, 0, 4, full)
            act_rms(act, 1)
            act_split(act, 8, mod2[:, 8:16])
            act_ffn(act, 0, 2, 8, gain=lambda k: gain_xg[:, k:k + 1], twice=True)
            act_rms(act, 2)
            act.wait_ge(S["dve_step"], 11)
            act.activation(rstd_xg[:, :], rstd_xg[:, :], ACT.Sqrt, bias=eps[:, :], scale=1.0 / D).then_inc(S["norm_rms"], 1)
            act_cp(act)
            act_resid(act, 4, Q_CPO, 16, 4, full, gain=lambda k: v_at("norm_ffn", k))
            act_rms(act, 5)
            act_ffn(act, 1, 5, 24)
            act_rms(act, 6)
            act_split(act, 16)
            act_hg(act)
            act_resid(act, 6, Q_HGO, 32, 4, full, gain=lambda k: v_at("norm_ffn", 8 + k))
            act_rms(act, 7)
            act_ffn(act, 2, 7, 40, last=True)
            act_rms(act, 8)

        def dve_start(dve):
            dve.wait_ge(S["vec_in"], 16)
            dve.tensor_tensor(lb[:, :], v_at("lb_logits", 0, HG), v_at("lb_logits", HG, HG), ALU.max).then_inc(S["dve_step"], 1)
            dve.wait_ge(S["dve_step"], 1)
            for i in range(2):
                dve.tensor_tensor(lb_t[:, i * HG:(i + 1) * HG], v_at("lb_logits", i * HG, HG), lb[:, :], ALU.subtract)\
                   .then_inc(S["dve_step"], 1)
            dve.memset(s_dir[0][:, :, :], 0.0).then_inc(S["zeros"], 1)
            dve.memset(s_dir[1][:, :, :], 0.0).then_inc(S["zeros"], 1)
            dve.wait_ge(S["cond_ready"], 1)
            dve.tensor_tensor(om_lb[:, :], lb_t[:, 0:HG], lb_t[:, HG:2 * HG], ALU.add).then_inc(S["dve_step"], 1)
            dve.wait_ge(S["dve_step"], 4)
            dve.reciprocal(om_lb[:, :], om_lb[:, :]).then_inc(S["dve_step"], 1)
            dve.wait_ge(S["dve_step"], 5)
            dve.tensor_tensor(lb[:, :], lb_t[:, HG:2 * HG], om_lb[:, :], ALU.mult).then_inc(S["dve_step"], 1)
            dve.wait_ge(S["dve_step"], 6)
            dve.tensor_scalar(om_lb[:, :], lb[:, :], -1.0, 1.0, ALU.mult, ALU.add).then_inc(S["dve_step"], 1)
            dve.tensor_tensor(gain_xg[:, :], v_at("g_final", 0, 8), v_at("norm_mix", 0, 8), ALU.mult)\
               .then_inc(S["dve_step"], 1)
            dve.wait_ge(S["cond_ready"], 2)

            def modulation(k):
                for i, n in enumerate((k, KC + k)):
                    a = 2 * k + i
                    dve.wait_ge(S[f"ada_full{a % 4}"], 16 * (a // 4 + 1))
                    if a:
                        dve.wait_ge(S["ada1_used"], a)
                    for v in range(2):
                        ins = dve.tensor_tensor_reduce(ada1_out[v][:, :], ada1_w[a % 4][:, :], cond[:, v, :], 1.0, 0.0,
                                                       ALU.mult, ALU.add, accum_out=mod1[:, n, v:v + 1])
                    ins.then_inc(S["ada1_used"], 1)
                both = slice(k, 2 * KC, KC)
                dve.wait_ge(S["ada1_used"], 2 * k + 2)
                dve.tensor_tensor(mod1[:, both, :], mod1[:, both, :], wide(vec[:, VEC["b_ada"]:VEC["b_ada"] + 16][:, both], 2),
                                  ALU.add).then_inc(S["mod1_ready"], 1)
                dve.wait_ge(S["mod1_ready"], 2 * k + 1)
                dve.tensor_scalar(amp1[:, k, :], mod1[:, KC + k, :], 1.0, v_at("g_mix", k), ALU.add, ALU.mult)\
                   .then_inc(S["mod1_ready"], 1)

            def low(k):
                dve.wait_ge(S["h_hi"], k + 1)
                dve.tensor_tensor(h1_lo[:, k, :], x_all[:, k, 0:T], h1_hi[:, k, :].bitcast(F32), ALU.subtract)
                dve.tensor_tensor(hc_lo[:, k, :], x_all[:, k, T:TC], hc_hi[:, k, :].bitcast(F32), ALU.subtract)\
                   .then_inc(S["h_lo"], 1)

            for k in range(KC):
                modulation(k)
                if k == 3:
                    dve.wait_ge(S["norm_rms"], 1)
                    dve.reciprocal(rstd0[:, :], rstd0[:, :]).then_inc(S["norm_recip"], 1)
                    dve.wait_ge(S["dd_hi"], 1)
                    dve.tensor_tensor(dd_lo[:, :], dd_raw[:, :], dd_hi[:, :].bitcast(F32), ALU.subtract)\
                       .then_inc(S["dd_split"], 1)
                if k >= 5:
                    low(k - 5)
            for k in range(3, KC):
                low(k)

        def dve_qkv(dve):
            dve.wait_ge(S["dd_mm"], 1)
            dve.tensor_copy(dd_sb[:, T:TC], ps[0:32, 7, 0:CTX]).then_inc(S["qkv_ctx_read"], 1)

            def v_read(m):
                dve.wait_ge(S["v_turned"], m + 1)
                i = m % 2
                out = v_sb[:, m // 2, :].rearrange("p (c v) -> p c v", v=HEAD_V)[:, :, i * P:(i + 1) * P]
                dve.tensor_copy(out[:, 0:TT, :], ps[:, 4 + i, :].rearrange("p (c v) -> p c v", v=P))
                dve.tensor_copy(out[:, TT:TTC, :], ps[:, 6 + i, 0:CTX].rearrange("p (c v) -> p c v", v=P))\
                   .then_inc(S["v_read"], 1)

            for u in range(4, 16):
                s, q = u % 4, u // 4
                dve.wait_ge(unit_done[s], q + 1)
                if u >= 10:
                    dve.wait_ge(S["v_turned"], u - 9)
                dve.tensor_copy(k_sb[:, s, T:TC] if u < 8 else vT[u % 2][:, T:TC], ps[:, 2 + u % 2, 0:CTX])\
                   .then_inc(S["qkv_ctx_read"], 1)
                if u > 8:
                    v_read(u - 9)
            v_read(7)

        def dve_gla(dve):
            def chunks(ap):
                return ap.rearrange("p (n c) -> p n c", c=CH)

            def each(ap, off, n):
                return wide(ap[:, off:n * CH:CH], CH)

            dve.wait_ge(S["const_ready"], 1)
            dve.wait_ge(S["zeros"], 2)
            def head(h):
                for d in range(2):
                    w = 2 * h + d
                    q = w + Q_GLA
                    dve.wait_ge(S["z_mm"], w + 1)
                    dve.wait_ge(S["b_dec_copied"], w + 1)
                    dve.wait_ge(S["z_log"], 3 * w + 1)
                    wait_former(dve, S["decay_exp"], 5 * w)
                    wait_former(dve, S["oT_mm"], h)
                    dve.tensor_scalar(t1[:, :], z_ps[:, 0:TC], b_dec_h[:, :], 0.0, ALU.add, ALU.min).then_inc(S["decay_sum"], 1)
                    dve.wait_ge(S["decay_sum"], 5 * w + 1)
                    dve.wait_ge(S["z_log"], 3 * w + 3)
                    dve.tensor_tensor(t1[:, :], t1[:, :], t0[:, :], ALU.subtract).then_inc(S["decay_sum"], 1)
                    dve.wait_ge(S["decay_sum"], 5 * w + 2)
                    wait_former(dve, S["decay_exp"], 5 * w)
                    wait_former(dve, S["o_ss"], 5 * h)
                    if d == 0:
                        dve.tensor_tensor_scan(t2[:, :], keep[:, 0:TC], t1[:, :], 0.0, ALU.mult, ALU.add)\
                           .then_inc(S["decay_sum"], 1)
                    else:
                        dve.tensor_tensor_scan(t2[:, ::-1], keep[:, TC:0:-1], t1[:, ::-1], 0.0, ALU.mult, ALU.add)\
                           .then_inc(S["decay_sum"], 1)
                    dve.wait_ge(S["decay_sum"], 5 * w + 3)
                    dve.tensor_tensor(chunks(t1[:, :]), each(t2, W_LAST[d], NCHC), chunks(t2[:, :]), ALU.subtract)\
                       .then_inc(S["decay_sum"], 1)
                    wait_former(dve, S["decay_exp"], 5 * w)
                    dve.tensor_tensor(chunks(t0[:, 0:T]), chunks(t2[:, 0:T]), each(t2, W_MID[d], NCH), ALU.subtract)\
                       .then_inc(S["decay_sum"], 1)
                    for i, (t, n, src) in enumerate(((k_dec, TC, k_sb), (q_mid, T, q_sb), (k_mid, T, k_sb),
                                                     (q_dec, T, q_sb))):
                        dve.wait_ge(S["decay_exp"], 5 * w + i + 1)
                        dve.tensor_tensor(t[:, :], t[:, :], at_index(src, h)[:, 0:n], ALU.mult).then_inc(S["decayed"], 1)
                    dve.wait_ge(S["cc_read"], w + 1)
                    dve.wait_ge(unit_done[1], q + 1)
                    dve.tensor_tensor(cc_sb[:, :], cc_sb[:, :], ps[:, 1, :], ALU.mult).then_inc(S["conv3"], 1)
                    dve.wait_ge(S["conv3"], 5 * w + 1)
                    y = at_index(y_sb, w)
                    yr, ur = chunks(y), chunks(cc_sb[:, :])
                    dve.tensor_scalar(y, cc_sb[:, :], v_dyn("w_conv", w + 8), None, ALU.mult).then_inc(S["conv3"], 1)
                    dve.wait_ge(S["conv3"], 5 * w + 2)
                    dve.scalar_tensor_tensor(out=yr[:, :, 1:CH], in0=ur[:, :, 0:CH - 1], scalar=v_dyn("w_conv", w),
                                             in1=yr[:, :, 1:CH], op0=ALU.mult, op1=ALU.add).then_inc(S["conv3"], 1)
                    dve.wait_ge(S["conv3"], 5 * w + 3)
                    dve.scalar_tensor_tensor(out=yr[:, :, 0:CH - 1], in0=ur[:, :, 1:CH], scalar=v_dyn("w_conv", w + 16),
                                             in1=yr[:, :, 0:CH - 1], op0=ALU.mult, op1=ALU.add).then_inc(S["conv3"], 1)
                    dve.wait_ge(S["conv3"], 5 * w + 4)
                    dve.wait_ge(unit_done[2], q + 1)
                    dve.tensor_tensor(y, y, ps[:, 2, :], ALU.mult).then_inc(S["conv3"], 1)
                    wait_apart(dve, S["kd_scores_mm"], 3 * w + 3)
                    mask = causal[d][:, :].bitcast(U32).unsqueeze(1).broadcast_to([P, TT, P])
                    dve.copy_predicated(s_dir[d][:, :, :], mask, ps[:, 1, :].rearrange("p (c t) -> p c t", t=P))\
                       .then_inc(S["scores_read"], 1)
                    order = [8, 9, 10, 11, *range(8)] if d == 0 else [11, 10, 9, 8, *range(7, -1, -1)]
                    dve.wait_ge(S["decay_exp"], 5 * w + 5)
                    for m in range(1, 12):
                        n = m - 1
                        kv = ps[:, (2, 3, 6, 7)[n % 4], 0:HEAD_V]
                        dve.wait_ge(S["kv_mm"], 11 * w + min(11, 2 * (n // 2) + 2))
                        if m == 1:
                            wait_former(dve, S["inter_mm"], 8 * w)
                            dve.tensor_copy(state[1][:, :], kv).then_inc(S["state_step"], 1)
                            continue
                        if m >= 7:
                            dve.wait_ge(S["inter_mm"], 8 * w + m - 6)
                        dve.wait_ge(S["state_step"], 11 * w + m - 1)
                        g = order[n]
                        dve.scalar_tensor_tensor(out=state[m % 3][:, :], in0=state[(m - 1) % 3][:, :],
                                                 scalar=dec[:, g:g + 1], in1=kv, op0=ALU.mult, op1=ALU.add)\
                           .then_inc(S["state_step"], 1)
                dve.wait_ge(S["o_ss"], 5 * h + 5)
                dve.reciprocal(o_rstd[:, :], o_rs[:, :]).then_inc(S["o_recip"], 1)
                dve.wait_ge(S["o_recip"], h + 1)
                for b in range(2):
                    dve.tensor_tensor(o_tok[:, 2 * b:2 * b + 2, :], ps[:, 4 + b, :].rearrange("p (c v) -> p c v", v=HEAD_V),
                                      wide(o_rstd[:, 2 * b:2 * b + 2], HEAD_V), ALU.mult).then_inc(S["o_tok_ready"], 1)
                dve.wait_ge(S["oT_mm"], h + 1)
                dve.tensor_copy(at_index(v_sb, h)[:, T:2 * T], ps[:, 7, :]).then_inc(S["oT_read_d"], 1)

            head(0)
            with dve.Fori(1, HEADS) as h:
                head(h)

        def dve_gated(dve):
            dve.wait_ge(S["oT_read_a"], HEADS)
            for j in range(KC + 1):
                if j < KC:
                    h, half = j // 2, j % 2
                    dve.wait_ge(S["og_sg"], j + 1)
                    if j >= 2:
                        dve.wait_ge(S["og_hi"], j - 1)
                        dve.wait_ge(S["og_lo"], j - 1)
                    if j == 0:
                        dve.wait_ge(S["oT_read_d"], HEADS)
                    dve.scalar_tensor_tensor(out=og_val[j % 2][:, :], in0=v_sb[:, h, half * T:(half + 1) * T],
                                             scalar=v_at("g_head", half), in1=og_sg[j % 2][:, :],
                                             op0=ALU.mult, op1=ALU.mult).then_inc(S["og_val"], 1)
                if j >= 1:
                    dve.wait_ge(S["og_hi"], j)
                    dve.tensor_tensor(og_lo[:, j - 1, :], og_val[(j - 1) % 2][:, :], og_hi[:, j - 1, :].bitcast(F32),
                                      ALU.subtract).then_inc(S["og_lo"], 1)
            for k in range(KC):
                dve.wait_ge(S["y_hi"], k + 1)
                dve.tensor_tensor(y_lo[:, k, :], y_sb[:, k, :], y_hi[:, k, :].bitcast(F32), ALU.subtract)\
                   .then_inc(S["y_lo"], 1)

        def dve_merge(dve):
            dve.wait_ge(S["cond_ready"], 3)
            def merge(r):
                q = r + Q_MERGE
                dve.wait_ge(S["sig_a"], r + 1)
                dve.wait_ge(unit_done[0], q + 1)
                dve.tensor_tensor(mrg_a[:, :], sig_a[:, :], ps[:, 0, :], ALU.mult).then_inc(S["merge_a"], 1)
                dve.wait_ge(S["sig_b"], r + 1)
                dve.tensor_tensor(mrg_b[:, :], sig_b[:, :], ps[:, 2, :], ALU.mult).then_inc(S["merge_b"], 1)
                dve.wait_ge(S["merge_a"], r + 1)
                dve.wait_ge(S["merge_b"], r + 1)
                wait_former(dve, S["mg_hi"], r)
                wait_former(dve, S["mg_lo"], r)
                dve.tensor_tensor(mrg_v[:, :], mrg_a[:, :], mrg_b[:, :], ALU.add).then_inc(S["merged"], 1)
                for i in range(4):
                    dve.wait_ge(S[f"ada_full{i % 2}"], 32 * r + (64 + 16 * (i // 2 + 1)))
                    if i == 0:
                        wait_former(dve, S["mod2_ready"], r)
                    dve.tensor_tensor_reduce(ada_w[i % 2][:, :], ada_w[i % 2][:, :], cond2, 1.0, 0.0, ALU.mult, ALU.add,
                                             accum_out=mod_sum[:, i:i + 1]).then_inc(S["ada2_used"], 1)
                dve.wait_ge(S["ada2_used"], 4 * r + 4)
                dve.tensor_tensor(mod2[:, span(4 * r, 4)], mod_sum[:, :], v_dyn("b_ada", 4 * r + 16, 4), ALU.add)\
                   .then_inc(S["mod2_ready"], 1)
                dve.wait_ge(S["mg_hi"], r + 1)
                dve.tensor_tensor(at_index(mg_lo, r), mrg_v[:, :], at_index(mg_hi, r).bitcast(F32), ALU.subtract)\
                   .then_inc(S["mg_lo"], 1)

            merge(0)
            with dve.Fori(1, KC) as r:
                merge(r)

        def dve_low(dve, n, h_base, gain):
            dve.wait_ge(S["h_hi"], h_base + n + 1)
            dve.scalar_tensor_tensor(out=h_lo[:, n, :], in0=x[:, n, :], scalar=gain, in1=h_hi[:, n, :].bitcast(F32),
                                     op0=ALU.mult, op1=ALU.subtract).then_inc(S["h_lo"], 1)

        def dve_resid(dve, i, q0, resid_base, per_round, bank, gate=None, source=None, h_base=None, gain=None,
                      twice=False):
            source = x if source is None else source
            for n in range(KC + 1):
                if n < KC:
                    r, s = (n, 3) if per_round == 1 else (n // 4, n % 4)
                    dve.wait_ge(unit_done[s], q0 + r + 1)
                    if gate is None:
                        ins = dve.tensor_tensor(x[:, n, :], ps[:, bank(n), :], source[:, n, :], ALU.add)
                    else:
                        ins = dve.scalar_tensor_tensor(out=x[:, n, :], in0=ps[:, bank(n), :], scalar=gate[:, n:n + 1],
                                                       in1=source[:, n, :], op0=ALU.mult, op1=ALU.add)
                    ins.then_inc(S["resid_x"], 1)
                    if gain and n < KC - 1:
                        dve_low(dve, n, h_base, gain(n))
                if n >= 2:
                    if n == KC and gain:
                        dve_low(dve, KC - 1, h_base, gain(KC - 1))
                    (dve_sums if twice else dve_sum)(dve, i, n - 1)

        def dve_sums(dve, i, k):
            for j, total in enumerate((acc, acc2)):
                dve.wait_ge(S["norm_sq"], 8 * i + 2 * k + j + 1)
                if k > 1:
                    dve.wait_ge(S["norm_acc"], 7 * (i - 1) + 2 * (k - 2) + j + 1)
                dve.tensor_tensor(total[:, :], total[:, :], sq[j][:, :], ALU.add).then_inc(S["norm_acc"], 1)

        def dve_sum(dve, i, k):
            dve.wait_ge(S["norm_sq"], 8 * i + k + 1)
            if k > 1:
                dve.wait_ge(S["norm_acc"], 7 * (i - 1) + k - 1)
            dve.tensor_tensor(acc[:, :], sq[0][:, :] if k == 1 else acc[:, :], sq[k % 2][:, :], ALU.add)\
               .then_inc(S["norm_acc"], 1)

        def dve_rstd(dve, i):
            dve.wait_ge(S["norm_rms"], i + 1)
            dve.reciprocal(rstd[:, :], rstd[:, :]).then_inc(S["norm_recip"], 1)
            dve.wait_ge(S["norm_recip"], i + 1)

        def dve_split(dve, h_base, gain, shift=None):
            for k in range(KC + 1):
                if k < KC:
                    if k >= 2:
                        dve.wait_ge(S["h_hi"], h_base + k - 1)
                        dve.wait_ge(S["h_lo"], h_base + k - 1)
                    dve.scalar_tensor_tensor(out=nv[k % 2][:, :], in0=x[:, k, :], scalar=gain(k), in1=rstd[:, :],
                                             op0=ALU.mult, op1=ALU.mult).then_inc(S["h_val"], 1)
                if k >= 1:
                    j = k - 1
                    dve.wait_ge(S["h_hi"], h_base + j + 1)
                    if shift is None:
                        ins = dve.tensor_tensor(h_lo[:, j, :], nv[j % 2][:, :], h_hi[:, j, :].bitcast(F32), ALU.subtract)
                    else:
                        ins = dve.scalar_tensor_tensor(out=h_lo[:, j, :], in0=nv[j % 2][:, :], scalar=shift[:, j:j + 1],
                                                       in1=h_hi[:, j, :].bitcast(F32), op0=ALU.add, op1=ALU.subtract)
                    ins.then_inc(S["h_lo"], 1)

        def dve_ffn(dve, e, i, resid_base, gate=None, **norm):
            def hidden(r):
                q = r + Q_FFI[e]
                for p in range(2):
                    n = r + 11 * e
                    if e == 0:
                        dve.wait_ge(S[f"ffn_sa{p}"], n + 1)
                        dve.wait_ge(unit_done[2 * p + 1], q + 1)
                        wait_former(dve, S[f"ffn_hi{p}"], n)
                        wait_former(dve, S[f"ffn_lo{p}"], n)
                        dve.tensor_tensor(fval[p][:, :], sa[p][:, :], ps[:, 2 * p + 1, :], ALU.mult)\
                           .then_inc(S[f"ffn_val{p}"], 1)
                    else:
                        dve.wait_ge(unit_done[2 * p], q + 1)
                        dve.wait_ge(S[f"ffn_val{p}"], n)
                        dve.tensor_tensor(sa[p][:, :], ps[:, 2 * p, :], rstd[:, :], ALU.mult).then_inc(S[f"ffn_scaled{p}"], 1)
                        dve.wait_ge(unit_done[2 * p + 1], q + 1)
                        dve.wait_ge(S[f"ffn_hi{p}"], n)
                        dve.wait_ge(S[f"ffn_lo{p}"], n)
                        dve.tensor_tensor(fval[p][:, :], ps[:, 2 * p + 1, :], rstd[:, :], ALU.mult)\
                           .then_inc(S[f"ffn_scaled{p}"], 1)
                        dve.wait_ge(S[f"ffn_sa{p}"], n + 1)
                        dve.wait_ge(S[f"ffn_scaled{p}"], 2 * r + 22 * (e - 1) + 2)
                        dve.tensor_tensor(fval[p][:, :], sa[p][:, :], fval[p][:, :], ALU.mult).then_inc(S[f"ffn_val{p}"], 1)
                    dve.wait_ge(S[f"ffn_hi{p}"], n + 1)
                    dve.tensor_tensor(at_index(gu_lo, 2 * r + p), fval[p][:, :], at_index(gu_hi, 2 * r + p).bitcast(F32),
                                      ALU.subtract).then_inc(S[f"ffn_lo{p}"], 1)

            hidden(0)
            with dve.Fori(1, FC // 2) as r:
                hidden(r)
            dve_resid(dve, i, Q_FFO[e], resid_base, 1, lambda n: 4 + n % 2, gate, **norm)

        def dve_cp(dve):
            dve.memset(a_sb[:, :, 0:APAD], 0.0).then_inc(S["zeros"], 1)
            dve.memset(u_sb[:, :, 0:UPAD], 0.0).then_inc(S["zeros"], 1)
            for i in range(2):
                dve.memset(win[i][:, 0:UPAD], 0.0).then_inc(S["zeros"], 1)
            dve.wait_ge(S["zeros"], 6)
            dve_rstd(dve, 2)
            dve.wait_ge(S["norm_stat"], 3)
            dve.tensor_tensor(rstd_xg[:, :], ps[:, 7, :], rstd[:, :], ALU.mult).then_inc(S["dve_step"], 1)
            dve.wait_ge(S["dve_step"], 10)
            dve.tensor_tensor(rstd_xg[:, :], rstd_xg[:, :], rstd[:, :], ALU.mult).then_inc(S["dve_step"], 1)
            dve.wait_ge(S["norm_rms"], 4)
            dve.reciprocal(rstd_xg[:, :], rstd_xg[:, :]).then_inc(S["norm_recip"], 1)
            dve.wait_ge(S["norm_recip"], 4)
            dve.tensor_tensor(rstd_xg[:, :], rstd_xg[:, :], rstd[:, :], ALU.mult).then_inc(S["dve_step"], 1)
            steps = 12
            dve.wait_ge(S["dve_step"], steps)

            def value(j):
                p = j % 2
                dve.wait_ge(unit_done[2 * p + 1], j // 2 + Q_CPI + 1)
                if j >= 2:
                    dve.wait_ge(S[f"conv_in{p}"], 1)
                dve.tensor_tensor(csg[p][:, :], ps[:, 2 * p + 1, :], rstd_xg[:, :], ALU.mult).then_inc(S["cp_scaled"], 1)
                dve.wait_ge(unit_done[2 * p], j // 2 + Q_CPI + 1)
                dve.tensor_tensor(a_sb[:, j, APAD:], ps[:, 2 * p, :], rstd_xg[:, :], ALU.mult).then_inc(S["cp_scaled"], 1)
                dve.wait_ge(S[f"conv_sg{p}"], j // 2 + 1)
                dve.wait_ge(S["cp_scaled"], 2 * j + 2)
                dve.tensor_tensor(a_sb[:, j, APAD:], csg[p][:, :], a_sb[:, j, APAD:], ALU.mult).then_inc(S[f"conv_in{p}"], 1)

            def convolve(*js):
                nonlocal taps
                for i in range(CONVW):
                    for j in js:
                        src, w = a_sb[:, j, i:i + T], v_at("dw_w", j * CONVW + i)
                        if i == 0:
                            dve.wait_ge(S[f"conv_in{j % 2}"], j // 2 + 1)
                            ins = dve.tensor_scalar(cv[:, j, :], src, w, v_at("dw_b", j), ALU.mult, ALU.add)
                        else:
                            dve.wait_ge(S["conv_dve"], taps - len(js) + 1)
                            ins = dve.scalar_tensor_tensor(out=cv[:, j, :], in0=src, scalar=w, in1=cv[:, j, :],
                                                           op0=ALU.mult, op1=ALU.add)
                        ins.then_inc(S["conv_dve"], 1)
                        taps += 1

            taps = 0
            value(0)
            value(1)
            for g in range(CPC):
                dve.wait_ge(S["dve_step"], steps)
                dve.tensor_scalar(cnt_f[:, :], cnt_i[:, :], float(2 << g), None, ALU.min).then_inc(S["dve_step"], 1)
                dve.wait_ge(S["dve_step"], steps + 1)
                dve.reciprocal(inv_cnt[:, g, :], cnt_f[:, :]).then_inc(S["dve_step"], 1)
                steps += 2
            for k in range(KC):
                dve.scalar_tensor_tensor(out=x[:, k, :], in0=x[:, k, :], scalar=v_at("g_final", k), in1=rstd[:, :],
                                         op0=ALU.mult, op1=ALU.mult)
            convolve(0)
            value(2)
            value(3)
            convolve(1, 2)
            for g in range(CPC):
                dve.wait_ge(S["cat_hi_p"], g + 1)
                dve.scalar_tensor_tensor(out=cat_lo[:, CPC + g, :], in0=ps[:, g, :], scalar=v_at("pool_scale", g),
                                         in1=cat_hi[:, CPC + g, :].bitcast(F32), op0=ALU.mult, op1=ALU.subtract)\
                   .then_inc(S["cat_lo_p"], 1)
            dve.wait_ge(S["ln_sum"], 1)
            for g in range(CPC):
                dve.scalar_tensor_tensor(out=cv[:, g, :], in0=ps[:, 5, :], scalar=-1.0 / (CPC * P), in1=cv[:, g, :],
                                         op0=ALU.mult, op1=ALU.add).then_inc(S["ln_centred"], 1)
            dve_rstd(dve, 4)
            for g in range(CPC):
                if g >= 2:
                    dve.wait_ge(S["ln_silu"], g - 1)
                dve.scalar_tensor_tensor(out=lnv[g % 2][:, :], in0=cv[:, g, :], scalar=v_at("ln_g", g), in1=rstd[:, :],
                                         op0=ALU.mult, op1=ALU.mult).then_inc(S["ln_val"], 1)
                dve.wait_ge(S["cat_hi_a"], g + 1)
                dve.tensor_tensor(cat_lo[:, g, :], lns[g % 2][:, :], cat_hi[:, g, :].bitcast(F32), ALU.subtract)\
                   .then_inc(S["cat_lo_a"], 1)

        def dve_hg(dve):
            def decays(g, par):
                k, qq, b = hk[par], hq[par], hb[par]
                dve.wait_ge(S["hlog_ready"], g + 1)
                dve.tensor_tensor_scan(b[:, :], keep[:, 0:T], hlf[:, :], 0.0, ALU.mult, ALU.add).then_inc(S["hb_ready"], 1)
                dve.wait_ge(S["hb_ready"], g + 1)

                def difference(n):
                    wait_former(dve, S["hd_used"], 13 * g + max(2 * n - 3, 0))
                    if n == 0:
                        bc = b[:, :].rearrange("p (n c) -> p n c", c=CH)
                        dve.tensor_tensor(hd[0][:, :].rearrange("p (n c) -> p n c", c=CH), wide(b[:, CH - 1:T:CH], CH), bc,
                                          ALU.subtract).then_inc(S["hd_ready"], 1)
                    else:
                        m = LEVELS[n - 1]
                        bc = b[:, :].rearrange("p (n c) -> p n c", c=2 * m)
                        dve.tensor_tensor(hd[n % 2][:, :].rearrange("p (n c) -> p n c", c=2 * m), bc,
                                          wide(b[:, m - 1:T:2 * m], 2 * m), ALU.subtract).then_inc(S["hd_ready"], 1)

                difference(0)
                difference(1)
                dve.wait_ge(S["hd_used"], 13 * g + 1)
                dve.tensor_tensor(hkd[:, :], hkd[:, :], k[:, :], ALU.mult).then_inc(S["hkd_ready"], 1)
                dve.wait_ge(S["hqb_exp"], g + 1)
                dve.tensor_tensor(hqb[:, :], hqb[:, :], qq[:, :], ALU.mult).then_inc(S["hqb_ready"], 1)
                wait_former(dve, S["hg_scores_mm"], 7 * g)
                for i, m in enumerate(LEVELS):
                    if i < 5:
                        difference(i + 2)
                    for half, src in ((0, k), (1, qq)):
                        def part(t):
                            return t[:, :].rearrange("p (b a m) -> p b a m", a=2, m=m)[:, :, half, :]
                        dve.wait_ge(S["hd_used"], 13 * g + 2 * i + 2 + half)
                        dve.tensor_tensor(part(hx[i]), part(he[i % 2]), part(src), ALU.mult).then_inc(S["hx_ready"], 1)

            def forget(w, par):
                dve.wait_ge(S["hg_f_read"], w + 1)
                dve.tensor_scalar(hlf[:, :], hsf[:, :], om_lb[:, dyn(w)], lb[:, dyn(w)], ALU.mult, ALU.add)\
                   .then_inc(S["hf_step"], 1)
                dve.wait_ge(S["hf_step"], 2 * w + 1)
                dve.tensor_scalar(hk[par][:, :], hlf[:, :], -1.0, 1.0, ALU.mult, ALU.add).then_inc(S["hf_step"], 1)
                dve.tensor_scalar(hlf[:, :], hlf[:, :], 1e-19, None, ALU.max).then_inc(S["hf_ready"], 1)

            def gate(w, par):
                dve.wait_ge(S["hg_sig"], w + 1)
                dve.tensor_tensor(hg[par][:, :], hg[par][:, :], ps[:, 3, :], ALU.mult).then_inc(S["hg_g_read"], 1)

            def finish(g, par):
                dve.wait_ge(S["hoT_mm"], g + 1)
                dve.wait_ge(S["hg_g_read"], g + 1)
                dve.scalar_tensor_tensor(out=hval[:, :], in0=ps[:, 4, :], scalar=v_dyn_or("gn_g", g),
                                         in1=hg[par][:, :], op0=ALU.mult, op1=ALU.mult).then_inc(S["hval_ready"], 1)

            def low(g):
                dve.wait_ge(S["r_hi"], g + 1)
                dve.tensor_tensor(at_index(r_lo, g), hval[:, :], at_index(r_hi, g).bitcast(F32), ALU.subtract)\
                   .then_inc(S["r_lo"], 1)

            def mix(g, par):
                wait_former(dve, S["r_lo"], g)
                dve.wait_ge(S["hv_mm"], g + 1)
                wait_former(dve, S["ho_mm"], g)
                dve.tensor_copy(hv_tok[:, :, :].rearrange("p c k -> p (c k)"), ps[:, 5, :]).then_inc(S["hv_tok_ready"], 1)
                for l in range(7):
                    dve.wait_ge(S["hg_scores_mm"], 7 * g + l + 1)
                    wait_former(dve, S["hg_scores_read"], 7 * g + l)
                    dve.memset(spare[:, l:l + 1], 0.0)
                    mask = ident[:, :] if l == 0 else level_mask[:, l - 1, :]
                    dve.copy_predicated(hs[:, :, :], mask.bitcast(U32).unsqueeze(1).broadcast_to([P, TT, P]),
                                        ps[:, l % 4, :].rearrange("p (c t) -> p c t", t=P)).then_inc(S["hg_scores_read"], 1)
                dve.wait_ge(S["hdec_ready"], g + 1)
                dve.wait_ge(S["hkv_mm"], 7 * g + 7)
                for n in range(7):
                    kv = ps[:, 6 + n % 2, (n // 2) * P:(n // 2 + 1) * P]
                    if n == 0:
                        dve.tensor_copy(hst[:, 1, :], kv).then_inc(S["hg_state"], 1)
                    else:
                        dve.wait_ge(S["hg_state"], 7 * g + n)
                        dve.scalar_tensor_tensor(out=hst[:, n + 1, :], in0=hst[:, n, :], scalar=hdec[:, n:n + 1], in1=kv,
                                                 op0=ALU.mult, op1=ALU.add).then_inc(S["hg_state"], 1)
                dve.wait_ge(S["ho_ss"], 5 * g + 5)
                dve.reciprocal(o_rstd[:, :], o_rs[:, :]).then_inc(S["ho_recip"], 1)
                dve.wait_ge(S["ho_recip"], g + 1)
                wait_former(dve, S["hoT_mm"], g)
                dve.tensor_tensor(ho_tok[:, :, :], ps[:, 5, :].rearrange("p (c v) -> p c v", v=P), wide(o_rstd[:, :], P),
                                  ALU.mult).then_inc(S["ho_tok_ready"], 1)

            def dyn(w):
                return slice(w, w + 1) if isinstance(w, int) else bass.ds(w, 1)

            def v_dyn_or(name, g):
                return v_at(name, g) if isinstance(g, int) else v_dyn(name, g)

            dve.memset(hs[:, :, :], 0.0).then_inc(S["zeros"], 1)
            dve.wait_ge(S["zeros"], 7)
            dve.wait_ge(S["level_step"], 1 + 3 * len(LEVELS))
            forget(0, 0)
            gate(0, 0)
            decays(0, 0)
            forget(1, 1)
            gate(1, 1)
            mix(0, 0)
            with dve.Fori(0, 3) as m:
                for p in range(2):
                    decays(2 * m + (1 + p), 1 - p)
                    finish(2 * m + p, p)
                    forget(2 * m + (2 + p), p)
                    low(2 * m + p)
                    gate(2 * m + (2 + p), p)
                    mix(2 * m + (1 + p), 1 - p)
            decays(7, 1)
            finish(6, 0)
            low(6)
            mix(7, 1)
            finish(7, 1)
            low(7)

        @block.vector
        def _(dve):
            dve_start(dve)
            dve_qkv(dve)
            dve_gla(dve)
            dve_gated(dve)
            dve_merge(dve)
            dve.wait_ge(S["mod2_ready"], KC)
            dve.scalar_tensor_tensor(out=amp2[:, :], in0=mod2[:, 16:24], scalar=1.0, in1=v_at("g_ffn", 0, 8),
                                     op0=ALU.add, op1=ALU.mult).then_inc(S["dve_step"], 1)
            dve.wait_ge(S["small_in"], 48)
            dve_resid(dve, 1, Q_MIX, 0, 4, lambda n: n % 4, mod2[:, 0:8], x_res)
            dve_rstd(dve, 1)
            dve.wait_ge(S["dve_step"], 9)
            dve_split(dve, 8, lambda k: amp2[:, k:k + 1], mod2[:, 8:16])
            dve_ffn(dve, 0, 2, 8, mod2[:, 24:32], h_base=16, gain=lambda k: gain_xg[:, k:k + 1], twice=True)
            dve_cp(dve)
            dve_resid(dve, 4, Q_CPO, 16, 4, lambda n: n % 4, h_base=24, gain=lambda k: v_at("norm_ffn", k))
            dve_rstd(dve, 5)
            dve_ffn(dve, 1, 5, 24)
            dve_rstd(dve, 6)
            dve_split(dve, 32, lambda k: v_at("norm_mix", 8 + k))
            dve_hg(dve)
            dve_resid(dve, 6, Q_HGO, 32, 4, lambda n: n % 4, h_base=40, gain=lambda k: v_at("norm_ffn", 8 + k))
            dve_rstd(dve, 7)
            dve_ffn(dve, 2, 7, 40)
            dve_rstd(dve, 8)
            for k in range(KC):
                dve.scalar_tensor_tensor(out=x[:, k, :], in0=x[:, k, :], scalar=v_at("final_g", k), in1=rstd[:, :],
                                         op0=ALU.mult, op1=ALU.mult).then_inc(S["out_ready"], 1)


def columns(a):
    return np.asarray(a).reshape(-1, P).T


def units(w):
    k, n = w.shape
    return np.ascontiguousarray(w.reshape(k // P, P, n // P, P).transpose(2, 1, 0, 3)).reshape(n // P, P, k)


def tokens_last(a):
    return np.ascontiguousarray(a.T.reshape(KC, P, -1).transpose(1, 0, 2))


def layouts(v):
    cols = {"b_ada": v["b_ada"][0], "g_mix": v["g_mix"][0], "b_dec": v["b_dec"][0],
            "g_head": v["g_head"][0], "w_conv": v["w_conv"][0], "g_ffn": v["g_ffn"][0], "g_final": v["g_final"],
            "norm_mix": v["norm_mix_g_2"], "norm_ffn": v["norm_ffn_g_2"], "final_g": v["final_g_2"],
            "dw_w": v["cp_dw_w_2"][0].reshape(CONVW, CPC, P).transpose(1, 0, 2), "dw_b": v["cp_dw_b_2"][0],
            "ln_g": v["cp_ln_g_2"][0], "ln_b": v["cp_ln_b_2"][0], "pool_scale": v["cp_pool_scale_2"][0],
            "lb_logits": v["hg_lb_logits_2"], "gn_g": v["hg_gn_g_2"][0]}
    out = {"vectors": np.concatenate([columns(cols[n]) for n, _ in VEC_SIZES], axis=1)}
    out["x"], out["ctx"] = tokens_last(v["x"][0]), tokens_last(v["ctx"][0])
    w_in = v["w_in"][0]
    q, k, vv, g, dd = 0, 512, 1024, 2048, 3072
    cb, cc, ch, ga, gb = (3104 + D * i for i in range(5))
    out["w_decay"] = units(w_in[:, dd:dd + P])[0]
    out["w_dec_up"] = v["w_dec_up"][0].reshape(2, 16, HEADS, P)
    out["w_ada"] = np.ascontiguousarray(v["w_ada"][0].T).reshape(48, P, D)
    out["conditions"] = np.stack([v["c"][0], v["c_ctx"]])
    out["w_qkv"] = units(w_in[:, q:g]).reshape(4, 4, P, D)

    def rounds(*parts):
        return np.ascontiguousarray(np.stack([units(p) for p in parts], axis=1))

    def wi(c):
        return w_in[:, c:c + D]

    out["w_conv_gate"] = rounds(wi(cc), wi(ch), wi(cb), wi(g))
    out["w_merge"] = rounds(v["w_gla_out"][0], wi(ga), v["w_conv_out"][0], wi(gb))
    out["w_mix"] = units(v["w_mix_out"][0]).reshape(2, 4, P, D)
    ins = [(v["w_ffn_in"][0][:, :DFF], v["w_ffn_in"][0][:, DFF:])] + [(v["ffn_w1_2"][i], v["ffn_w3_2"][i]) for i in range(2)]
    outs = [v["w_ffn_out"][0], v["ffn_w2_2"][0], v["ffn_w2_2"][1]]
    for e in range(3):
        out[f"w_ffn_in{e}"] = rounds(*ins[e]).reshape(FC // 2, 4, P, D)
        out[f"w_ffn_out{e}"] = units(outs[e])
    cp = v["cp_w_in_2"][0]
    out["w_cp"] = np.concatenate([rounds(cp[:, :512], cp[:, 512:1024]).reshape(2, 4, P, D),
                                  units(cp[:, 1024:]).reshape(1, 4, P, D),
                                  units(v["cp_w_out_2"][0]).reshape(2, 4, P, D)])
    out["pool_w"] = np.ascontiguousarray(v["cp_pool_w_2"][0].transpose(1, 0, 2))
    hg = v["hg_w_in_2"][0]
    out["w_hg"] = np.concatenate([rounds(hg[:, D:2 * D], hg[:, :D], hg[:, 2 * D:3 * D], hg[:, 3 * D:]),
                                  units(v["hg_w_out_2"][0]).reshape(2, 4, P, D)])
    return {n: np.ascontiguousarray(a) for n, a in out.items()}


def kernel(**inputs):
    import concourse.bacc as bacc
    from concourse.bass_utils import run_bass_kernel_spmd

    arrays = layouts({n: np.asarray(a) for n, a in inputs.items()})
    nc = bacc.Bacc("TRN2", target_bir_lowering=False, num_devices=1)
    dram = {n: nc.dram_tensor(f"in_{n}", a.shape, F32, kind="ExternalInput").ap() for n, a in arrays.items()}
    dram["out"] = nc.dram_tensor("out_x", (P, KC, T), F32, kind="ExternalOutput").ap()
    for name in ("w_ffn_in", "w_ffn_out"):
        dram[name] = [dram[f"{name}{e}"] for e in range(3)]
    build(nc, dram)
    got = run_bass_kernel_spmd(nc, [{f"in_{n}": a for n, a in arrays.items()}], core_ids=[0]).results[0]["out_x"]
    return np.ascontiguousarray(got.transpose(1, 0, 2).reshape(D, T).T).reshape(1, T, D)
```

```python
from contextlib import ExitStack

import numpy as np

import concourse.bass as bass
import concourse.mybir as mybir
from concourse.alu_op_type import AluOpType as ALU

ACT = mybir.ActivationFunctionType
F32 = mybir.dt.float32
F32R = mybir.dt.float32r
U32 = mybir.dt.uint32
I32 = mybir.dt.int32

P = 128
D = 1024
KC = D // P
T = 512
CTX = 256
TC = T + CTX
TT, TTC = T // P, TC // P
CH = 64
NCH, NCHC = T // CH, TC // CH
HEADS, HEAD_V = 4, 256
DFF = 2816
FC = DFF // P
HG = 8
CONVW = 31
CPC = 4
EPS = 1e-6
ROOT = 1.0 / D ** 0.5
DECAY_TAU = 16.0
W_MID = {0: CH // 2 - 1, 1: CH // 2}
W_LAST = {0: CH - 1, 1: 0}
LEVELS = [32, 16, 8, 4, 2, 1]
FFO = [6, 6, 5, 5]
FFO_AT = [0, 6, 12, 17]

VEC_SIZES = [("b_ada", 48), ("g_mix", 8), ("b_dec", 8), ("g_head", 2),
             ("w_conv", 24), ("g_ffn", 8), ("g_final", 8), ("norm_mix", 16), ("norm_ffn", 16),
             ("final_g", 8), ("dw_w", 4 * CONVW), ("dw_b", 4), ("ln_g", 4), ("ln_b", 4),
             ("pool_scale", 4), ("lb_logits", 16), ("gn_g", 8)]
VEC = {}
NVEC = 0
for _name, _n in VEC_SIZES:
    VEC[_name] = NVEC
    NVEC += _n

Q_QK, Q_V, Q_GLA, Q_MERGE, Q_MIX = 0, 2, 4, 12, 20
Q_FFI = [22, 46, 75]
Q_FFO = [33, 57, 86]
Q_CPI, Q_CPO, Q_HG, Q_HGO = 41, 44, 65, 73
Q_END = 94

KB = 1024
SBUF_AT = 16512


def at_index(t, i):
    if isinstance(i, int):
        return t[:, i]
    return t[:, bass.ds(i, 1)].squeeze(1)


def span(i, n):
    return slice(i, i + n) if isinstance(i, int) else bass.ds(i, n)


def wide(ap, n):
    u = ap.unsqueeze(len(ap.shape))
    return u.broadcast_to(list(ap.shape) + [n])


def build(nc, dram):
    ctx = ExitStack()
    with ctx:
        def at(name, shape, dt, kb):
            return nc.alloc_sbuf_tensor_at(name, shape, dt, offset=SBUF_AT + int(kb * KB))

        raw = [at(f"w_raw{s}", [P, D], F32, 4 * s) for s in range(4)]
        w_hi = [at(f"w_hi{s}", [P, D], F32R, 16 + 4 * s) for s in range(4)]
        w_lo = [at(f"w_lo{s}", [P, D], F32R, 32 + 4 * s) for s in range(4)]

        vec = at("vec", [P, NVEC], F32, 48)
        ident = at("ident", [P, P], F32, 49.5)
        ones = at("ones", [P, P], F32, 50)
        causal = [at("causal_f", [P, P], F32, 50.5), at("causal_b", [P, P], F32, 51)]
        keep = at("keep", [P, TC + 1], F32, 51.5)
        w_up = at("w_up", [32, 2, HEADS, P], F32, 55872 / KB)
        level_mask = at("level_mask", [P, len(LEVELS), P], F32, 55872 / KB)
        mod1 = at("mod1", [P, 16, 2], F32, 59968 / KB)
        mod2 = at("mod2", [P, 32], F32, 60096 / KB)
        mod_sum = at("mod_sum", [P, 4], F32, 60224 / KB)
        amp1 = at("amp1", [P, KC, 2], F32, 60288 / KB)
        amp2 = at("amp2", [P, KC], F32, 60352 / KB)
        eps = at("eps", [P, 1], F32, 60384 / KB)
        gain_xg = at("gain_xg", [P, KC], F32, 60416 / KB)
        root_g = at("root_g", [P, KC], F32, 60448 / KB)
        eps_xg = at("eps_xg", [P, 1], F32, 61056 / KB)
        b_dec_h = at("b_dec_h", [P, 1], F32, 60480 / KB)
        dec = at("dec", [P, NCHC], F32, 60512 / KB)
        lb = at("lb", [P, HG], F32, 60576 / KB)
        om_lb = at("om_lb", [P, HG], F32, 60608 / KB)
        lb_t = at("lb_t", [P, 16], F32, 60640 / KB)
        inv_cnt = at("inv_cnt", [P, CPC, 16], F32, 60704 / KB)
        cnt_i = at("cnt_i", [P, 16], I32, 60960 / KB)
        o_ss = at("o_ss", [P, TT], F32, 61024 / KB)
        o_rstd = at("o_rstd", [P, TT], F32, 61088 / KB)
        cnt_f = at("cnt_f", [P, 16], F32, 61120 / KB)
        spare = at("spare", [P, 16], F32, 61184 / KB)

        h1_hi, h1_lo = at("h1_hi", [P, KC, T], F32R, 60), at("h1_lo", [P, KC, T], F32R, 92)
        x_all = at("x_all", [P, KC, TC], F32, 128)
        hc_hi, hc_lo = at("hc_hi", [P, KC, CTX], F32R, 152), at("hc_lo", [P, KC, CTX], F32R, 160)
        sq0 = [at(f"sq0_{i}", [P, TC], F32, 168 + 3 * i) for i in range(2)]
        rstd0 = at("rstd0", [P, TC], F32, 174)
        cond = at("cond", [P, 2, D], F32, 196)
        ada1_w = [at(f"ada1_w{i}", [P, D], F32, 108 + 4 * i) for i in range(4)]
        ada1_out = [at("ada1_out0", [P, D], F32, 124), at("ada1_out1", [P, D], F32, 80)]
        dd_raw, dd_hi, dd_lo = at("dd_raw", [P, D], F32, 184), at("dd_hi", [P, D], F32R, 188), at("dd_lo", [P, D], F32R, 192)
        q_sb = at("q_sb", [P, HEADS, T], F32, 108)
        k_sb = at("k_sb", [P, HEADS, TC], F32, 116)
        v_sb = at("v_sb", [P, HEADS, TTC * HEAD_V], F32, 128)
        y_sb = at("y_sb", [P, KC, T], F32, 152)
        g_sb = at("g_sb", [P, KC, T], F32, 168)
        vT = [at(f"vT{i}", [P, TC], F32, 82 + 3 * i) for i in range(2)]
        dd_sb = at("dd_sb", [32, TC], F32, 76)
        state = [at(f"state{i}", [P, HEAD_V], F32, 79 + i) for i in range(3)]
        v_h = at("v_h", [P, TTC, HEAD_V], F32, 82)
        s_dir = [at("s_f", [P, TT, P], F32, 205), at("s_b", [P, TT, P], F32, 88)]
        cc_sb = at("cc_sb", [P, T], F32, 90)
        t0, t1, t2 = (at(f"t{i}", [P, TC], F32, 184 + 3 * i) for i in range(3))
        o_tok = [at(f"o_tok{b}", [P, 2, HEAD_V], F32, kb) for b, kb in enumerate((166, 182))]
        o_tok_last = [at(f"o_tok_last{b}", [P, 2, HEAD_V], F32, 184 + 2 * b) for b in range(2)]
        q_mid, k_mid, q_dec = (at(n, [P, T], F32, 193 + 2 * i) for i, n in enumerate(("q_mid", "k_mid", "q_dec")))
        k_dec = at("k_dec", [P, TC], F32, 199)
        kd_tok = at("kd_tok", [P, TTC, P], F32, 202)
        w_up_h = at("w_up_h", [32, P], F32, 207)

        og_hi, og_lo = at("og_hi", [P, KC, T], F32R, 108), at("og_lo", [P, KC, T], F32R, 184)
        og_sg = [at(f"og_sg{i}", [P, T], F32, 124 + 2 * i) for i in range(2)]
        og_val = [at(f"og_val{i}", [P, T], F32, 200 + 2 * i) for i in range(2)]
        y_hi, y_lo = at("y_hi", [P, KC, T], F32R, 128), at("y_lo", [P, KC, T], F32R, 168)
        mg_hi, mg_lo = at("mg_hi", [P, KC, T], F32R, 152), at("mg_lo", [P, KC, T], F32R, 76)
        ada_w = [at(f"ada_w{i}", [P, D], F32, 144 + 4 * i) for i in range(2)]
        sig_a, mrg_a = at("sig_a", [P, T], F32, 124), at("mrg_a", [P, T], F32, 126)
        sig_b, mrg_b = at("sig_b", [P, T], F32, 200), at("mrg_b", [P, T], F32, 202)
        mrg_v = at("mrg_v", [P, T], F32, 204)
        x_res = at("x_res", [P, KC, T], F32, 108)

        x = at("x", [P, KC, T], F32, 60)
        h_hi, h_lo = at("h_hi", [P, KC, T], F32R, 76), at("h_lo", [P, KC, T], F32R, 92)
        gu_hi, gu_lo = at("gu_hi", [P, FC, T], F32R, 108), at("gu_lo", [P, FC, T], F32R, 152)
        sa = [at(f"sa{i}", [P, T], F32, 196 + 2 * i) for i in range(2)]
        fval = [at(f"fval{i}", [P, T], F32, 200 + 2 * i) for i in range(2)]
        sq = [at(f"sq{i}", [P, T], F32, 196 + 2 * i) for i in range(2)]
        acc = at("acc", [P, T], F32, 200)
        nv = [at("nv0", [P, T], F32, 202), at("nv1", [P, T], F32, 196)]
        acc2 = at("acc2", [P, T], F32, 202)
        rstd_xg = at("rstd_xg", [P, T], F32, 198)
        rstd = at("rstd", [P, T], F32, 204)

        APAD, UPAD = CONVW - 1, 16
        a_sb = at("a_sb", [P, CPC, APAD + T], F32, 108)
        u_sb = at("u_sb", [P, CPC, UPAD + T], F32, 117)
        cv = at("cv", [P, CPC, T], F32, 126)
        cat_hi, cat_lo = at("cat_hi", [P, KC, T], F32R, 134), at("cat_lo", [P, KC, T], F32R, 150)
        win = [at(f"win{i}", [P, UPAD + T], F32, 166 + 2.25 * i) for i in range(2)]
        pd = at("pd", [P, CPC, T], F32, 171)
        tap = [at(f"tap{i}", [P, P], F32, 179 + 0.5 * i) for i in range(4)]
        pool_w = at("pool_w", [P, CPC, P], F32, 181)
        csg = [at(f"csg{i}", [P, T], F32, 183 + 2 * i) for i in range(2)]
        csq = at("csq", [P, CPC, T], F32, 187)
        lnv = [at(f"lnv{i}", [P, T], F32, 183 + 2 * i) for i in range(2)]
        lns = [at(f"lns{i}", [P, T], F32, 166 + 2 * i) for i in range(2)]

        r_hi, r_lo = at("r_hi", [P, KC, T], F32R, 108), at("r_lo", [P, KC, T], F32R, 124)
        hq, hk, hb, hg, hv = ([at(f"{n}{i}", [P, T], F32, 140 + 10 * i + 2 * m) for i in range(2)]
                              for m, n in enumerate(("hq", "hk", "hb", "hg", "hv")))
        hv_tok, hkd_tok = at("hv_tok", [P, TT, P], F32, 160), at("hkd_tok", [P, TT, P], F32, 162)
        hx = [at(f"hx{i}", [P, T], F32, 164 + 2 * i) for i in range(6)]
        hqb, hkd = at("hqb", [P, T], F32, 176), at("hkd", [P, T], F32, 178)
        hd = [at(f"hd{i}", [P, T], F32, 180 + 2 * i) for i in range(2)]
        he = [at(f"he{i}", [P, T], F32, 184 + 2 * i) for i in range(2)]
        hs = at("hs", [P, TT, P], F32, 188)
        hst = at("hst", [P, NCH, P], F32, 190)
        ho_tok = at("ho_tok", [P, TT, P], F32, 194)
        hsf = at("hsf", [P, T], F32, 196)
        hval = at("hval", [P, T], F32, 198)
        hlf = at("hlf", [P, T], F32, 200)
        hdec = at("hdec", [P, NCH], F32, 206)
        hsquares = at("hsquares", [P, T], F32, 202)

        ps = ctx.enter_context(nc.psum_tensor("ps", [P, 8, 512], F32))
        z_ps = ps[:, 6:8, :].rearrange("p a n -> p (a n)")

        cond2 = ps[:, 4:6, :].rearrange("p a n -> p (a n)")

        block = ctx.enter_context(nc.Block())

        class Semaphores(dict):
            def __missing__(self, name):
                self[name] = ctx.enter_context(nc.semaphore(name))
                return self[name]

        S = Semaphores()
        raw_full, hi_done, lo_done, unit_done = ([S[f"{n}{s}"] for s in range(4)]
                                                 for n in ("raw_full", "hi_done", "lo_done", "unit_done"))

        def v_at(name, i=0, n=1):
            return vec[:, VEC[name] + i:VEC[name] + i + n]

        def v_dyn(name, i, n=1):
            if isinstance(i, int):
                return v_at(name, i, n)
            return vec[:, bass.ds(VEC[name] + i, n)]

        def wait_former(eng, sem, count):
            if not (isinstance(count, int) and count == 0):
                eng.wait_ge(sem, count)

        def wait_apart(eng, sem, count):
            if isinstance(count, int):
                wait_former(eng, sem, count)
                return
            need = eng.snap(count)
            eng.wait_ge(S["const_ready"], 1)
            eng.wait_ge(sem, need)

        def sp_unit(sp, s, q, src, n=D):
            wait_former(sp, lo_done[s], q)
            sp.dma_start(raw[s][:, 0:n], src).then_inc(raw_full[s], 16)

        def sp_rounds(sp, q0, n, units):
            with sp.Fori(0, n) as r:
                for s in range(4):
                    sp_unit(sp, s, r + q0, units[bass.ds(r, 1), s].squeeze(0))

        def sp_start(sp):
            sp.dma_start(cond[:, :, :], dram["conditions"].unsqueeze(0).broadcast_to([P, 2, D])).then_inc(S["small_in"], 16)
            sp.dma_start(vec[:, :], dram["vectors"]).then_inc(S["vec_in"], 16)

            def ada(a):
                if a >= 4:
                    sp.wait_ge(S["ada1_used"], a - 3)
                sp.dma_start(ada1_w[a % 4][:, :], dram["w_ada"][a // 2 + KC * (a % 2)]).then_inc(S[f"ada_full{a % 4}"], 16)

            for a in (0, 1):
                ada(a)
            sp.dma_start(x_all[:, :, 0:T], dram["x"]).then_inc(S["x_in"], 16)
            ada(2)
            sp.dma_start(x_all[:, :, T:TC], dram["ctx"]).then_inc(S["ctx_in"], 16)
            for a in (3, 4, 5):
                ada(a)
            sp.dma_start(dd_raw[:, :], dram["w_decay"]).then_inc(S["dd_in"], 16)
            sp.wait_ge(S["const_step"], 1)
            for d in range(2):
                sp.dma_start(w_up[16 * d:16 * d + 16, d, :, :], dram["w_dec_up"][d]).then_inc(S["dd_in"], 16)
            for s in range(4):
                sp_unit(sp, s, 0, dram["w_qkv"][0, s])
                if s == 1:
                    for a in (6, 7):
                        ada(a)
            for a in range(8, 16):
                ada(a)
            for q in range(1, 4):
                for s in range(4):
                    sp_unit(sp, s, q, dram["w_qkv"][q, s])
            sp_rounds(sp, Q_GLA, 8, dram["w_conv_gate"])

        def sp_ada(sp, a, i):
            sp.wait_ge(S["ada2_used"], a - 1)
            sp.dma_start(ada_w[i][:, :], dram["w_ada"][bass.ds(a + 16, 1)].squeeze(0)).then_inc(S[f"ada_full{i}"], 16)

        def sp_merge(sp):
            for q in range(Q_MERGE, Q_MERGE + 2):
                for s in range(4):
                    sp_unit(sp, s, q, dram["w_merge"][q - Q_MERGE, s])
            sp.wait_ge(S["og_val"], KC)
            sp.dma_start(ada_w[1][:, :], dram["conditions"][0:1].broadcast_to([P, D])).then_inc(S["small_in"], 16)
            sp.dma_start(ada_w[0][:, :], dram["w_ada"][16]).then_inc(S["ada_full0"], 16)
            sp.wait_ge(S["cond_ready"], 3)
            sp.dma_start(ada_w[1][:, :], dram["w_ada"][17]).then_inc(S["ada_full1"], 16)
            with sp.Fori(0, 6) as r:
                for half in range(2):
                    for s in (2 * half, 2 * half + 1):
                        sp_unit(sp, s, r + (Q_MERGE + 2), dram["w_merge"][bass.ds(r + 2, 1), s].squeeze(0))
                    for i in range(2):
                        sp_ada(sp, 4 * r + (2 * half + 2 + i), i)
            for r in (6, 7):
                for half in range(2):
                    for s in (2 * half, 2 * half + 1):
                        sp_unit(sp, s, Q_MIX + r - 6, dram["w_mix"][r - 6, s])
                    for i in range(2):
                        a = 4 * r + 2 * half + 2 + i
                        if a < 32:
                            sp.wait_ge(S["ada2_used"], a - 1)
                            sp.dma_start(ada_w[i][:, :], dram["w_ada"][a + 16]).then_inc(S[f"ada_full{i}"], 16)
            sp.wait_ge(unit_done[0], Q_MERGE + 8)
            sp.dma_start(x_res[:, :, :], dram["x"]).then_inc(S["small_in"], 16)

        def sp_ffn(sp, e):
            sp_rounds(sp, Q_FFI[e], FC // 2, dram["w_ffn_in"][e])
            with sp.Fori(0, KC) as n:
                for s in range(4):
                    sp_unit(sp, s, n + Q_FFO[e],
                            dram["w_ffn_out"][e][bass.ds(n, 1), :, FFO_AT[s] * P:(FFO_AT[s] + FFO[s]) * P].squeeze(0),
                            FFO[s] * P)

        def sp_cp(sp):
            for s in range(4):
                sp_unit(sp, s, Q_CPI, dram["w_cp"][0, s])
            sp.wait_ge(S["resid_x"], 16)
            sp.dma_start(pool_w[:, :, :], dram["pool_w"]).then_inc(S["small_in"], 16)
            sp_rounds(sp, Q_CPI + 1, 4, dram["w_cp"][1:5])

        @block.sync
        def _(sp):
            sp_start(sp)
            sp_merge(sp)
            sp_ffn(sp, 0)
            sp_cp(sp)
            sp_ffn(sp, 1)
            sp_rounds(sp, Q_HG, 10, dram["w_hg"])
            sp_ffn(sp, 2)
            for k in range(0, KC, 2):
                sp.wait_ge(S["out_ready"], k + 2)
                sp.dma_start(dram["out"][:, k:k + 2, :], x[:, k:k + 2, :]).then_inc(S["out_stored"], 16)
            sp.wait_ge(S["out_stored"], 16 * KC // 2)

        def pool_lo(pool, s, q, n=D):
            pool.wait_ge(hi_done[s], q + 1)
            wait_former(pool, unit_done[s], q)
            pool.tensor_tensor(w_lo[s][:, 0:n], raw[s][:, 0:n], w_hi[s][:, 0:n].bitcast(F32),
                               ALU.subtract).then_inc(lo_done[s], 1)

        def pool_rounds(pool, q0, q1, sizes=(D, D, D, D)):
            with pool.Fori(q0, q1) as q:
                for s in range(4):
                    pool_lo(pool, s, q, sizes[s])

        def pool_constants(pool):
            done = 0

            def step(ins):
                nonlocal done
                ins.then_inc(S["const_step"], 1)
                done += 1
                pool.wait_ge(S["const_step"], done)

            step(pool.memset(w_up[:, :, :, :], 0.0))
            step(pool.memset(ones[:, :], 1.0))
            step(pool.memset(ident[:, :], 0.0))
            step(pool.affine_select(out=ident[:, :], in_=ident[:, :], compare_op=ALU.not_equal, fill=1.0,
                                    base=0, pattern=[[-1, P]], channel_multiplier=1))
            for d in range(2):
                step(pool.memset(causal[d][:, :], 1.0))
                sign = 1 - 2 * d
                step(pool.affine_select(out=causal[d][:, :], in_=causal[d][:, :], compare_op=ALU.is_ge, fill=0.0,
                                        base=0, pattern=[[sign, P]], channel_multiplier=-sign))
                step(pool.memset(causal[d][CH * d:CH * d + CH, CH - CH * d:P - CH * d], 0.0))
            step(pool.memset(keep[:, :], 1.0))
            step(pool.memset(keep[:, 0:TC + 1:CH], 0.0))
            step(pool.iota(cnt_i[:, :], pattern=[[1, 16]], base=1, channel_multiplier=0))
            step(pool.memset(eps_xg[:, :], EPS * EPS))
            pool.memset(eps[:, :], EPS).then_inc(S["const_ready"], 1)

        def pool_normalise(pool):
            pool.wait_ge(S["dd_hi"], 1)
            pool.tensor_tensor(dd_lo[:, :], dd_raw[:, :], dd_hi[:, :].bitcast(F32), ALU.subtract).then_inc(S["dd_split"], 1)
            for s in range(2):
                pool_lo(pool, s, 0)
            pool.wait_ge(S["norm_rstd"], 2)
            for k in range(KC):
                pool.tensor_tensor(x_all[:, k, :], x_all[:, k, :], rstd0[:, :], ALU.mult).then_inc(S["x_normed"], 1)
                if k in (0, 1):
                    pool_lo(pool, k + 2, 0)

        def pool_levels(pool):
            done = 0

            def step(ins):
                nonlocal done
                done += 1
                ins.then_inc(S["level_step"], 1)
                pool.wait_ge(S["level_step"], done)

            pool.wait_ge(S["w_up_copied"], 2 * HEADS)
            step(pool.memset(level_mask[:, :, :], 0.0))
            for i, m in enumerate(LEVELS):
                second = level_mask[:, i, :].rearrange("p (b a m) -> p b a m", a=2, m=m)[:, :, 1, :]
                step(pool.memset(second, 1.0))
                step(pool.affine_select(out=second, in_=second, compare_op=ALU.is_ge, fill=0.0, base=0,
                                        pattern=[[-2 * m, P // (2 * m)], [0, m]], channel_multiplier=1))
                step(pool.affine_select(out=second, in_=second, compare_op=ALU.is_ge, fill=0.0, base=m - 1,
                                        pattern=[[2 * m, P // (2 * m)], [0, m]], channel_multiplier=-1))

        def pool_pooling(pool):
            steps = 0

            def step(ins):
                nonlocal steps
                ins.then_inc(S["window"], 1)
                steps += 1
                pool.wait_ge(S["window"], steps)

            pool.wait_ge(S["zeros"], 6)
            pool.wait_ge(S["norm_rstd"], 6)
            pool.wait_ge(S["dve_step"], 11 + 2 * CPC)
            for g in range(CPC):
                pool.wait_ge(S["cp_u"], g + 1)
                step(pool.tensor_tensor(u_sb[:, g, UPAD:], u_sb[:, g, UPAD:], rstd_xg[:, :], ALU.mult))
                src = u_sb[:, g, :]
                for e in range(g + 1):
                    dst = win[e % 2]
                    step(pool.tensor_tensor(dst[:, UPAD:], src[:, UPAD:], src[:, UPAD - (1 << e):UPAD + T - (1 << e)],
                                            ALU.add))
                    src = dst[:, :]
                step(pool.tensor_scalar(pd[:, g, 16:T], src[:, UPAD + 16:], 1.0 / (2 << g), None, ALU.mult))
                step(pool.tensor_tensor(pd[:, g, 0:16], src[:, UPAD:UPAD + 16], inv_cnt[:, g, :], ALU.mult))
                pool.tensor_tensor(pd[:, g, :], pd[:, g, :], u_sb[:, g, UPAD:], ALU.subtract).then_inc(S["pd_ready"], 1)

        @block.gpsimd
        def _(pool):
            pool_constants(pool)
            pool_normalise(pool)
            pool_rounds(pool, 1, Q_FFI[0])
            pool_levels(pool)
            ffo = [n * P for n in FFO]
            pool_rounds(pool, Q_FFI[0], Q_FFO[0])
            pool_rounds(pool, Q_FFO[0], Q_CPI, ffo)
            pool_rounds(pool, Q_CPI, Q_CPO + 1)
            pool_pooling(pool)
            pool_rounds(pool, Q_CPO + 1, Q_FFO[1])
            pool_rounds(pool, Q_FFO[1], Q_HG, ffo)
            pool_rounds(pool, Q_HG, Q_FFO[2])
            pool_rounds(pool, Q_FFO[2], Q_END, ffo)

        def products(pe, out, s, k, hi, lo, first, last):
            wl, wh = w_lo[s][:, k * P:(k + 1) * P], w_hi[s][:, k * P:(k + 1) * P]
            pe.matmul(out, wl, hi, start=first, stop=False)
            pe.matmul(out, wh, lo, start=False, stop=False)
            return pe.matmul(out, wh, hi, start=False, stop=last)

        def pe_unit(pe, bank, s, q, hi, lo, ready=None):
            pe.wait_ge(lo_done[s], q + 1)
            for k in range(KC):
                if ready:
                    ready(k)
                mm = products(pe, ps[:, bank, :], s, k, hi[:, k, :], lo[:, k, :], k == 0, k == KC - 1)
            mm.then_inc(unit_done[s], 1)

        def pe_pair(pe, q, hi, lo, ready):
            for k in range(KC):
                ready(k)
                for s in (0, 1):
                    if k == 0:
                        pe.wait_ge(lo_done[s], q + 1)
                    mm = products(pe, ps[:, s, :], s, k, hi[:, k, :], lo[:, k, :], k == 0, k == KC - 1)
                    if k == KC - 1:
                        mm.then_inc(unit_done[s], 1)

        def pe_start(pe):
            pe.wait_ge(S["const_ready"], 1)
            for i, (ready, out, cols) in enumerate((("norm_sq", ps[:, 4, :], slice(0, T)),
                                                    ("ctx_sq", ps[:, 5, 0:CTX], slice(T, TC)))):
                for k in range(KC):
                    pe.wait_ge(S[ready], k + 1)
                    pe.matmul(out, ones[:, :], sq0[k % 2][:, cols], start=(k == 0), stop=(k == KC - 1))\
                      .then_inc(S["sq0_mm"], 1)
            pe.wait_ge(S["dd_split"], 1)
            for k in range(KC):
                pe.wait_ge(S["h_lo"], k + 1)
                wl, wh = dd_lo[:, k * P:(k + 1) * P], dd_hi[:, k * P:(k + 1) * P]
                for out, hi, lo in ((ps[:, 6, :], h1_hi, h1_lo), (ps[:, 7, 0:CTX], hc_hi, hc_lo)):
                    pe.matmul(out, wl, hi[:, k, :], start=(k == 0), stop=False)
                    pe.matmul(out, wh, lo[:, k, :], start=False, stop=False)
                    mm = pe.matmul(out, wh, hi[:, k, :], start=False, stop=(k == KC - 1))
                if k == KC - 1:
                    mm.then_inc(S["dd_mm"], 1)
                for s in range(4):
                    pe.wait_ge(lo_done[s], 1)
                    mm = products(pe, ps[:, s, :], s, k, h1_hi[:, k, :], h1_lo[:, k, :], k == 0, k == KC - 1)
                    if k == KC - 1:
                        mm.then_inc(unit_done[s], 1)

        def pe_qkv(pe):
            def unit(u):
                s, q, bank = u % 4, u // 4, u % 2
                pe.wait_ge(lo_done[s], q + 1)
                pe.wait_ge(S["qkv_lat_read"], u if u >= 6 else u - 2)
                for k in range(KC):
                    mm = products(pe, ps[:, bank, :], s, k, h1_hi[:, k, :], h1_lo[:, k, :], k == 0, k == KC - 1)
                pe.wait_ge(*((S["qkv_ctx_read"], u - 4) if u >= 6 else (S["qkv_lat_read"], u)))
                for k in range(KC):
                    mm = products(pe, ps[:, 2 + bank, 0:CTX], s, k, hc_hi[:, k, :], hc_lo[:, k, :],
                                  k == 0, k == KC - 1)
                mm.then_inc(unit_done[s], 1)

            def v_turn(m):
                pe.wait_ge(S["qkv_lat_read"], m + 10)
                pe.wait_ge(S["qkv_ctx_read"], m + 6)
                if m >= 2:
                    pe.wait_ge(S["v_read"], m - 1)
                for c in range(TTC):
                    mm = pe.transpose(ps[:, (4 if c < TT else 6) + m % 2, (c % TT) * P:(c % TT + 1) * P],
                                      vT[m % 2][:, c * P:(c + 1) * P], ident[:, :])
                mm.then_inc(S["v_turned"], 1)

            for u in range(4, 16):
                unit(u)
                if u > 8:
                    v_turn(u - 9)
            v_turn(7)

        def pe_gla(pe):
            pe.wait_ge(S["v_read"], 8)

            def turn_back(h, tok):
                pe.wait_ge(S["o_tok_ready"], 2 * h + 2)
                if tok is o_tok:
                    pe.wait_ge(S["z_log"], 6 * h + 7)
                    pe.wait_ge(S["decay_sum"], 10 * h + 11)
                for c in range(TT):
                    for half in range(2):
                        mm = pe.transpose(ps[:, 6 + half, c * P:(c + 1) * P],
                                          tok[c // 2][:, c % 2, half * P:(half + 1) * P], ident[:, :])
                mm.then_inc(S["oT_mm"], 1)

            def head(h):
                for d in range(2):
                    w = 2 * h + d
                    pe.wait_ge(S["w_up_copied"], w + 1)
                    wait_former(pe, S["kd_read"], 2 * w)
                    wait_former(pe, S["state_step"], 11 * w)
                    pe.matmul(ps[:, 6, :], w_up_h[:, :], dd_sb[:, 0:T], start=True, stop=True)
                    pe.matmul(ps[:, 7, 0:CTX], w_up_h[:, :], dd_sb[:, T:TC], start=True, stop=True)\
                      .then_inc(S["z_mm"], 1)
                    for s, (name, n) in enumerate((("kd_read", 2 * w), ("scores_read", w), ("state_step", 11 * w),
                                                   ("state_step", 11 * w))):
                        wait_former(pe, S[name], n)
                        pe_unit(pe, s, s, w + Q_GLA, h1_hi, h1_lo)
                        if d == 0 and s == 2 and not (isinstance(h, int) and h == 0):
                            turn_back(h - 1, o_tok)
                    pe.wait_ge(S["decayed"], 4 * w + 1)
                    pe.wait_ge(S["decay_sum"], 5 * w + 1)
                    pe.wait_ge(S["z_log"], 3 * w + 1)
                    wait_former(pe, S["oT_read_a"], h)
                    for c in range(TT, TTC):
                        mm = pe.transpose(ps[:, 6, (c - TT) * P:(c - TT + 1) * P], k_dec[:, c * P:(c + 1) * P], ident[:, :])
                    mm.then_inc(S["kd_scores_mm"], 1)
                    pe.wait_ge(S["cc_read"], w + 1)
                    for c in range(TT):
                        mm = pe.transpose(ps[:, 0, c * P:(c + 1) * P], k_dec[:, c * P:(c + 1) * P], ident[:, :])
                    mm.then_inc(S["kd_scores_mm"], 1)
                    pe.wait_ge(S["decayed"], 4 * w + 2)
                    pe.wait_ge(S["decayed"], 4 * w + 3)
                    pe.wait_ge(S["conv3"], 5 * w + 1)
                    for c in range(TT):
                        mm = pe.matmul(ps[:, 1, c * P:(c + 1) * P], k_mid[:, c * P:(c + 1) * P],
                                       q_mid[:, c * P:(c + 1) * P], start=True, stop=True)
                    mm.then_inc(S["kd_scores_mm"], 1)
                    order = [8, 9, 10, 11, *range(8)] if d == 0 else [11, 10, 9, 8, *range(7, -1, -1)]

                    def k_v(p):
                        if p == 0:
                            wait_former(pe, S["oT_read_d"], h)
                            pe.wait_ge(S["conv3"], 5 * w + 5)
                            pe.wait_ge(S["v_h_ready"], h + 1)
                            pe.wait_ge(S["kd_read"], 2 * w + 1)
                            pe.wait_ge(S["g_read"], w + 1)
                        else:
                            pe.wait_ge(S["kd_read"], 2 * w + 2)
                            if p >= 2:
                                pe.wait_ge(S["state_step"], 11 * w + 2 * (p - 1))
                        for n in (2 * p, 2 * p + 1):
                            if n < 11:
                                c, rows = order[n] // 2, slice(order[n] % 2 * CH, order[n] % 2 * CH + CH)
                                pe.matmul(ps[:, (2, 3, 6, 7)[n % 4], 0:HEAD_V],
                                          kd_tok[rows, c, :], v_h[rows, c, :], start=True, stop=True)\
                                  .then_inc(S["kv_mm"], 1)

                    def o_at(c, rows=slice(0, P)):
                        return ps[rows, 4 + c // 2, (c % 2) * HEAD_V:(c % 2 + 1) * HEAD_V]

                    def inter(i):
                        pe.wait_ge(S["state_step"], 11 * w + 4 + i)
                        g = order[4 + i]
                        rows = slice(g % 2 * CH, g % 2 * CH + CH)
                        pe.matmul(o_at(g // 2, rows), q_dec[:, g * CH:(g + 1) * CH], state[(4 + i) % 3][:, :],
                                  start=False, stop=(i == 7 and d == 1), skip_group_check=True)\
                          .then_inc(S["inter_mm"], 1)

                    k_v(0)
                    k_v(1)
                    pe.wait_ge(S["scores_read"], w + 1)
                    if d == 0:
                        wait_former(pe, S["o_tok_ready"], 2 * h)
                    for c in range(TT):
                        pe.matmul(o_at(c), s_dir[d][:, c, :], v_h[:, c, :], start=(d == 0 and c % 2 == 0), stop=False,
                                  skip_group_check=True)
                    k_v(2)
                    pe.wait_ge(S["decayed"], 4 * w + 4)
                    for p in range(3, 6):
                        k_v(p)
                        inter(2 * p - 6)
                        inter(2 * p - 5)
                    inter(6)
                    inter(7)

            head(0)
            with pe.Fori(1, HEADS - 1) as h:
                head(h)
            head(HEADS - 1)
            pe.wait_ge(S["scores_read"], 2 * HEADS)
            pe_unit(pe, 1, 1, Q_MERGE, h1_hi, h1_lo)
            turn_back(HEADS - 1, o_tok_last)

        def pe_merge(pe):
            def merge(r, order=None):
                units = ((og_hi, og_lo, "og_lo"), (h1_hi, h1_lo, None), (y_hi, y_lo, "y_lo"), (h1_hi, h1_lo, None))
                for s in order or range(4):
                    hi, lo, split = units[s]
                    wait_former(pe, S["merge_a" if s < 2 else "merge_b"], r)
                    chunk = (lambda k, split=split: pe.wait_ge(S[split], k + 1)) if order and split else None
                    pe_unit(pe, s, s, r + Q_MERGE, hi, lo, chunk)

            pe.wait_ge(S["state_step"], 11 * 2 * HEADS)
            merge(0, (3, 0, 2))
            with pe.Fori(1, KC) as r:
                merge(r)

        def pe_columns(pe, q, hi, lo, columns_read):
            for s in range(4):
                pe.wait_ge(S["resid_x"], columns_read + s + 1)
                pe_unit(pe, s, s, q, hi, lo)

        def pe_mix(pe):
            def output(s, k):
                return products(pe, ps[:, s, :], s, k, mg_hi[:, k, :], mg_lo[:, k, :], k == 0, k == KC - 1)

            for s in (0, 1):
                pe.wait_ge(lo_done[s], Q_MIX + 1)
                pe.wait_ge(S["merge_a"], KC)
                for k in range(KC - 1):
                    pe.wait_ge(S["mg_lo"], k + 1)
                    output(s, k)
            pe.wait_ge(S["mg_lo"], KC)
            for s in (0, 1):
                output(s, KC - 1).then_inc(unit_done[s], 1)
            for s in (2, 3):
                pe.wait_ge(S["merge_b"], KC)
                pe_unit(pe, s, s, Q_MIX, mg_hi, mg_lo)
            pe_columns(pe, Q_MIX + 1, mg_hi, mg_lo, 0)

        def pe_norm(pe, n_acc):
            pe.wait_ge(S["norm_acc"], n_acc)
            pe.matmul(ps[:, 6, :], ones[:, :], acc[:, :], start=True, stop=True).then_inc(S["norm_stat"], 1)

        def h_ready(pe, base):
            return lambda k: pe.wait_ge(S["h_lo"], base + k + 1)

        def pe_ffn(pe, e, h_base, resid_base, n_acc=None):
            def hidden(r):
                q = r + Q_FFI[e]
                for s in range(4):
                    if s % 2 == 0:
                        wait_former(pe, S[f"ffn_val{s // 2}"], r + 11 * e)
                    if isinstance(r, int) and e == 0 and s < 2:
                        if s == 0:
                            pe_pair(pe, q, h_hi, h_lo, h_ready(pe, h_base))
                        continue
                    if isinstance(r, int):
                        pe.wait_ge(S["resid_x"], resid_base - 3 + s)
                    pe_unit(pe, s, s, q, h_hi, h_lo, h_ready(pe, h_base) if s == 0 else None)
                    if isinstance(r, int) and s == 0 and n_acc:
                        pe_norm(pe, n_acc)

            hidden(0)
            with pe.Fori(1, FC // 2) as r:
                hidden(r)
            with pe.Fori(0, KC // 2) as m:
                for p in range(2):
                    q = 2 * m + (p + Q_FFO[e])
                    for i in range(2):
                        pe.wait_ge(S[f"ffn_lo{i}"], 11 * (e + 1) - 1)
                    pe.wait_ge(S["resid_x"], 2 * m + (p + resid_base - 1))
                    for s in range(4):
                        pe.wait_ge(lo_done[s], q + 1)
                        for k in range(FFO[s]):
                            g = FFO_AT[s] + k
                            if g >= FC - 2:
                                pe.wait_ge(S[f"ffn_lo{g % 2}"], 11 * (e + 1))
                            mm = products(pe, ps[:, 4 + p, :], s, k, gu_hi[:, g, :], gu_lo[:, g, :], g == 0, g == FC - 1)
                        mm.then_inc(unit_done[s], 1)

        def pe_cp(pe):
            for r in range(2):
                for s in range(4):
                    wait_former(pe, S[f"conv_in{s // 2}"], r)
                    pe_unit(pe, s, s, r + Q_CPI, h_hi, h_lo, h_ready(pe, 16) if s == 0 else None)
                    if r == 0 and s == 0:
                        pe.wait_ge(S["dve_step"], 11)
                        pe.matmul(ps[:, 7, :], ones[:, :], acc2[:, :], start=True, stop=True).then_inc(S["norm_stat"], 1)
                        pe_norm(pe, 7 + 2 * 7)
            for s in range(4):
                pe.wait_ge(S[f"conv_in{s // 2}"], 2)
                pe_unit(pe, s, s, Q_CPI + 2, h_hi, h_lo)
            pe.wait_ge(S["conv_in1"], 2)
            for i in range(CONVW):
                pe.wait_ge(S["tap_ready"], i + 1)
                pe.matmul(ps[:, 4, :], tap[i % 4][:, :], a_sb[:, 3, i:i + T], start=(i == 0), stop=(i == CONVW - 1))\
                  .then_inc(S["tap_mm"], 1)
            pe.wait_ge(S["small_in"], 64)
            for g in range(CPC):
                pe.wait_ge(S["pd_ready"], g + 1)
                pe.wait_ge(S["cp_u"], g + 1)
                pe.matmul(ps[:, g, :], pool_w[:, g, :], pd[:, g, :], start=True, stop=True).then_inc(S["pool_mm"], 1)
            for name, n in (("conv_dve", 3 * CONVW), ("conv_pe", 1)):
                pe.wait_ge(S[name], n)
            for g in range(CPC):
                mm = pe.matmul(ps[:, 5, :], ones[:, :], cv[:, g, :], start=(g == 0), stop=(g == CPC - 1))
            mm.then_inc(S["ln_sum"], 1)

            def output(s, k):
                return products(pe, ps[:, s, :], s, k, cat_hi[:, k, :], cat_lo[:, k, :], k == CPC, k == CPC - 1)

            def pooled(s):
                pe.wait_ge(lo_done[s], Q_CPO + 1)
                pe.wait_ge(S["cat_lo_p"], CPC)
                for k in range(CPC, KC):
                    output(s, k)

            pooled(0)
            pe.wait_ge(S["ln_sq"], CPC)
            for g in range(CPC):
                mm = pe.matmul(ps[:, 6, :], ones[:, :], csq[:, g, :], start=(g == 0), stop=(g == CPC - 1))
            mm.then_inc(S["norm_stat"], 1)

            for s in range(1, 4):
                pooled(s)
            for k in range(CPC):
                pe.wait_ge(S["cat_lo_a"], k + 1)
                for s in range(4):
                    mm = output(s, k)
                    if k == CPC - 1:
                        mm.then_inc(unit_done[s], 1)
            pe_columns(pe, Q_CPO + 1, cat_hi, cat_lo, 16)

        def pe_hg(pe):
            taken = ("hg_f_read", "hg_q_read", "hg_i_read", "hg_g_read")

            def units(w, free, between=None):
                for s in range(4):
                    free(s)
                    pe_unit(pe, s, s, w + Q_HG, h_hi, h_lo)
                    if s == 1 and between:
                        between()

            def turn_back(g):
                pe.wait_ge(S["ho_tok_ready"], g + 1)
                pe.wait_ge(S["hkd_tok_ready"], g + 1)
                for c in range(TT):
                    mm = pe.transpose(ps[:, 4, c * P:(c + 1) * P], ho_tok[:, c, :], ident[:, :])
                mm.then_inc(S["hoT_mm"], 1)

            def mix(g, par, heads_taken, banks=4):
                pe.wait_ge(S["hkd_ready"], g + 1)
                wait_former(pe, S["hval_ready"], g)
                for c in range(TT):
                    mm = pe.transpose(ps[:, 4, c * P:(c + 1) * P], hkd[:, c * P:(c + 1) * P], ident[:, :])
                mm.then_inc(S["hkd_mm"], 1)
                pe.wait_ge(S["hg_i_read"], g + 1)
                wait_former(pe, S["ho_tok_ready"], g)
                for c in range(TT):
                    mm = pe.transpose(ps[:, 5, c * P:(c + 1) * P], hv[par][:, c * P:(c + 1) * P], ident[:, :])
                mm.then_inc(S["hv_mm"], 1)
                for l in range(7):
                    if l < banks:
                        pe.wait_ge(S[taken[l]], heads_taken)
                    else:
                        pe.wait_ge(S["hg_scores_read"], 7 * g + l - (banks - 1))
                    if l:
                        pe.wait_ge(S["hx_ready"], 12 * g + 2 * l)
                    for c in range(TT):
                        cols = slice(c * P, (c + 1) * P)
                        a, b = (hk[par], hq[par]) if l == 0 else (hx[l - 1], hx[l - 1])
                        mm = pe.matmul(ps[:, l % banks, cols], a[:, cols], b[:, cols], start=True, stop=True)
                    mm.then_inc(S["hg_scores_mm"], 1)
                pe.wait_ge(S["hkd_tok_ready"], g + 1)
                pe.wait_ge(S["hv_tok_ready"], g + 1)
                wait_former(pe, S["hg_state"], 7 * g)
                for n in range(7):
                    rows = slice(n % 2 * CH, n % 2 * CH + CH)
                    pe.matmul(ps[:, 6 + n % 2, (n // 2) * P:(n // 2 + 1) * P], hkd_tok[rows, n // 2, :],
                              hv_tok[rows, n // 2, :], start=True, stop=True).then_inc(S["hkv_mm"], 1)
                pe.wait_ge(S["hg_scores_read"], 7 * g + 7)
                for c in range(TT):
                    pe.matmul(ps[:, 5, c * P:(c + 1) * P], hs[:, c, :], hv_tok[:, c, :], start=(c == 0), stop=False,
                              skip_group_check=True)
                pe.wait_ge(S["hqb_ready"], g + 1)
                for n in range(1, NCH):
                    pe.wait_ge(S["hg_state"], 7 * g + n)
                    rows = slice(n % 2 * CH, n % 2 * CH + CH)
                    mm = pe.matmul(ps[rows, 5, (n // 2) * P:(n // 2 + 1) * P], hqb[:, n * CH:(n + 1) * CH], hst[:, n, :],
                                   start=False, stop=(n == NCH - 1), skip_group_check=True)
                mm.then_inc(S["ho_mm"], 1)

            pe_pair(pe, Q_HG, h_hi, h_lo, h_ready(pe, 32))
            for s in (2, 3):
                pe_unit(pe, s, s, Q_HG, h_hi, h_lo)
            units(1, lambda s: pe.wait_ge(S[taken[s]], 1))
            mix(0, 0, 2)
            last_score = (5, 6, 7, 4)
            with pe.Fori(0, 3) as m:
                for p in range(2):
                    units(2 * m + (2 + p), lambda s: pe.wait_ge(S["hg_scores_read"], 14 * m + (7 * p + last_score[s])),
                          between=lambda: turn_back(2 * m + p))
                    mix(2 * m + (1 + p), 1 - p, 2 * m + (3 + p))

            def output(s, k0, k1):
                for k in range(k0, k1):
                    pe.wait_ge(S["r_lo"], k + 1)
                    mm = products(pe, ps[:, s, :], s, k, r_hi[:, k, :], r_lo[:, k, :], k == 0, k == KC - 1)
                return mm

            for s in (2, 3):
                pe.wait_ge(lo_done[s], Q_HGO + 1)
                pe.wait_ge(S["hg_scores_read"], 7 * (HG - 1))
                if s == 3:
                    turn_back(6)
                output(s, 0, 6)
            mix(7, 1, HG, banks=2)
            for s in (2, 3):
                output(s, 6, 7)
            for s in (0, 1):
                pe.wait_ge(lo_done[s], Q_HGO + 1)
                pe.wait_ge(S["hg_scores_read"], 7 * HG)
                output(s, 0, 7)
                if s == 0:
                    turn_back(7)
            for s in range(4):
                output(s, 7, 8).then_inc(unit_done[s], 1)
            pe_columns(pe, Q_HGO + 1, r_hi, r_lo, 32)

        @block.tensor
        def _(pe):
            pe_start(pe)
            pe_qkv(pe)
            pe_gla(pe)
            pe_merge(pe)
            pe_mix(pe)
            pe_norm(pe, 7)
            pe_ffn(pe, 0, 8, 8)
            pe_cp(pe)
            pe_ffn(pe, 1, 24, 24, 7 * 4)
            pe_norm(pe, 7 * 5)
            pe_hg(pe)
            pe_ffn(pe, 2, 40, 40, 7 * 6)
            pe_norm(pe, 7 * 7)

        def act_hi(act, s, q, n=D):
            act.wait_ge(raw_full[s], 16 * (q + 1))
            wait_former(act, unit_done[s], q)
            act.activation(w_hi[s][:, 0:n], raw[s][:, 0:n], ACT.Copy).then_inc(hi_done[s], 1)

        def act_power(act, out, mean, sem, done, eps=eps, between=None):
            act.activation(out, mean, ACT.Ln, bias=eps[:, :]).then_inc(sem, 1)
            if between:
                between()
            act.wait_ge(sem, done + 1)
            act.activation(out, out, ACT.Exp, scale=-0.5).then_inc(sem, 1)

        def act_rstd(act, i, out, mean):
            act_power(act, out, mean, S["norm_rstd"], 2 * i)

        def act_start(act):
            act.wait_ge(S["dve_step"], 3)
            act.activation(lb_t[:, :], lb_t[:, :], ACT.Exp).then_inc(S["cond_ready"], 1)
            act.wait_ge(S["small_in"], 16)
            act.activation(cond[:, :, :], cond[:, :, :], ACT.Silu).then_inc(S["cond_ready"], 1)
            for i, (loaded, squared, cols) in enumerate((("x_in", "norm_sq", slice(0, T)), ("ctx_in", "ctx_sq", slice(T, TC)))):
                act.wait_ge(S[loaded], 16)
                for k in range(KC):
                    if k >= 2:
                        act.wait_ge(S["sq0_mm"], KC * i + k - 1)
                    act.activation(sq0[k % 2][:, cols], x_all[:, k, cols], ACT.Square, scale=ROOT).then_inc(S[squared], 1)
            act.wait_ge(S["dd_in"], 48)
            act.activation(dd_hi[:, :], dd_raw[:, :], ACT.Copy).then_inc(S["dd_hi"], 1)
            for s in range(2):
                act_hi(act, s, 0)
            act.wait_ge(S["sq0_mm"], 2 * KC)
            act.wait_ge(S["const_ready"], 1)
            act_rstd(act, 0, rstd0[:, :], ps[:, 4:6, :].rearrange("p a n -> p (a n)")[:, 0:TC])
            for s in range(2, 4):
                act_hi(act, s, 0)
            sides = ((slice(0, T), h1_hi), (slice(T, TC), hc_hi))
            for k in range(KC):
                act.wait_ge(S["x_normed"], k + 1)
                act.wait_ge(S["mod1_ready"], 2 * k + 2)
                for v, (cols, _) in enumerate(sides):
                    ins = act.activation(x_all[:, k, cols], x_all[:, k, cols], ACT.Identity, bias=mod1[:, k, v:v + 1],
                                         scale=amp1[:, k, v:v + 1])
                ins.then_inc(S["h_val"], 1)
                act.wait_ge(S["h_val"], k + 1)
                for cols, hi in sides:
                    ins = act.activation(hi[:, k, :], x_all[:, k, cols], ACT.Copy)
                ins.then_inc(S["h_hi"], 1)

        def act_qkv(act):
            act.wait_ge(S["dd_mm"], 1)
            act.activation(dd_sb[:, 0:T], ps[0:32, 6, :], ACT.Copy).then_inc(S["qkv_lat_read"], 1)
            for u in range(16):
                s, q = u % 4, u // 4
                act.wait_ge(unit_done[s], q + 1)
                if u < 4:
                    act.activation(q_sb[:, s, :], ps[:, s, :], ACT.Copy, scale=float(P) ** -0.5)\
                       .then_inc(S["qkv_lat_read"], 1)
                elif u < 8:
                    act.activation(k_sb[:, s, 0:T], ps[:, u % 2, :], ACT.Copy).then_inc(S["qkv_lat_read"], 1)
                else:
                    if u >= 10:
                        act.wait_ge(S["v_turned"], u - 9)
                    act.activation(vT[u % 2][:, 0:T], ps[:, u % 2, :], ACT.Copy).then_inc(S["qkv_lat_read"], 1)
                act_hi(act, s, q + 1)

        def act_gla(act):
            act.wait_ge(S["v_read"], 8)

            def decay_weights(h, d):
                w = 2 * h + d
                wait_former(act, S["z_mm"], w)
                wait_apart(act, S["decay_sum"], 5 * w)
                act.activation(b_dec_h[:, :], v_dyn("b_dec", h + 4 * d), ACT.Copy).then_inc(S["b_dec_copied"], 1)
                act.activation(w_up_h[:, :], at_index(w_up[:, d, :, :], h), ACT.Copy).then_inc(S["w_up_copied"], 1)

            def turned_back(h):
                act.wait_ge(S["oT_mm"], h + 1)
                act.activation(spare[:, 8:9], ones[:, 0:1], ACT.Copy)
                act.activation(at_index(v_sb, h)[:, 0:T], ps[:, 6, :], ACT.Copy).then_inc(S["oT_read_a"], 1)

            def head(h):
                for d in range(2):
                    w = 2 * h + d
                    if d == 0:
                        wait_apart(act, S["inter_mm"], 16 * h)
                        act.activation(v_h[:, :, :].rearrange("p c v -> p (c v)"), at_index(v_sb, h), ACT.Copy)\
                           .then_inc(S["v_h_ready"], 1)
                    act.wait_ge(S["z_mm"], w + 1)
                    act.wait_ge(S["b_dec_copied"], w + 1)
                    act.activation(t0[:, :], z_ps[:, 0:TC], ACT.Abs, bias=b_dec_h[:, :]).then_inc(S["z_log"], 1)
                    act.wait_ge(S["z_log"], 3 * w + 1)
                    act.activation(t0[:, :], t0[:, :], ACT.Exp, scale=-1.0).then_inc(S["z_log"], 1)
                    act.wait_ge(S["z_log"], 3 * w + 2)
                    act.activation(t0[:, :], t0[:, :], ACT.Ln, bias=ones[:, 0:1]).then_inc(S["z_log"], 1)
                    inv = 1.0 / DECAY_TAU
                    act.wait_ge(S["decay_sum"], 5 * w + 4)
                    wait_former(act, S["kd_scores_mm"], 3 * w)
                    act.activation(k_dec[:, :], t1[:, :], ACT.Exp, scale=inv).then_inc(S["decay_exp"], 1)
                    act.wait_ge(S["decay_sum"], 5 * w + 5)
                    wait_former(act, S["kd_scores_mm"], 3 * w)
                    act.activation(q_mid[:, :], t0[:, 0:T], ACT.Exp, scale=inv).then_inc(S["decay_exp"], 1)
                    act.activation(k_mid[:, :], t0[:, 0:T], ACT.Exp, scale=-inv).then_inc(S["decay_exp"], 1)
                    wait_former(act, S["inter_mm"], 8 * w)
                    act.activation(q_dec[:, :], t2[:, 0:T], ACT.Exp, scale=inv).then_inc(S["decay_exp"], 1)
                    wait_former(act, S["state_step"], 11 * w)
                    act.activation(dec[:, :], t2[:, W_LAST[d]:TC:CH], ACT.Exp, scale=inv).then_inc(S["decay_exp"], 1)
                    q = w + Q_GLA
                    act.wait_ge(unit_done[0], q + 1)
                    wait_former(act, S["conv3"], 5 * w)
                    act.activation(cc_sb[:, :], ps[:, 0, :], ACT.Copy).then_inc(S["cc_read"], 1)
                    for s in range(3):
                        act_hi(act, s, q + 1)
                    if d == 0 and not (isinstance(h, int) and h == 0):
                        turned_back(h - 1)
                    wait_apart(act, unit_done[3], q + 1)
                    act.activation(at_index(g_sb, w), ps[:, 3, :], ACT.Copy).then_inc(S["g_read"], 1)
                    act_hi(act, 3, q + 1)
                    wait_former(act, S["kv_mm"], 11 * w)
                    act.wait_ge(S["kd_scores_mm"], 3 * w + 1)
                    act.activation(kd_tok[:, TT:TTC, :].rearrange("p c k -> p (c k)"), ps[:, 6, 0:CTX], ACT.Copy)\
                       .then_inc(S["kd_read"], 1)
                    act.wait_ge(S["kd_scores_mm"], 3 * w + 2)
                    act.activation(kd_tok[:, 0:TT, :].rearrange("p c k -> p (c k)"), ps[:, 0, :], ACT.Copy)\
                       .then_inc(S["kd_read"], 1)
                    if d == 0:
                        decay_weights(h, 1)
                    elif not (isinstance(h, int) and h == HEADS - 1):
                        decay_weights(h + 1, 0)
                act.wait_ge(S["inter_mm"], 16 * h + 16)
                for c in range(TT):
                    squares = t1[:, T:TC] if c == 3 else t2[:, c * HEAD_V:(c + 1) * HEAD_V]
                    act.activation(squares, ps[:, 4 + c // 2, (c % 2) * HEAD_V:(c % 2 + 1) * HEAD_V], ACT.Square,
                                   scale=1.0 / HEAD_V ** 0.5, accum_out=o_ss[:, c:c + 1]).then_inc(S["o_ss"], 1)
                act.wait_ge(S["o_ss"], 4 * h + 4)
                act_power(act, o_rstd[:, :], o_ss[:, :], S["o_rstd"], 2 * h)

            decay_weights(0, 0)
            head(0)
            with act.Fori(1, HEADS - 1) as h:
                head(h)
            head(HEADS - 1)
            turned_back(HEADS - 1)

        def act_gated(act):
            for j in range(KC + 1):
                if j < KC:
                    if j >= 2:
                        act.wait_ge(S["og_val"], j - 1)
                    act.activation(og_sg[j % 2][:, :], g_sb[:, j, :], ACT.Silu).then_inc(S["og_sg"], 1)
                if j >= 1:
                    act.wait_ge(S["og_val"], j)
                    act.activation(og_hi[:, j - 1, :], og_val[(j - 1) % 2][:, :], ACT.Copy).then_inc(S["og_hi"], 1)
            act.wait_ge(unit_done[1], Q_MERGE + 1)
            act.activation(sig_a[:, :], ps[:, 1, :], ACT.Sigmoid).then_inc(S["sig_a"], 1)
            for k in range(KC):
                if k == 4:
                    act_hi(act, 0, Q_MERGE + 1)
                act.activation(y_hi[:, k, :], y_sb[:, k, :], ACT.Copy).then_inc(S["y_hi"], 1)

        def act_merge(act):
            act.wait_ge(S["y_lo"], KC)

            def merge(r):
                q = r + Q_MERGE
                if not isinstance(r, int):
                    wait_former(act, S["merge_a"], r)
                    act.wait_ge(unit_done[1], q + 1)
                    act.activation(sig_a[:, :], ps[:, 1, :], ACT.Sigmoid).then_inc(S["sig_a"], 1)
                    act_hi(act, 0, q + 1)
                act_hi(act, 1, q + 1)
                wait_former(act, S["merge_b"], r)
                act.wait_ge(unit_done[3], q + 1)
                act.activation(sig_b[:, :], ps[:, 3, :], ACT.Sigmoid).then_inc(S["sig_b"], 1)
                act_hi(act, 2, q + 1)
                if isinstance(r, int):
                    act.wait_ge(S["small_in"], 32)
                    act.activation(cond2, ada_w[1][:, :], ACT.Silu).then_inc(S["cond_ready"], 1)
                act_hi(act, 3, q + 1)
                wait_apart(act, S["merged"], r + 1)
                act.activation(at_index(mg_hi, r), mrg_v[:, :], ACT.Copy).then_inc(S["mg_hi"], 1)

            merge(0)
            with act.Fori(1, KC) as r:
                merge(r)

        def act_square(act, i, n):
            wait_former(act, S["norm_acc"], 7 * (i - 1) + (max(1, n - 2) if n >= 2 else 0))
            act.activation(sq[n % 2][:, :], x[:, n, :], ACT.Square, scale=ROOT).then_inc(S["norm_sq"], 1)

        def act_high(act, n, gain):
            act.activation(h_hi[:, n, :], x[:, n, :], ACT.Copy, scale=gain).then_inc(S["h_hi"], 1)

        def act_resid(act, i, q0, resid_base, per_round, sizes, last=False, gain=None, twice=False):
            for n in range(KC):
                r, s0 = (n, 0) if per_round == 1 else (n // 4, n % 4)
                for s in (range(4) if per_round == 1 else (s0,)):
                    if not (last and r == KC // per_round - 1):
                        act_hi(act, s, q0 + r + 1, sizes[s] if r < KC // per_round - 1 else D)
                act.wait_ge(S["resid_x"], resid_base + n + 1)
                if gain:
                    act_high(act, n, gain(n))
                if not twice:
                    act_square(act, i, n)
                    continue
                wait_former(act, S["norm_acc"], 7 * (i - 1) + 2 * max(0, n - 1))
                for j, (total, scale) in enumerate(((acc, ROOT), (acc2, root_g[:, n:n + 1]))):
                    act.activation((total if n == 0 else sq[j])[:, :], x[:, n, :], ACT.Square, scale=scale)\
                       .then_inc(S["norm_sq"], 1)

        def act_rms(act, i):
            act.wait_ge(S["norm_stat"], i)
            act_rstd(act, i, rstd[:, :], ps[:, 6, :])

        def act_split(act, val_base, shift=None):
            for k in range(KC):
                act.wait_ge(S["h_val"], val_base + k + 1)
                if shift is None:
                    act.activation(h_hi[:, k, :], nv[k % 2][:, :], ACT.Copy).then_inc(S["h_hi"], 1)
                else:
                    act.activation(h_hi[:, k, :], nv[k % 2][:, :], ACT.Identity, bias=shift[:, k:k + 1])\
                       .then_inc(S["h_hi"], 1)

        FFO_N = [n * P for n in FFO]

        def act_ffn(act, e, i, resid_base, last=False, gain=None, twice=False):
            def hidden(r):
                q = r + Q_FFI[e]
                for p in range(2):
                    if e == 0:
                        act.wait_ge(unit_done[2 * p], q + 1)
                        wait_former(act, S[f"ffn_val{p}"], r)
                        act.activation(sa[p][:, :], ps[:, 2 * p, :], ACT.Silu).then_inc(S[f"ffn_sa{p}"], 1)
                    else:
                        act.wait_ge(S[f"ffn_scaled{p}"], 2 * r + (22 * (e - 1) + 1))
                        act.activation(sa[p][:, :], sa[p][:, :], ACT.Silu).then_inc(S[f"ffn_sa{p}"], 1)
                    for s in (2 * p, 2 * p + 1):
                        act_hi(act, s, q + 1)
                    wait_apart(act, S[f"ffn_val{p}"], r + (11 * e + 1))
                    act.activation(at_index(gu_hi, 2 * r + p), fval[p][:, :], ACT.Copy).then_inc(S[f"ffn_hi{p}"], 1)

            hidden(0)
            with act.Fori(1, FC // 2) as r:
                hidden(r)
            act_resid(act, i, Q_FFO[e], resid_base, 1, FFO_N, last, gain, twice)

        def act_cp(act):
            for r in range(2):
                q = r + Q_CPI
                for p in range(2):
                    act.wait_ge(S["cp_scaled"], 4 * r + 2 * p + 1)
                    act.activation(csg[p][:, :], csg[p][:, :], ACT.Sigmoid).then_inc(S[f"conv_sg{p}"], 1)
                    act_hi(act, 2 * p, q + 1)
                    act_hi(act, 2 * p + 1, q + 1)
            for s in range(4):
                act.wait_ge(unit_done[s], Q_CPI + 3)
                act.activation(u_sb[:, s, UPAD:], ps[:, s, :], ACT.Copy).then_inc(S["cp_u"], 1)
                act_hi(act, s, Q_CPO)
            for i in range(CONVW):
                if i >= 4:
                    act.wait_ge(S["tap_mm"], i - 3)
                act.activation(tap[i % 4][:, :], ident[:, :], ACT.Copy, scale=v_at("dw_w", 3 * CONVW + i))\
                   .then_inc(S["tap_ready"], 1)
            act.wait_ge(S["tap_mm"], CONVW)
            act.activation(cv[:, 3, :], ps[:, 4, :], ACT.Identity, bias=v_at("dw_b", 3)).then_inc(S["conv_pe"], 1)
            for g in range(CPC):
                act.wait_ge(S["pool_mm"], g + 1)
                act.activation(cat_hi[:, CPC + g, :], ps[:, g, :], ACT.Copy, scale=v_at("pool_scale", g))\
                   .then_inc(S["cat_hi_p"], 1)
            for g in range(CPC):
                act.wait_ge(S["ln_centred"], g + 1)
                act.activation(csq[:, g, :], cv[:, g, :], ACT.Square, scale=1.0 / (CPC * P) ** 0.5).then_inc(S["ln_sq"], 1)
            act.wait_ge(S["first_out"], KC)
            act_rms(act, 4)
            for g in range(CPC):
                act.wait_ge(S["ln_val"], g + 1)
                if g >= 2:
                    act.wait_ge(S["cat_lo_a"], g - 1)
                act.activation(lns[g % 2][:, :], lnv[g % 2][:, :], ACT.Silu, bias=v_at("ln_b", g)).then_inc(S["ln_silu"], 1)
                act.wait_ge(S["ln_silu"], g + 1)
                act.activation(cat_hi[:, g, :], lns[g % 2][:, :], ACT.Copy).then_inc(S["cat_hi_a"], 1)

        def act_hg(act):
            def log(g):
                act.wait_ge(S["hf_ready"], g + 1)
                act.activation(hlf[:, :], hlf[:, :], ACT.Ln).then_inc(S["hlog_ready"], 1)

            def decays(g, par):
                act.wait_ge(S["hd_ready"], 7 * g + 1)
                wait_former(act, S["hkd_mm"], g)
                act.activation(hkd[:, :], hd[0][:, :], ACT.Exp).then_inc(S["hd_used"], 1)
                wait_former(act, S["ho_mm"], g)
                act.activation(hqb[:, :], hb[par][:, :], ACT.Exp).then_inc(S["hqb_exp"], 1)
                wait_former(act, S["hg_state"], 7 * g)
                act.activation(hdec[:, :], hb[par][:, CH - 1:T:CH], ACT.Exp).then_inc(S["hdec_ready"], 1)
                for i, m in enumerate(LEVELS):
                    act.wait_ge(S["hd_ready"], 7 * g + i + 2)
                    wait_former(act, S["hx_ready"], 12 * g + 2 * max(i - 1, 0))
                    for half, scale in ((0, -1.0), (1, 1.0)):
                        def part(t):
                            return t[:, :].rearrange("p (b a m) -> p b a m", a=2, m=m)[:, :, half, :]
                        act.activation(part(he[i % 2]), part(hd[(i + 1) % 2]), ACT.Exp, scale=scale)\
                           .then_inc(S["hd_used"], 1)

            def take(w, par, between=None):
                q = w + Q_HG
                act.wait_ge(unit_done[0], q + 1)
                wait_former(act, S["hf_ready"], w)
                act.activation(hsf[:, :], ps[:, 0, :], ACT.Sigmoid).then_inc(S["hg_f_read"], 1)
                act_hi(act, 0, q + 1)
                act.wait_ge(unit_done[1], q + 1)
                act.activation(hq[par][:, :], ps[:, 1, :], ACT.Copy).then_inc(S["hg_q_read"], 1)
                act_hi(act, 1, q + 1)
                if between:
                    between()
                act.wait_ge(unit_done[2], q + 1)
                act.activation(hv[par][:, :], ps[:, 2, :], ACT.Copy).then_inc(S["hg_i_read"], 1)
                act_hi(act, 2, q + 1)
                act.wait_ge(unit_done[3], q + 1)
                act.activation(hg[par][:, :], ps[:, 3, :], ACT.Sigmoid).then_inc(S["hg_sig"], 1)
                act_hi(act, 3, q + 1)

            def high(g):
                wait_apart(act, S["hval_ready"], g + 1)
                act.activation(at_index(r_hi, g), hval[:, :], ACT.Copy).then_inc(S["r_hi"], 1)

            def mix(g, last=False):
                act.wait_ge(S["hkd_mm"], g + 1)
                wait_former(act, S["hkv_mm"], 7 * g)
                act.activation(hkd_tok[:, :, :].rearrange("p c k -> p (c k)"), ps[:, 4, :], ACT.Copy)\
                   .then_inc(S["hkd_tok_ready"], 1)
                act.wait_ge(S["ho_mm"], g + 1)
                for c in range(TT):
                    act.activation(hsquares[:, c * P:(c + 1) * P], ps[:, 5, c * P:(c + 1) * P], ACT.Square,
                                   scale=1.0 / P ** 0.5, accum_out=o_ss[:, c:c + 1])\
                       .then_inc(S["ho_ss"], 1)
                act.wait_ge(S["ho_ss"], 4 * g + 4)
                act_power(act, o_rstd[:, :], o_ss[:, :], S["ho_rstd"], 2 * g, between=None if last else lambda: log(g + 1))

            take(0, 0)
            log(0)
            decays(0, 0)
            take(1, 1)
            mix(0)
            with act.Fori(0, 3) as m:
                for p in range(2):
                    decays(2 * m + (1 + p), 1 - p)
                    take(2 * m + (2 + p), p, between=lambda: high(2 * m + p))
                    mix(2 * m + (1 + p))
            decays(7, 1)
            high(6)
            mix(7, last=True)
            high(7)

        @block.scalar
        def _(act):
            full = [D] * 4
            act_start(act)
            act_qkv(act)
            act_gla(act)
            act_gated(act)
            act_merge(act)
            act_resid(act, 1, Q_MIX, 0, 4, full)
            act_rms(act, 1)
            act_split(act, 8, mod2[:, 8:16])
            act_ffn(act, 0, 2, 8, gain=lambda k: gain_xg[:, k:k + 1], twice=True)
            act.wait_ge(S["norm_stat"], 2)
            act_power(act, rstd_xg[:, :], ps[:, 7, :], S["norm_rstd"], 4, eps_xg)
            act_rms(act, 3)
            act_cp(act)
            act_resid(act, 4, Q_CPO, 16, 4, full, gain=lambda k: v_at("norm_ffn", k))
            act_rms(act, 5)
            act_ffn(act, 1, 5, 24)
            act_rms(act, 6)
            act_split(act, 16)
            act_hg(act)
            act_resid(act, 6, Q_HGO, 32, 4, full, gain=lambda k: v_at("norm_ffn", 8 + k))
            act_rms(act, 7)
            act_ffn(act, 2, 7, 40, last=True)
            act_rms(act, 8)

        def dve_start(dve):
            dve.wait_ge(S["vec_in"], 16)
            dve.tensor_tensor(lb[:, :], v_at("lb_logits", 0, HG), v_at("lb_logits", HG, HG), ALU.max).then_inc(S["dve_step"], 1)
            dve.wait_ge(S["dve_step"], 1)
            for i in range(2):
                dve.tensor_tensor(lb_t[:, i * HG:(i + 1) * HG], v_at("lb_logits", i * HG, HG), lb[:, :], ALU.subtract)\
                   .then_inc(S["dve_step"], 1)
            dve.memset(s_dir[0][:, :, :], 0.0).then_inc(S["zeros"], 1)
            dve.memset(s_dir[1][:, :, :], 0.0).then_inc(S["zeros"], 1)
            dve.wait_ge(S["cond_ready"], 1)
            dve.tensor_tensor(om_lb[:, :], lb_t[:, 0:HG], lb_t[:, HG:2 * HG], ALU.add).then_inc(S["dve_step"], 1)
            dve.wait_ge(S["dve_step"], 4)
            dve.reciprocal(om_lb[:, :], om_lb[:, :]).then_inc(S["dve_step"], 1)
            dve.wait_ge(S["dve_step"], 5)
            dve.tensor_tensor(lb[:, :], lb_t[:, HG:2 * HG], om_lb[:, :], ALU.mult).then_inc(S["dve_step"], 1)
            dve.wait_ge(S["dve_step"], 6)
            dve.tensor_scalar(om_lb[:, :], lb[:, :], -1.0, 1.0, ALU.mult, ALU.add).then_inc(S["dve_step"], 1)
            dve.tensor_tensor(gain_xg[:, :], v_at("g_final", 0, 8), v_at("norm_mix", 0, 8), ALU.mult)\
               .then_inc(S["dve_step"], 1)
            dve.tensor_scalar(root_g[:, :], v_at("g_final", 0, 8), ROOT, None, ALU.mult).then_inc(S["dve_step"], 1)
            dve.wait_ge(S["cond_ready"], 2)

            def modulation(k):
                for i, n in enumerate((k, KC + k)):
                    a = 2 * k + i
                    dve.wait_ge(S[f"ada_full{a % 4}"], 16 * (a // 4 + 1))
                    if a:
                        dve.wait_ge(S["ada1_used"], a)
                    for v in range(2):
                        ins = dve.tensor_tensor_reduce(ada1_out[v][:, :], ada1_w[a % 4][:, :], cond[:, v, :], 1.0, 0.0,
                                                       ALU.mult, ALU.add, accum_out=mod1[:, n, v:v + 1])
                    ins.then_inc(S["ada1_used"], 1)
                both = slice(k, 2 * KC, KC)
                dve.wait_ge(S["ada1_used"], 2 * k + 2)
                dve.tensor_tensor(mod1[:, both, :], mod1[:, both, :], wide(vec[:, VEC["b_ada"]:VEC["b_ada"] + 16][:, both], 2),
                                  ALU.add).then_inc(S["mod1_ready"], 1)
                dve.wait_ge(S["mod1_ready"], 2 * k + 1)
                dve.tensor_scalar(amp1[:, k, :], mod1[:, KC + k, :], 1.0, v_at("g_mix", k), ALU.add, ALU.mult)\
                   .then_inc(S["mod1_ready"], 1)

            def low(k):
                dve.wait_ge(S["h_hi"], k + 1)
                dve.tensor_tensor(h1_lo[:, k, :], x_all[:, k, 0:T], h1_hi[:, k, :].bitcast(F32), ALU.subtract)
                dve.tensor_tensor(hc_lo[:, k, :], x_all[:, k, T:TC], hc_hi[:, k, :].bitcast(F32), ALU.subtract)\
                   .then_inc(S["h_lo"], 1)

            for k in range(KC):
                modulation(k)
                for low_k in ((), (), (), (0,), (1,), (2, 3), (4, 5), (6, 7))[k]:
                    low(low_k)

        def dve_qkv(dve):
            dve.wait_ge(S["dd_mm"], 1)
            dve.tensor_copy(dd_sb[:, T:TC], ps[0:32, 7, 0:CTX]).then_inc(S["qkv_ctx_read"], 1)

            def v_read(m):
                dve.wait_ge(S["v_turned"], m + 1)
                i = m % 2
                out = v_sb[:, m // 2, :].rearrange("p (c v) -> p c v", v=HEAD_V)[:, :, i * P:(i + 1) * P]
                dve.tensor_copy(out[:, 0:TT, :], ps[:, 4 + i, :].rearrange("p (c v) -> p c v", v=P))
                dve.tensor_copy(out[:, TT:TTC, :], ps[:, 6 + i, 0:CTX].rearrange("p (c v) -> p c v", v=P))\
                   .then_inc(S["v_read"], 1)

            for u in range(4, 16):
                s, q = u % 4, u // 4
                dve.wait_ge(unit_done[s], q + 1)
                if u >= 10:
                    dve.wait_ge(S["v_turned"], u - 9)
                dve.tensor_copy(k_sb[:, s, T:TC] if u < 8 else vT[u % 2][:, T:TC], ps[:, 2 + u % 2, 0:CTX])\
                   .then_inc(S["qkv_ctx_read"], 1)
                if u > 8:
                    v_read(u - 9)
            v_read(7)

        def dve_gla(dve):
            def chunks(ap):
                return ap.rearrange("p (n c) -> p n c", c=CH)

            def each(ap, off, n):
                return wide(ap[:, off:n * CH:CH], CH)

            dve.wait_ge(S["const_ready"], 1)
            dve.wait_ge(S["zeros"], 2)

            def turned_back(h):
                dve.wait_ge(S["oT_mm"], h + 1)
                dve.tensor_scalar(at_index(v_sb, h)[:, T:2 * T], ps[:, 7, :], 1.0, None, ALU.mult).then_inc(S["oT_read_d"], 1)

            def head(h):
                for d in range(2):
                    w = 2 * h + d
                    q = w + Q_GLA
                    dve.wait_ge(S["z_mm"], w + 1)
                    dve.wait_ge(S["b_dec_copied"], w + 1)
                    dve.wait_ge(S["z_log"], 3 * w + 1)
                    wait_former(dve, S["decay_exp"], 5 * w)
                    dve.tensor_scalar(t1[:, :], z_ps[:, 0:TC], b_dec_h[:, :], 0.0, ALU.add, ALU.min).then_inc(S["decay_sum"], 1)
                    dve.wait_ge(S["decay_sum"], 5 * w + 1)
                    dve.wait_ge(S["z_log"], 3 * w + 3)
                    dve.tensor_tensor(t1[:, :], t1[:, :], t0[:, :], ALU.subtract).then_inc(S["decay_sum"], 1)
                    dve.wait_ge(S["decay_sum"], 5 * w + 2)
                    wait_former(dve, S["decay_exp"], 5 * w)
                    wait_former(dve, S["o_ss"], 4 * h)
                    if d == 0:
                        dve.tensor_tensor_scan(t2[:, :], keep[:, 0:TC], t1[:, :], 0.0, ALU.mult, ALU.add)\
                           .then_inc(S["decay_sum"], 1)
                    else:
                        dve.tensor_tensor_scan(t2[:, ::-1], keep[:, TC:0:-1], t1[:, ::-1], 0.0, ALU.mult, ALU.add)\
                           .then_inc(S["decay_sum"], 1)
                    dve.wait_ge(S["decay_sum"], 5 * w + 3)
                    dve.tensor_tensor(chunks(t1[:, :]), each(t2, W_LAST[d], NCHC), chunks(t2[:, :]), ALU.subtract)\
                       .then_inc(S["decay_sum"], 1)
                    wait_former(dve, S["decay_exp"], 5 * w)
                    dve.tensor_tensor(chunks(t0[:, 0:T]), chunks(t2[:, 0:T]), each(t2, W_MID[d], NCH), ALU.subtract)\
                       .then_inc(S["decay_sum"], 1)
                    for i, (t, n, src) in enumerate(((k_dec, TC, k_sb), (q_mid, T, q_sb), (k_mid, T, k_sb),
                                                     (q_dec, T, q_sb))):
                        dve.wait_ge(S["decay_exp"], 5 * w + i + 1)
                        dve.tensor_tensor(t[:, :], t[:, :], at_index(src, h)[:, 0:n], ALU.mult).then_inc(S["decayed"], 1)
                    dve.wait_ge(S["cc_read"], w + 1)
                    dve.wait_ge(unit_done[1], q + 1)
                    dve.tensor_tensor(cc_sb[:, :], cc_sb[:, :], ps[:, 1, :], ALU.mult).then_inc(S["conv3"], 1)
                    dve.wait_ge(S["conv3"], 5 * w + 1)
                    y = at_index(y_sb, w)
                    yr, ur = chunks(y), chunks(cc_sb[:, :])
                    dve.tensor_scalar(y, cc_sb[:, :], v_dyn("w_conv", w + 8), None, ALU.mult).then_inc(S["conv3"], 1)
                    dve.wait_ge(S["conv3"], 5 * w + 2)
                    dve.scalar_tensor_tensor(out=yr[:, :, 1:CH], in0=ur[:, :, 0:CH - 1], scalar=v_dyn("w_conv", w),
                                             in1=yr[:, :, 1:CH], op0=ALU.mult, op1=ALU.add).then_inc(S["conv3"], 1)
                    dve.wait_ge(S["conv3"], 5 * w + 3)
                    dve.scalar_tensor_tensor(out=yr[:, :, 0:CH - 1], in0=ur[:, :, 1:CH], scalar=v_dyn("w_conv", w + 16),
                                             in1=yr[:, :, 0:CH - 1], op0=ALU.mult, op1=ALU.add).then_inc(S["conv3"], 1)
                    dve.wait_ge(S["conv3"], 5 * w + 4)
                    dve.wait_ge(unit_done[2], q + 1)
                    dve.tensor_tensor(y, y, ps[:, 2, :], ALU.mult).then_inc(S["conv3"], 1)
                    if d == 0 and not (isinstance(h, int) and h == 0):
                        turned_back(h - 1)
                    wait_apart(dve, S["kd_scores_mm"], 3 * w + 3)
                    mask = causal[d][:, :].bitcast(U32).unsqueeze(1).broadcast_to([P, TT, P])
                    dve.copy_predicated(s_dir[d][:, :, :], mask, ps[:, 1, :].rearrange("p (c t) -> p c t", t=P))\
                       .then_inc(S["scores_read"], 1)
                    order = [8, 9, 10, 11, *range(8)] if d == 0 else [11, 10, 9, 8, *range(7, -1, -1)]
                    dve.wait_ge(S["decay_exp"], 5 * w + 5)
                    for m in range(1, 12):
                        n = m - 1
                        kv = ps[:, (2, 3, 6, 7)[n % 4], 0:HEAD_V]
                        dve.wait_ge(S["kv_mm"], 11 * w + min(11, 2 * (n // 2) + 2))
                        if m == 1:
                            wait_former(dve, S["inter_mm"], 8 * w)
                            dve.tensor_copy(state[1][:, :], kv).then_inc(S["state_step"], 1)
                            continue
                        if m >= 7:
                            dve.wait_ge(S["inter_mm"], 8 * w + m - 6)
                        dve.wait_ge(S["state_step"], 11 * w + m - 1)
                        g = order[n]
                        dve.scalar_tensor_tensor(out=state[m % 3][:, :], in0=state[(m - 1) % 3][:, :],
                                                 scalar=dec[:, g:g + 1], in1=kv, op0=ALU.mult, op1=ALU.add)\
                           .then_inc(S["state_step"], 1)
                tok = o_tok_last if isinstance(h, int) and h == HEADS - 1 else o_tok
                wait_former(dve, S["oT_mm"], h)
                dve.wait_ge(S["o_rstd"], 2 * h + 2)
                for b in range(2):
                    dve.tensor_tensor(tok[b][:, :, :], ps[:, 4 + b, :].rearrange("p (c v) -> p c v", v=HEAD_V),
                                      wide(o_rstd[:, 2 * b:2 * b + 2], HEAD_V), ALU.mult).then_inc(S["o_tok_ready"], 1)

            head(0)
            with dve.Fori(1, HEADS - 1) as h:
                head(h)
            head(HEADS - 1)
            turned_back(HEADS - 1)

        def dve_gated(dve):
            dve.wait_ge(S["oT_read_a"], HEADS)
            for j in range(KC + 1):
                if j < KC:
                    h, half = j // 2, j % 2
                    dve.wait_ge(S["og_sg"], j + 1)
                    if j >= 2:
                        dve.wait_ge(S["og_hi"], j - 1)
                        dve.wait_ge(S["og_lo"], j - 1)
                    if j == 0:
                        dve.wait_ge(S["oT_read_d"], HEADS)
                    dve.scalar_tensor_tensor(out=og_val[j % 2][:, :], in0=v_sb[:, h, half * T:(half + 1) * T],
                                             scalar=v_at("g_head", half), in1=og_sg[j % 2][:, :],
                                             op0=ALU.mult, op1=ALU.mult).then_inc(S["og_val"], 1)
                if j >= 1:
                    dve.wait_ge(S["og_hi"], j)
                    dve.tensor_tensor(og_lo[:, j - 1, :], og_val[(j - 1) % 2][:, :], og_hi[:, j - 1, :].bitcast(F32),
                                      ALU.subtract).then_inc(S["og_lo"], 1)
            for k in range(KC):
                dve.wait_ge(S["y_hi"], k + 1)
                dve.tensor_tensor(y_lo[:, k, :], y_sb[:, k, :], y_hi[:, k, :].bitcast(F32), ALU.subtract)\
                   .then_inc(S["y_lo"], 1)

        def dve_merge(dve):
            def merge(r):
                q = r + Q_MERGE
                dve.wait_ge(S["sig_a"], r + 1)
                dve.wait_ge(unit_done[0], q + 1)
                dve.tensor_tensor(mrg_a[:, :], sig_a[:, :], ps[:, 0, :], ALU.mult).then_inc(S["merge_a"], 1)
                dve.wait_ge(S["sig_b"], r + 1)
                dve.wait_ge(unit_done[2], q + 1)
                dve.tensor_tensor(mrg_b[:, :], sig_b[:, :], ps[:, 2, :], ALU.mult).then_inc(S["merge_b"], 1)
                dve.wait_ge(S["merge_a"], r + 1)
                dve.wait_ge(S["merge_b"], r + 1)
                wait_former(dve, S["mg_hi"], r)
                wait_former(dve, S["mg_lo"], r)
                dve.tensor_tensor(mrg_v[:, :], mrg_a[:, :], mrg_b[:, :], ALU.add).then_inc(S["merged"], 1)
                dve.wait_ge(S["mg_hi"], r + 1)
                dve.tensor_tensor(at_index(mg_lo, r), mrg_v[:, :], at_index(mg_hi, r).bitcast(F32), ALU.subtract)\
                   .then_inc(S["mg_lo"], 1)
                dve.wait_ge(S["cond_ready"], 3)
                for i in range(4):
                    dve.wait_ge(S[f"ada_full{i % 2}"], 32 * r + (64 + 16 * (i // 2 + 1)))
                    if i == 0:
                        wait_former(dve, S["mod2_ready"], r)
                    dve.tensor_tensor_reduce(ada_w[i % 2][:, :], ada_w[i % 2][:, :], cond2, 1.0, 0.0, ALU.mult, ALU.add,
                                             accum_out=mod_sum[:, i:i + 1]).then_inc(S["ada2_used"], 1)
                dve.wait_ge(S["ada2_used"], 4 * r + 4)
                dve.tensor_tensor(mod2[:, span(4 * r, 4)], mod_sum[:, :], v_dyn("b_ada", 4 * r + 16, 4), ALU.add)\
                   .then_inc(S["mod2_ready"], 1)

            merge(0)
            with dve.Fori(1, KC) as r:
                merge(r)

        def dve_low(dve, n, h_base, gain):
            dve.wait_ge(S["h_hi"], h_base + n + 1)
            dve.scalar_tensor_tensor(out=h_lo[:, n, :], in0=x[:, n, :], scalar=gain, in1=h_hi[:, n, :].bitcast(F32),
                                     op0=ALU.mult, op1=ALU.subtract).then_inc(S["h_lo"], 1)

        def dve_resid(dve, i, q0, resid_base, per_round, bank, gate=None, source=None, h_base=None, gain=None,
                      twice=False):
            source = x if source is None else source
            for n in range(KC + 1):
                if n < KC:
                    r, s = (n, 3) if per_round == 1 else (n // 4, n % 4)
                    dve.wait_ge(unit_done[s], q0 + r + 1)
                    if gate is None:
                        ins = dve.tensor_tensor(x[:, n, :], ps[:, bank(n), :], source[:, n, :], ALU.add)
                    else:
                        ins = dve.scalar_tensor_tensor(out=x[:, n, :], in0=ps[:, bank(n), :], scalar=gate[:, n:n + 1],
                                                       in1=source[:, n, :], op0=ALU.mult, op1=ALU.add)
                    ins.then_inc(S["resid_x"], 1)
                    if gain and n < KC - 1:
                        dve_low(dve, n, h_base, gain(n))
                if n >= 2:
                    if n == KC and gain:
                        dve_low(dve, KC - 1, h_base, gain(KC - 1))
                    (dve_sums if twice else dve_sum)(dve, i, n - 1)

        def dve_sums(dve, i, k):
            for j, total in enumerate((acc, acc2)):
                dve.wait_ge(S["norm_sq"], 8 * i + 2 * k + j + 1)
                if k > 1:
                    dve.wait_ge(S["norm_acc"], 7 * (i - 1) + 2 * (k - 2) + j + 1)
                dve.tensor_tensor(total[:, :], total[:, :], sq[j][:, :], ALU.add).then_inc(S["norm_acc"], 1)

        def dve_sum(dve, i, k):
            dve.wait_ge(S["norm_sq"], 8 * i + k + 1)
            if k > 1:
                dve.wait_ge(S["norm_acc"], 7 * (i - 1) + k - 1)
            dve.tensor_tensor(acc[:, :], sq[0][:, :] if k == 1 else acc[:, :], sq[k % 2][:, :], ALU.add)\
               .then_inc(S["norm_acc"], 1)

        def dve_rstd(dve, i):
            dve.wait_ge(S["norm_rstd"], 2 * i + 2)

        def dve_split(dve, h_base, gain, shift=None):
            for k in range(KC + 1):
                if k < KC:
                    if k >= 2:
                        dve.wait_ge(S["h_hi"], h_base + k - 1)
                        dve.wait_ge(S["h_lo"], h_base + k - 1)
                    dve.scalar_tensor_tensor(out=nv[k % 2][:, :], in0=x[:, k, :], scalar=gain(k), in1=rstd[:, :],
                                             op0=ALU.mult, op1=ALU.mult).then_inc(S["h_val"], 1)
                if k >= 1:
                    j = k - 1
                    dve.wait_ge(S["h_hi"], h_base + j + 1)
                    if shift is None:
                        ins = dve.tensor_tensor(h_lo[:, j, :], nv[j % 2][:, :], h_hi[:, j, :].bitcast(F32), ALU.subtract)
                    else:
                        ins = dve.scalar_tensor_tensor(out=h_lo[:, j, :], in0=nv[j % 2][:, :], scalar=shift[:, j:j + 1],
                                                       in1=h_hi[:, j, :].bitcast(F32), op0=ALU.add, op1=ALU.subtract)
                    ins.then_inc(S["h_lo"], 1)

        def dve_ffn(dve, e, i, resid_base, gate=None, **norm):
            def hidden(r):
                q = r + Q_FFI[e]
                for p in range(2):
                    n = r + 11 * e
                    if e == 0:
                        dve.wait_ge(S[f"ffn_sa{p}"], n + 1)
                        dve.wait_ge(unit_done[2 * p + 1], q + 1)
                        wait_former(dve, S[f"ffn_hi{p}"], n)
                        wait_former(dve, S[f"ffn_lo{p}"], n)
                        dve.tensor_tensor(fval[p][:, :], sa[p][:, :], ps[:, 2 * p + 1, :], ALU.mult)\
                           .then_inc(S[f"ffn_val{p}"], 1)
                    else:
                        dve.wait_ge(unit_done[2 * p], q + 1)
                        dve.wait_ge(S[f"ffn_val{p}"], n)
                        dve.tensor_tensor(sa[p][:, :], ps[:, 2 * p, :], rstd[:, :], ALU.mult).then_inc(S[f"ffn_scaled{p}"], 1)
                        dve.wait_ge(unit_done[2 * p + 1], q + 1)
                        dve.wait_ge(S[f"ffn_hi{p}"], n)
                        dve.wait_ge(S[f"ffn_lo{p}"], n)
                        dve.tensor_tensor(fval[p][:, :], ps[:, 2 * p + 1, :], rstd[:, :], ALU.mult)\
                           .then_inc(S[f"ffn_scaled{p}"], 1)
                        dve.wait_ge(S[f"ffn_sa{p}"], n + 1)
                        dve.wait_ge(S[f"ffn_scaled{p}"], 2 * r + 22 * (e - 1) + 2)
                        dve.tensor_tensor(fval[p][:, :], sa[p][:, :], fval[p][:, :], ALU.mult).then_inc(S[f"ffn_val{p}"], 1)
                    dve.wait_ge(S[f"ffn_hi{p}"], n + 1)
                    dve.tensor_tensor(at_index(gu_lo, 2 * r + p), fval[p][:, :], at_index(gu_hi, 2 * r + p).bitcast(F32),
                                      ALU.subtract).then_inc(S[f"ffn_lo{p}"], 1)

            hidden(0)
            with dve.Fori(1, FC // 2) as r:
                hidden(r)
            dve_resid(dve, i, Q_FFO[e], resid_base, 1, lambda n: 4 + n % 2, gate, **norm)

        def dve_cp(dve):
            dve.wait_ge(S["norm_acc"], 7 + 2 * 7)
            dve.scalar_tensor_tensor(out=acc2[:, :], in0=acc[:, :], scalar=EPS, in1=acc2[:, :], op0=ALU.mult, op1=ALU.add)\
               .then_inc(S["dve_step"], 1)
            dve.memset(a_sb[:, :, 0:APAD], 0.0).then_inc(S["zeros"], 1)
            dve.memset(u_sb[:, :, 0:UPAD], 0.0).then_inc(S["zeros"], 1)
            for i in range(2):
                dve.memset(win[i][:, 0:UPAD], 0.0).then_inc(S["zeros"], 1)
            dve.wait_ge(S["zeros"], 6)
            steps = 11
            for g in range(CPC):
                dve.wait_ge(S["dve_step"], steps)
                dve.tensor_scalar(cnt_f[:, :], cnt_i[:, :], float(2 << g), None, ALU.min).then_inc(S["dve_step"], 1)
                dve.wait_ge(S["dve_step"], steps + 1)
                dve.reciprocal(inv_cnt[:, g, :], cnt_f[:, :]).then_inc(S["dve_step"], 1)
                steps += 2
            dve.wait_ge(S["norm_rstd"], 6)

            def value(j):
                p = j % 2
                dve.wait_ge(unit_done[2 * p + 1], j // 2 + Q_CPI + 1)
                if j >= 2:
                    dve.wait_ge(S[f"conv_in{p}"], 1)
                dve.tensor_tensor(csg[p][:, :], ps[:, 2 * p + 1, :], rstd_xg[:, :], ALU.mult).then_inc(S["cp_scaled"], 1)
                dve.wait_ge(unit_done[2 * p], j // 2 + Q_CPI + 1)
                dve.tensor_tensor(a_sb[:, j, APAD:], ps[:, 2 * p, :], rstd_xg[:, :], ALU.mult).then_inc(S["cp_scaled"], 1)
                dve.wait_ge(S[f"conv_sg{p}"], j // 2 + 1)
                dve.wait_ge(S["cp_scaled"], 2 * j + 2)
                dve.tensor_tensor(a_sb[:, j, APAD:], csg[p][:, :], a_sb[:, j, APAD:], ALU.mult).then_inc(S[f"conv_in{p}"], 1)

            def convolve(first, last, *js):
                nonlocal taps
                for i in range(first, last):
                    for j in js:
                        src, w = a_sb[:, j, i:i + T], v_at("dw_w", j * CONVW + i)
                        if i == 0:
                            dve.wait_ge(S[f"conv_in{j % 2}"], j // 2 + 1)
                            ins = dve.tensor_scalar(cv[:, j, :], src, w, v_at("dw_b", j), ALU.mult, ALU.add)
                        else:
                            dve.wait_ge(S["conv_dve"], taps - len(js) + 1)
                            ins = dve.scalar_tensor_tensor(out=cv[:, j, :], in0=src, scalar=w, in1=cv[:, j, :],
                                                           op0=ALU.mult, op1=ALU.add)
                        ins.then_inc(S["conv_dve"], 1)
                        taps += 1

            taps = 0
            value(0)
            convolve(0, 5, 0)
            value(1)
            convolve(5, 18, 0)
            value(2)
            convolve(18, CONVW, 0)
            value(3)
            convolve(0, CONVW, 1, 2)
            dve.wait_ge(S["norm_rstd"], 8)
            for k in range(KC):
                dve.scalar_tensor_tensor(out=x[:, k, :], in0=x[:, k, :], scalar=v_at("g_final", k), in1=rstd[:, :],
                                         op0=ALU.mult, op1=ALU.mult).then_inc(S["first_out"], 1)
            for g in range(CPC):
                dve.wait_ge(S["cat_hi_p"], g + 1)
                dve.scalar_tensor_tensor(out=cat_lo[:, CPC + g, :], in0=ps[:, g, :], scalar=v_at("pool_scale", g),
                                         in1=cat_hi[:, CPC + g, :].bitcast(F32), op0=ALU.mult, op1=ALU.subtract)\
                   .then_inc(S["cat_lo_p"], 1)
            dve.wait_ge(S["ln_sum"], 1)
            for g in range(CPC):
                dve.scalar_tensor_tensor(out=cv[:, g, :], in0=ps[:, 5, :], scalar=-1.0 / (CPC * P), in1=cv[:, g, :],
                                         op0=ALU.mult, op1=ALU.add).then_inc(S["ln_centred"], 1)
            dve_rstd(dve, 4)
            for g in range(CPC):
                if g >= 2:
                    dve.wait_ge(S["ln_silu"], g - 1)
                dve.scalar_tensor_tensor(out=lnv[g % 2][:, :], in0=cv[:, g, :], scalar=v_at("ln_g", g), in1=rstd[:, :],
                                         op0=ALU.mult, op1=ALU.mult).then_inc(S["ln_val"], 1)
                dve.wait_ge(S["cat_hi_a"], g + 1)
                dve.tensor_tensor(cat_lo[:, g, :], lns[g % 2][:, :], cat_hi[:, g, :].bitcast(F32), ALU.subtract)\
                   .then_inc(S["cat_lo_a"], 1)

        def dve_hg(dve):
            def decays(g, par):
                k, qq, b = hk[par], hq[par], hb[par]
                dve.wait_ge(S["hlog_ready"], g + 1)
                dve.tensor_tensor_scan(b[:, :], keep[:, 0:T], hlf[:, :], 0.0, ALU.mult, ALU.add).then_inc(S["hb_ready"], 1)
                dve.wait_ge(S["hb_ready"], g + 1)

                def difference(n):
                    wait_former(dve, S["hd_used"], 13 * g + max(2 * n - 3, 0))
                    if n == 0:
                        bc = b[:, :].rearrange("p (n c) -> p n c", c=CH)
                        dve.tensor_tensor(hd[0][:, :].rearrange("p (n c) -> p n c", c=CH), wide(b[:, CH - 1:T:CH], CH), bc,
                                          ALU.subtract).then_inc(S["hd_ready"], 1)
                    else:
                        m = LEVELS[n - 1]
                        bc = b[:, :].rearrange("p (n c) -> p n c", c=2 * m)
                        dve.tensor_tensor(hd[n % 2][:, :].rearrange("p (n c) -> p n c", c=2 * m), bc,
                                          wide(b[:, m - 1:T:2 * m], 2 * m), ALU.subtract).then_inc(S["hd_ready"], 1)

                difference(0)
                difference(1)
                dve.wait_ge(S["hd_used"], 13 * g + 1)
                dve.tensor_tensor(hkd[:, :], hkd[:, :], k[:, :], ALU.mult).then_inc(S["hkd_ready"], 1)
                dve.wait_ge(S["hqb_exp"], g + 1)
                dve.tensor_tensor(hqb[:, :], hqb[:, :], qq[:, :], ALU.mult).then_inc(S["hqb_ready"], 1)
                wait_former(dve, S["hg_scores_mm"], 7 * g)
                for i, m in enumerate(LEVELS):
                    if i < 5:
                        difference(i + 2)
                    for half, src in ((0, k), (1, qq)):
                        def part(t):
                            return t[:, :].rearrange("p (b a m) -> p b a m", a=2, m=m)[:, :, half, :]
                        dve.wait_ge(S["hd_used"], 13 * g + 2 * i + 2 + half)
                        dve.tensor_tensor(part(hx[i]), part(he[i % 2]), part(src), ALU.mult).then_inc(S["hx_ready"], 1)

            def forget(w, par):
                dve.wait_ge(S["hg_f_read"], w + 1)
                dve.tensor_scalar(hlf[:, :], hsf[:, :], om_lb[:, dyn(w)], lb[:, dyn(w)], ALU.mult, ALU.add)\
                   .then_inc(S["hf_step"], 1)
                dve.wait_ge(S["hf_step"], 2 * w + 1)
                dve.tensor_scalar(hk[par][:, :], hlf[:, :], -1.0, 1.0, ALU.mult, ALU.add).then_inc(S["hf_step"], 1)
                dve.tensor_scalar(hlf[:, :], hlf[:, :], 1e-19, None, ALU.max).then_inc(S["hf_ready"], 1)

            def gate(w, par):
                dve.wait_ge(S["hg_sig"], w + 1)
                dve.tensor_tensor(hg[par][:, :], hg[par][:, :], ps[:, 3, :], ALU.mult).then_inc(S["hg_g_read"], 1)

            def finish(g, par):
                dve.wait_ge(S["hoT_mm"], g + 1)
                dve.wait_ge(S["hg_g_read"], g + 1)
                dve.scalar_tensor_tensor(out=hval[:, :], in0=ps[:, 4, :], scalar=v_dyn_or("gn_g", g),
                                         in1=hg[par][:, :], op0=ALU.mult, op1=ALU.mult).then_inc(S["hval_ready"], 1)

            def low(g):
                dve.wait_ge(S["r_hi"], g + 1)
                dve.tensor_tensor(at_index(r_lo, g), hval[:, :], at_index(r_hi, g).bitcast(F32), ALU.subtract)\
                   .then_inc(S["r_lo"], 1)

            def mix(g, par, banks=4):
                wait_former(dve, S["r_lo"], g)
                dve.wait_ge(S["hv_mm"], g + 1)
                wait_former(dve, S["ho_mm"], g)
                dve.tensor_copy(hv_tok[:, :, :].rearrange("p c k -> p (c k)"), ps[:, 5, :]).then_inc(S["hv_tok_ready"], 1)
                for l in range(7):
                    dve.wait_ge(S["hg_scores_mm"], 7 * g + l + 1)
                    wait_former(dve, S["hg_scores_read"], 7 * g + l)
                    dve.memset(spare[:, l:l + 1], 0.0)
                    mask = ident[:, :] if l == 0 else level_mask[:, l - 1, :]
                    dve.copy_predicated(hs[:, :, :], mask.bitcast(U32).unsqueeze(1).broadcast_to([P, TT, P]),
                                        ps[:, l % banks, :].rearrange("p (c t) -> p c t", t=P)).then_inc(S["hg_scores_read"], 1)
                dve.wait_ge(S["hdec_ready"], g + 1)
                dve.wait_ge(S["hkv_mm"], 7 * g + 7)
                for n in range(7):
                    kv = ps[:, 6 + n % 2, (n // 2) * P:(n // 2 + 1) * P]
                    if n == 0:
                        dve.tensor_copy(hst[:, 1, :], kv).then_inc(S["hg_state"], 1)
                    else:
                        dve.wait_ge(S["hg_state"], 7 * g + n)
                        dve.scalar_tensor_tensor(out=hst[:, n + 1, :], in0=hst[:, n, :], scalar=hdec[:, n:n + 1], in1=kv,
                                                 op0=ALU.mult, op1=ALU.add).then_inc(S["hg_state"], 1)
                dve.wait_ge(S["ho_rstd"], 2 * g + 2)
                wait_former(dve, S["hoT_mm"], g)
                dve.tensor_tensor(ho_tok[:, :, :], ps[:, 5, :].rearrange("p (c v) -> p c v", v=P), wide(o_rstd[:, :], P),
                                  ALU.mult).then_inc(S["ho_tok_ready"], 1)

            def dyn(w):
                return slice(w, w + 1) if isinstance(w, int) else bass.ds(w, 1)

            def v_dyn_or(name, g):
                return v_at(name, g) if isinstance(g, int) else v_dyn(name, g)

            dve.memset(hs[:, :, :], 0.0).then_inc(S["zeros"], 1)
            dve.wait_ge(S["zeros"], 7)
            dve.wait_ge(S["level_step"], 1 + 3 * len(LEVELS))
            forget(0, 0)
            gate(0, 0)
            decays(0, 0)
            forget(1, 1)
            gate(1, 1)
            mix(0, 0)
            with dve.Fori(0, 3) as m:
                for p in range(2):
                    decays(2 * m + (1 + p), 1 - p)
                    finish(2 * m + p, p)
                    forget(2 * m + (2 + p), p)
                    low(2 * m + p)
                    gate(2 * m + (2 + p), p)
                    mix(2 * m + (1 + p), 1 - p)
            finish(6, 0)
            decays(7, 1)
            low(6)
            mix(7, 1, banks=2)
            finish(7, 1)
            low(7)

        @block.vector
        def _(dve):
            dve_start(dve)
            dve_qkv(dve)
            dve_gla(dve)
            dve_gated(dve)
            dve_merge(dve)
            dve.wait_ge(S["mod2_ready"], KC)
            dve.scalar_tensor_tensor(out=amp2[:, :], in0=mod2[:, 16:24], scalar=1.0, in1=v_at("g_ffn", 0, 8),
                                     op0=ALU.add, op1=ALU.mult).then_inc(S["dve_step"], 1)
            dve.wait_ge(S["small_in"], 48)
            dve_resid(dve, 1, Q_MIX, 0, 4, lambda n: n % 4, mod2[:, 0:8], x_res)
            dve_rstd(dve, 1)
            dve.wait_ge(S["dve_step"], 10)
            dve_split(dve, 8, lambda k: amp2[:, k:k + 1], mod2[:, 8:16])
            dve_ffn(dve, 0, 2, 8, mod2[:, 24:32], h_base=16, gain=lambda k: gain_xg[:, k:k + 1], twice=True)
            dve_cp(dve)
            dve_resid(dve, 4, Q_CPO, 16, 4, lambda n: n % 4, h_base=24, gain=lambda k: v_at("norm_ffn", k))
            dve_rstd(dve, 5)
            dve_ffn(dve, 1, 5, 24)
            dve_rstd(dve, 6)
            dve_split(dve, 32, lambda k: v_at("norm_mix", 8 + k))
            dve_hg(dve)
            dve_resid(dve, 6, Q_HGO, 32, 4, lambda n: n % 4, h_base=40, gain=lambda k: v_at("norm_ffn", 8 + k))
            dve_rstd(dve, 7)
            dve_ffn(dve, 2, 7, 40)
            dve_rstd(dve, 8)
            for k in range(KC):
                dve.scalar_tensor_tensor(out=x[:, k, :], in0=x[:, k, :], scalar=v_at("final_g", k), in1=rstd[:, :],
                                         op0=ALU.mult, op1=ALU.mult).then_inc(S["out_ready"], 1)


def columns(a):
    return np.asarray(a).reshape(-1, P).T


def units(w):
    k, n = w.shape
    return np.ascontiguousarray(w.reshape(k // P, P, n // P, P).transpose(2, 1, 0, 3)).reshape(n // P, P, k)


def tokens_last(a):
    return np.ascontiguousarray(a.T.reshape(KC, P, -1).transpose(1, 0, 2))


def layouts(v):
    cols = {"b_ada": v["b_ada"][0], "g_mix": v["g_mix"][0], "b_dec": v["b_dec"][0],
            "g_head": v["g_head"][0], "w_conv": v["w_conv"][0], "g_ffn": v["g_ffn"][0], "g_final": v["g_final"],
            "norm_mix": v["norm_mix_g_2"], "norm_ffn": v["norm_ffn_g_2"], "final_g": v["final_g_2"],
            "dw_w": v["cp_dw_w_2"][0].reshape(CONVW, CPC, P).transpose(1, 0, 2), "dw_b": v["cp_dw_b_2"][0],
            "ln_g": v["cp_ln_g_2"][0], "ln_b": v["cp_ln_b_2"][0], "pool_scale": v["cp_pool_scale_2"][0],
            "lb_logits": v["hg_lb_logits_2"], "gn_g": v["hg_gn_g_2"][0]}
    out = {"vectors": np.concatenate([columns(cols[n]) for n, _ in VEC_SIZES], axis=1)}
    out["x"], out["ctx"] = tokens_last(v["x"][0]), tokens_last(v["ctx"][0])
    w_in = v["w_in"][0]
    q, k, vv, g, dd = 0, 512, 1024, 2048, 3072
    cb, cc, ch, ga, gb = (3104 + D * i for i in range(5))
    out["w_decay"] = units(w_in[:, dd:dd + P])[0]
    out["w_dec_up"] = v["w_dec_up"][0].reshape(2, 16, HEADS, P)
    out["w_ada"] = np.ascontiguousarray(v["w_ada"][0].T).reshape(48, P, D)
    out["conditions"] = np.stack([v["c"][0], v["c_ctx"]])
    out["w_qkv"] = units(w_in[:, q:g]).reshape(4, 4, P, D)

    def rounds(*parts):
        return np.ascontiguousarray(np.stack([units(p) for p in parts], axis=1))

    def wi(c):
        return w_in[:, c:c + D]

    out["w_conv_gate"] = rounds(wi(cc), wi(ch), wi(cb), wi(g))
    out["w_merge"] = rounds(v["w_gla_out"][0], wi(ga), v["w_conv_out"][0], wi(gb))
    out["w_mix"] = units(v["w_mix_out"][0]).reshape(2, 4, P, D)
    ins = [(v["w_ffn_in"][0][:, :DFF], v["w_ffn_in"][0][:, DFF:])] + [(v["ffn_w1_2"][i], v["ffn_w3_2"][i]) for i in range(2)]
    outs = [v["w_ffn_out"][0], v["ffn_w2_2"][0], v["ffn_w2_2"][1]]
    for e in range(3):
        out[f"w_ffn_in{e}"] = rounds(*ins[e]).reshape(FC // 2, 4, P, D)
        out[f"w_ffn_out{e}"] = units(outs[e])
    cp = v["cp_w_in_2"][0]
    out["w_cp"] = np.concatenate([rounds(cp[:, :512], cp[:, 512:1024]).reshape(2, 4, P, D),
                                  units(cp[:, 1024:]).reshape(1, 4, P, D),
                                  units(v["cp_w_out_2"][0]).reshape(2, 4, P, D)])
    out["pool_w"] = np.ascontiguousarray(v["cp_pool_w_2"][0].transpose(1, 0, 2))
    hg = v["hg_w_in_2"][0]
    out["w_hg"] = np.concatenate([rounds(hg[:, D:2 * D], hg[:, :D], hg[:, 2 * D:3 * D], hg[:, 3 * D:]),
                                  units(v["hg_w_out_2"][0]).reshape(2, 4, P, D)])
    return {n: np.ascontiguousarray(a) for n, a in out.items()}


def kernel(**inputs):
    import concourse.bacc as bacc
    from concourse.bass_utils import run_bass_kernel_spmd

    arrays = layouts({n: np.asarray(a) for n, a in inputs.items()})
    nc = bacc.Bacc("TRN2", target_bir_lowering=False, num_devices=1)
    dram = {n: nc.dram_tensor(f"in_{n}", a.shape, F32, kind="ExternalInput").ap() for n, a in arrays.items()}
    dram["out"] = nc.dram_tensor("out_x", (P, KC, T), F32, kind="ExternalOutput").ap()
    for name in ("w_ffn_in", "w_ffn_out"):
        dram[name] = [dram[f"{name}{e}"] for e in range(3)]
    build(nc, dram)
    got = run_bass_kernel_spmd(nc, [{f"in_{n}": a for n, a in arrays.items()}], core_ids=[0]).results[0]["out_x"]
    return np.ascontiguousarray(got.transpose(1, 0, 2).reshape(D, T).T).reshape(1, T, D)
```
